# Optimizing a Trainium2 kernel written in Bass

```python
import jax, jax.numpy as jnp
from jax import lax
import numpy as np

D_MODEL = 1024
BATCH = 1
SEQ = 256
DEPTH = 1

GRID_W = 64
D_MIX = D_MODEL
D_CONV = D_MIX // 2
D_ATTN = D_MIX - D_CONV
HEAD_DIM = 64
N_HEADS = D_ATTN // HEAD_DIM
CONV_WIDTH = 31
NA_ROWS = 8
NA_COLS = 16
D_FF = -(-8 * D_MODEL // (3 * 256)) * 256
D_IN = 2 * D_CONV + 3 * D_ATTN
EPS = 1e-6


def rms_norm(x, g):
    xf = x.astype(jnp.float32)
    y = xf * lax.rsqrt(jnp.mean(xf * xf, axis=-1, keepdims=True) + EPS)
    return (y * g.astype(jnp.float32)).astype(x.dtype)

def layer_norm(x, g, b):
    xf = x.astype(jnp.float32)
    mu = jnp.mean(xf, axis=-1, keepdims=True)
    xc = xf - mu
    y = xc * lax.rsqrt(jnp.mean(xc * xc, axis=-1, keepdims=True) + EPS)
    return (y * g.astype(jnp.float32) + b.astype(jnp.float32)).astype(x.dtype)

def conformer_conv(a, gate, dw_kernel, dw_bias, ln_g, ln_b):
    u = a * jax.nn.sigmoid(gate)
    pad = CONV_WIDTH // 2
    y = lax.conv_general_dilated(
        u, dw_kernel[:, None, :], window_strides=(1,), padding=[(pad, pad)],
        dimension_numbers=("NWC", "WIO", "NWC"), feature_group_count=u.shape[-1])
    y = y + dw_bias
    y = layer_norm(y, ln_g, ln_b)
    return jax.nn.silu(y)

def neighbourhood_attention(q, k, v, rpb):
    B, S, H, Dh = q.shape
    rows = S // GRID_W
    kh = min(NA_ROWS, rows)
    kw = NA_COLS
    qg = q.reshape(B, rows, GRID_W, H, Dh)
    kg = k.reshape(B, rows, GRID_W, H, Dh)
    vg = v.reshape(B, rows, GRID_W, H, Dh)
    cols = jnp.arange(GRID_W)
    col_start = jnp.clip(cols - kw // 2, 0, GRID_W - kw)
    col_idx = col_start[:, None] + jnp.arange(kw)[None, :]
    col_bias_idx = col_idx - cols[:, None] + (NA_COLS - 1)
    scale = Dh ** -0.5

    def row_block(r):
        row_start = jnp.clip(r - kh // 2, 0, rows - kh)
        q_r = lax.dynamic_index_in_dim(qg, r, axis=1, keepdims=False)
        k_rows = lax.dynamic_slice_in_dim(kg, row_start, kh, axis=1)
        v_rows = lax.dynamic_slice_in_dim(vg, row_start, kh, axis=1)
        k_win = k_rows[:, :, col_idx]
        v_win = v_rows[:, :, col_idx]
        s = jnp.einsum("bqhd,brqchd->bhqrc", q_r, k_win,
                       preferred_element_type=jnp.float32) * scale
        row_bias_idx = row_start + jnp.arange(kh) - r + (NA_ROWS - 1)
        bias = rpb[:, row_bias_idx][:, :, col_bias_idx]
        s = s + jnp.transpose(bias, (0, 2, 1, 3))[None].astype(jnp.float32)
        p = jax.nn.softmax(s, axis=(-2, -1))
        return jnp.einsum("bhqrc,brqchd->bqhd", p.astype(v_win.dtype), v_win)

    out = lax.map(row_block, jnp.arange(rows))
    return jnp.moveaxis(out, 0, 1).reshape(B, S, H * Dh)

def first_inputs(seed: int = 0) -> dict:
    key = jax.random.key(seed)
    ks = jax.random.split(key, 16)
    f32 = jnp.float32
    n = lambda k, shape, s: (jax.random.normal(k, shape, f32) * s).astype(f32)
    return {
        "x": n(ks[0], (BATCH, SEQ, D_MODEL), 1.0),
        "norm1_g": 1.0 + n(ks[1], (DEPTH, D_MODEL), 0.02),
        "w_in": n(ks[2], (DEPTH, D_MODEL, D_IN), D_MODEL ** -0.5),
        "q_norm_g": 1.0 + n(ks[3], (DEPTH, HEAD_DIM), 0.02),
        "k_norm_g": 1.0 + n(ks[4], (DEPTH, HEAD_DIM), 0.02),
        "rpb": n(ks[5], (DEPTH, N_HEADS, 2 * NA_ROWS - 1, 2 * NA_COLS - 1), 0.1),
        "dw_kernel": n(ks[6], (DEPTH, CONV_WIDTH, D_CONV), CONV_WIDTH ** -0.5),
        "dw_bias": n(ks[7], (DEPTH, D_CONV), 0.02),
        "conv_ln_g": 1.0 + n(ks[8], (DEPTH, D_CONV), 0.02),
        "conv_ln_b": n(ks[9], (DEPTH, D_CONV), 0.02),
        "w_out": n(ks[10], (DEPTH, D_MIX, D_MODEL), D_MIX ** -0.5),
        "norm2_g": 1.0 + n(ks[11], (DEPTH, D_MODEL), 0.02),
        "w_gate": n(ks[12], (DEPTH, D_MODEL, D_FF), D_MODEL ** -0.5),
        "w_up": n(ks[13], (DEPTH, D_MODEL, D_FF), D_MODEL ** -0.5),
        "w_down": n(ks[14], (DEPTH, D_FF, D_MODEL), D_FF ** -0.5),
    }

def first_block(x, norm1_g, w_in, q_norm_g, k_norm_g, rpb, dw_kernel, dw_bias,
              conv_ln_g, conv_ln_b, w_out, norm2_g, w_gate, w_up, w_down):
    B, S, _ = x.shape
    splits = [D_CONV, 2 * D_CONV, 2 * D_CONV + D_ATTN, 2 * D_CONV + 2 * D_ATTN]
    for l in range(DEPTH):
        h = rms_norm(x, norm1_g[l])
        z = h @ w_in[l]
        a, gate, q, k, v = jnp.split(z, splits, axis=-1)
        conv_out = conformer_conv(a, gate, dw_kernel[l], dw_bias[l],
                                  conv_ln_g[l], conv_ln_b[l])
        q = rms_norm(q.reshape(B, S, N_HEADS, HEAD_DIM), q_norm_g[l])
        k = rms_norm(k.reshape(B, S, N_HEADS, HEAD_DIM), k_norm_g[l])
        v = v.reshape(B, S, N_HEADS, HEAD_DIM)
        attn_out = neighbourhood_attention(q, k, v, rpb[l])
        mix = jnp.concatenate([conv_out, attn_out], axis=-1)
        x = x + mix @ w_out[l]
        h = rms_norm(x, norm2_g[l])
        x = x + (jax.nn.silu(h @ w_gate[l]) * (h @ w_up[l])) @ w_down[l]
    return x


DEPTH_2 = 2

CHUNK = 64

ATTN_WIDTH = D_MODEL // 2
ATTN_HEADS = ATTN_WIDTH // HEAD_DIM
ROPE_DIM = HEAD_DIM // 4
ROPE_THETA = 500000.0
IDX_HEADS = 4
IDX_DIM = 64
IDX_SCALE = (IDX_DIM ** -0.5) * (IDX_HEADS ** -0.5)
TOPK_MAX = 256
QBLOCK = 64

CONV_WIDTH_2 = D_MODEL // 2
CONV_GROUPS = 8
CONV_K = 3

N_BRANCH = 2
MLP_HIDDEN = 4 * D_MODEL

PROJ_SIZES = (ATTN_WIDTH, ATTN_WIDTH, ATTN_WIDTH, IDX_HEADS * IDX_DIM, IDX_DIM, IDX_HEADS,
              CONV_WIDTH_2, CONV_WIDTH_2, CONV_WIDTH_2, N_BRANCH * D_MODEL)
IN_COLS = sum(PROJ_SIZES)


def rmsnorm(x, g):
    xf = x.astype(jnp.float32)
    y = xf * lax.rsqrt(jnp.mean(xf * xf, axis=-1, keepdims=True) + EPS)
    return (y * g.astype(jnp.float32)).astype(x.dtype)

def rope_tables(T):
    inv = 1.0 / (ROPE_THETA ** (jnp.arange(0, ROPE_DIM, 2, dtype=jnp.float32) / ROPE_DIM))
    ang = jnp.arange(T, dtype=jnp.float32)[:, None] * inv[None, :]
    return jnp.cos(ang), jnp.sin(ang)

def apply_partial_rope(x, cos, sin):
    half = ROPE_DIM // 2
    xr = x[..., :ROPE_DIM].astype(jnp.float32)
    x1, x2 = xr[..., :half], xr[..., half:]
    c = cos[None, :, None, :]
    s = sin[None, :, None, :]
    rot = jnp.concatenate([x1 * c - x2 * s, x2 * c + x1 * s], axis=-1)
    return jnp.concatenate([rot.astype(x.dtype), x[..., ROPE_DIM:]], axis=-1)

def dsa_attention(q, k, v, iq, ik, iw):
    B, T, H, Dh = q.shape
    topk = min(TOPK_MAX, T // 4)
    nblk = T // QBLOCK
    key_pos = jnp.arange(T)
    scale = Dh ** -0.5
    ikf = ik.astype(jnp.float32)

    def block(i):
        t0 = i * QBLOCK
        qb = lax.dynamic_slice_in_dim(q, t0, QBLOCK, axis=1)
        iqb = lax.dynamic_slice_in_dim(iq, t0, QBLOCK, axis=1).astype(jnp.float32)
        iwb = lax.dynamic_slice_in_dim(iw, t0, QBLOCK, axis=1).astype(jnp.float32)
        tpos = t0 + jnp.arange(QBLOCK)
        limit = (tpos // CHUNK + 1) * CHUNK
        admissible = key_pos[None, :] < limit[:, None]
        logits = jnp.einsum('bthd,bsd->bths', iqb, ikf)
        score = jnp.einsum('bths,bth->bts', jax.nn.relu(logits), iwb) * IDX_SCALE
        score = jnp.where(admissible[None], score, -jnp.inf)
        _, idx = lax.top_k(score, topk)
        valid = idx < limit[None, :, None]
        kg = jax.vmap(lambda kk, ii: kk[ii])(k, idx)
        vg = jax.vmap(lambda vv, ii: vv[ii])(v, idx)
        s = jnp.einsum('bthd,btkhd->bthk', qb, kg).astype(jnp.float32) * scale
        s = jnp.where(valid[:, :, None, :], s, -jnp.inf)
        p = jax.nn.softmax(s, axis=-1).astype(v.dtype)
        return jnp.einsum('bthk,btkhd->bthd', p, vg)

    out = lax.map(block, jnp.arange(nblk))
    return out.transpose(1, 0, 2, 3, 4).reshape(B, T, H * Dh)

def short_conv(xc, conv_w):
    T = xc.shape[1]
    xp = jnp.pad(xc, ((0, 0), (CONV_K - 1, 0), (0, 0)))
    out = xp[:, 0:T] * conv_w[0]
    for j in range(1, CONV_K):
        out = out + xp[:, j:j + T] * conv_w[j]
    return out

def second_inputs(seed: int = 0) -> dict:
    key = jax.random.key(seed)
    ks = jax.random.split(key, 12)
    f32 = jnp.float32
    x = jax.random.normal(ks[0], (BATCH, SEQ, D_MODEL), f32)
    norm_mix = 1.0 + 0.02 * jax.random.normal(ks[1], (DEPTH_2, D_MODEL), f32)
    w_in = jax.random.normal(ks[2], (DEPTH_2, D_MODEL, IN_COLS), f32) * D_MODEL ** -0.5
    conv_w = jax.random.normal(ks[3], (DEPTH_2, CONV_K, CONV_WIDTH_2), f32) * CONV_K ** -0.5
    w_attn_out = jax.random.normal(ks[4], (DEPTH_2, ATTN_WIDTH, D_MODEL), f32) * ATTN_WIDTH ** -0.5
    w_conv_out = jax.random.normal(ks[5], (DEPTH_2, CONV_WIDTH_2, D_MODEL), f32) * CONV_WIDTH_2 ** -0.5
    w_mix_out = jax.random.normal(ks[6], (DEPTH_2, D_MODEL, D_MODEL), f32) * D_MODEL ** -0.5
    norm_mlp = 1.0 + 0.02 * jax.random.normal(ks[7], (DEPTH_2, D_MODEL), f32)
    w_mlp_up = jax.random.normal(ks[8], (DEPTH_2, D_MODEL, MLP_HIDDEN), f32) * D_MODEL ** -0.5
    w_mlp_down = jax.random.normal(ks[9], (DEPTH_2, MLP_HIDDEN, D_MODEL), f32) * MLP_HIDDEN ** -0.5
    norm_final = 1.0 + 0.02 * jax.random.normal(ks[10], (D_MODEL,), f32)
    return {"x": x, "norm_mix": norm_mix, "w_in": w_in, "conv_w": conv_w,
            "w_attn_out": w_attn_out, "w_conv_out": w_conv_out, "w_mix_out": w_mix_out,
            "norm_mlp": norm_mlp, "w_mlp_up": w_mlp_up, "w_mlp_down": w_mlp_down,
            "norm_final": norm_final}

def second_block(x, norm_mix, w_in, conv_w, w_attn_out, w_conv_out, w_mix_out,
              norm_mlp, w_mlp_up, w_mlp_down, norm_final):
    B, T, D = x.shape
    cos, sin = rope_tables(T)
    offsets = np.cumsum(PROJ_SIZES)[:-1].tolist()
    for l in range(DEPTH_2):
        u = rmsnorm(x, norm_mix[l])
        proj = u @ w_in[l]
        q, k, v, iq, ik, iw, cB, cC, ch, g = jnp.split(proj, offsets, axis=-1)
        q = apply_partial_rope(q.reshape(B, T, ATTN_HEADS, HEAD_DIM), cos, sin)
        k = apply_partial_rope(k.reshape(B, T, ATTN_HEADS, HEAD_DIM), cos, sin)
        v = v.reshape(B, T, ATTN_HEADS, HEAD_DIM)
        iq = apply_partial_rope(iq.reshape(B, T, IDX_HEADS, IDX_DIM), cos, sin)
        ik = apply_partial_rope(ik[:, :, None, :], cos, sin)[:, :, 0, :]
        y_attn = dsa_attention(q, k, v, iq, ik, iw) @ w_attn_out[l]
        y_conv = (cB * short_conv(cC * ch, conv_w[l])) @ w_conv_out[l]
        gates = jax.nn.sigmoid(g.reshape(B, T, N_BRANCH, D))
        merged = gates[:, :, 0] * y_attn + gates[:, :, 1] * y_conv
        x = x + merged @ w_mix_out[l]
        u = rmsnorm(x, norm_mlp[l])
        x = x + jnp.square(jax.nn.relu(u @ w_mlp_up[l])) @ w_mlp_down[l]
    return rmsnorm(x, norm_final)


def setup_inputs(seed=0):
    out = dict(first_inputs(seed))
    for name, value in second_inputs(seed + 1).items():
        if name != "x":
            out[name + "_2"] = value
    return out


def reference(
    x, norm1_g, w_in, q_norm_g, k_norm_g, rpb, dw_kernel, dw_bias, conv_ln_g, conv_ln_b, w_out,
    norm2_g, w_gate, w_up, w_down, norm_mix_2, w_in_2, conv_w_2, w_attn_out_2, w_conv_out_2,
    w_mix_out_2, norm_mlp_2, w_mlp_up_2, w_mlp_down_2, norm_final_2,
):
    x = first_block(
        x, norm1_g, w_in, q_norm_g, k_norm_g, rpb, dw_kernel, dw_bias, conv_ln_g, conv_ln_b,
        w_out, norm2_g, w_gate, w_up, w_down,
    )
    return second_block(
        x, norm_mix_2, w_in_2, conv_w_2, w_attn_out_2, w_conv_out_2, w_mix_out_2, norm_mlp_2,
        w_mlp_up_2, w_mlp_down_2, norm_final_2,
    )


_drawn_inputs = setup_inputs


def setup_inputs(seed=0):
    import zlib

    import numpy as np

    out = dict(_drawn_inputs(seed))
    spreads = {}
    factors = {'q_norm_g': 5.871,
     'k_norm_g': 7.095,
     'conv_ln_g': 2.86,
     'conv_ln_b': 3.057,
     'norm_final_2': 23.686,
     'rpb': 7.03,
     'norm2_g': 4.217,
     'norm_mix_2': 3.178,
     'norm_mlp_2': 9.408}
    for name, (base, spread) in spreads.items():
        noise = np.random.default_rng([zlib.crc32(name.encode()), seed]).standard_normal(out[name].shape)
        drawn = base * np.exp(spread * noise) if base else spread * noise
        out[name] = __import__('jax').numpy.asarray(drawn.astype(out[name].dtype))
    for name, factor in factors.items():
        out[name] = (out[name] * factor).astype(out[name].dtype)
    return out
```

```python
from contextlib import ExitStack, contextmanager

import numpy as np
import concourse.bass as bass
from concourse import mybir

F32 = mybir.dt.float32
F32R = mybir.dt.float32r
ALU = mybir.AluOpType
ACT = mybir.ActivationFunctionType
AX_X = mybir.AxisListType.X

P = 128
D = 1024
T = 256
NT = T // P
KD = D // P
HEADS, DH = 8, 64
DA = HEADS * DH
KA = DA // P
GRID_W, NA_ROWS, NA_COLS = 64, 8, 16
GRID_ROWS = T // GRID_W
TAPS = 31
PAD = TAPS // 2
D_FF = 2816
D_MLP = 4096
LAYERS = 2
IDX_HEADS = 4
CHUNK, TOPK = 64, 64
CONV_K = 3
ROPE_HALF = 8
EPS = 1e-6
SCALE = DH ** -0.5
IDX_SCALE = (64 ** -0.5) * (IDX_HEADS ** -0.5)
OUTSIDE = -1e30
NOT_ADMISSIBLE = -1e38
TAKEN = -3e38

COLS = 256
UNIT = 2048
RING, SPLIT = 6, 3
FF_BLOCKS, MLP_BLOCKS = D_FF // COLS, D_MLP // COLS
A_OUT, A_FF = 10, 14
A_UNITS = A_FF + 3 * FF_BLOCKS
L_CONV, L_ATTN, L_MIX, L_MLP = 22, 26, 30, 34
L_UNITS = L_MLP + 2 * MLP_BLOCKS
LOOPS = 5
IQ0, IK0, CB0, CC0, CH0, G0 = 1536, 1792, 1860, 2372, 2884, 3396
IKW = 68
L_COLS = [IQ0, IK0, 0, 256, 512, 768, 1024, 1280, CC0, CC0 + 256, CH0, CH0 + 256, CB0, CB0 + 256] \
    + [G0 + COLS * i for i in range(8)]
A_COLS = [512, 0, 768, 256, 1024, 1280, 1536, 1792, 2048, 2304]
A_OUT_ROWS = [2, 3, 0, 1]

G_N1, G_N2, G_DWB, G_LNG, G_LNB, G_QG, G_KG, G_LAYER = 0, 8, 16, 20, 24, 28, 29, 30
LG_MIX, LG_MLP, LG_CONV, LG_N = 0, 8, 16, 28
G_N = G_LAYER + LAYERS * LG_N
LAYER_LINKS = 96
POOL_LINKS = 23
POOL_CHUNK = 0


class Unit:
    def __init__(self, st, turns=0):
        self.st, self.turns = st, turns
        self.slot, self.buf = st % RING, st % SPLIT
        self.landed = 16 * (st // RING + 1) + 16 * turns

    def upto(self, back=0):
        return self.st - back + 1 + RING * self.turns


class Chain:
    def __init__(self, eng, sem):
        self.eng, self.sem, self.n, self.run = eng, sem, 0, 0

    def link(self, ins):
        self.n += 1
        ins.then_inc(self.sem, 1)
        self.eng.wait_ge(self.sem, self.n + self.run)

    def link_apart(self, ins, scratch):
        self.link(ins)
        self.eng.memset(scratch, 0.0)

    @contextmanager
    def loop(self, turns, per):
        with self.eng.Fori(0, turns) as i:
            n, run = self.n, self.run
            self.run = run + per * i
            yield i
            assert self.n - n == per, (self.n - n, per)
            self.n, self.run = n + per * turns, run


def build(nc, d):
    w_in = d["w_in"][0].rearrange("(k p) n -> p k n", p=P)
    w_out = d["w_out"][0].rearrange("(k p) n -> p k n", p=P)
    w_gate = d["w_gate"][0].rearrange("(k p) n -> p k n", p=P)
    w_up = d["w_up"][0].rearrange("(k p) n -> p k n", p=P)
    w_down = d["w_down"][0].rearrange("(k p) n -> p k n", p=P)

    def per_layer(name):
        return d[name].rearrange("l (k p) n -> p l k n", p=P)

    w_in2, w_attn2, w_conv2 = per_layer("w_in_2"), per_layer("w_attn_out_2"), per_layer("w_conv_out_2")
    w_mix2, w_mup2, w_mdown2 = per_layer("w_mix_out_2"), per_layer("w_mlp_up_2"), per_layer("w_mlp_down_2")

    with ExitStack() as ctx:
        def sb(name, shape, dt=F32):
            return ctx.enter_context(nc.sbuf_tensor(name, shape, dt))

        def sem(name):
            return ctx.enter_context(nc.semaphore(name))

        raw = sb("raw", [P, RING, UNIT])
        whi = sb("whi", [P, SPLIT, UNIT], F32R)
        wlo = sb("wlo", [P, SPLIT, UNIT], F32R)
        x = sb("x", [P, NT, D])
        xn = sb("xn", [P, 4, 512])
        uhi = sb("uhi", [P, KD, T], F32R)
        ulo = sb("ulo", [P, KD, T], F32R)
        mhi = sb("mhi", [P, KD, T], F32R)
        mlo = sb("mlo", [P, KD, T], F32R)
        big = sb("big", [P, 16, T])
        qtok = sb("qtok", [P, NT, DA])
        ktok = sb("ktok", [P, NT, DA])
        vtok = sb("vtok", [P, NT, DA])
        qT = sb("qT", [P, KA, T])
        kT = sb("kT", [P, KA, T])
        prob = sb("prob", [P, 2, NT * T])
        wk = sb("wk", [P, NT, T])
        cu = sb("cu", [P, KA, T + 2 * PAD])
        y = sb("y", [P, KA, T])
        cB = sb("cB", [P, KA, T])
        ident = sb("ident", [P, P])
        ones = sb("ones", [P, P])
        grow = sb("grow", [P, P])
        krow = sb("krow", [P, P])
        gcol = sb("gcol", [P, G_N])
        kcol = sb("kcol", [P, TAPS * KA])
        lg = sb("lg", [P, LG_N])
        rope = sb("rope", [P, NT, 2 * ROPE_HALF])
        iw = sb("iw", [P, NT, IDX_HEADS])
        ss = sb("ss", [P, 16])
        sd = sb("sd", [P, 16])
        rn = sb("rn", [P, 16])
        mx = sb("mx", [P, 2, NT])
        nmx = sb("nmx", [P, 2, NT])
        den = sb("den", [P, 2, NT])
        rden = sb("rden", [P, 2, NT])
        m8 = sb("m8", [P, 8])
        apart = sb("apart", [P, 1])
        eps = sb("eps", [P, 1])
        zeros = sb("zeros", [P, 512], mybir.dt.bfloat16)
        rtmp = sb("rtmp", [P, 4, NT * HEADS * ROPE_HALF])
        itmp = sb("itmp", [P, 4, NT * IDX_HEADS * ROPE_HALF])
        xnt = xn[:].rearrange("p (t a) b -> p t (a b)", t=NT)
        score = [xn[:, 0, :].rearrange("p (t k) -> p t k", t=NT), xn[:, 1, :].rearrange("p (t k) -> p t k", t=NT)]
        expo = [xn[:, 2, :].rearrange("p (t k) -> p t k", t=NT), xn[:, 3, :].rearrange("p (t k) -> p t k", t=NT)]
        iqtok = y[:, 0:2, :]
        iktok = y[:, 2, :].rearrange("p (t c) -> p t c", t=NT)
        iqT = prob[:, 0, :].rearrange("p (c t) -> p c t", c=2)
        ikT = prob[:, 1, 0:T]
        cC = qtok[:].rearrange("p a (b t) -> p (a b) t", t=T)
        cH = ktok[:].rearrange("p a (b t) -> p (a b) t", t=T)
        lnsq, lne = cC, cH
        gfin = qT[:].rearrange("p a b -> p (a b)")
        ff_e = [xn[:, 0, :], xn[:, 1, :]]
        ff_h = [xn[:, 2, :], xn[:, 3, :]]
        mlp_h = [xn[:, 0, :], xn[:, 1, :], xn[:, 2, :]]
        bias = big[:].rearrange("p (t h) k -> p t h k", t=NT)

        acc = [ctx.enter_context(nc.psum_tensor(f"acc{i}", [P, 512], F32)) for i in range(4)]
        col = [ctx.enter_context(nc.psum_tensor(f"col{i}", [P, 512], F32)) for i in range(4)]
        S_BANK, T_BANK, O_BANK = (acc[0], acc[1]), acc[2], acc[3]
        MU, VAR = col[0], col[1]

        landed = [sem(f"landed{i}") for i in range(RING)]
        w_hi = sem("w_hi")
        w_lo = sem("w_lo")
        used = sem("used")
        x_in = sem("x_in")
        par_in = sem("par_in")
        rope_in = sem("rope_in")
        skew_in = sem("skew_in")
        bias_in = sem("bias_in")
        gfin_in = sem("gfin_in")
        out_done = sem("out_done")
        consts = sem("consts")
        par_ps = sem("par_ps")
        par_sb = sem("par_sb")
        bias_ok = sem("bias_ok")
        x_new = sem("x_new")
        sq_done = sem("sq_done")
        sd_done = sem("sd_done")
        xn_ok = sem("xn_ok")
        u_ps = sem("u_ps")
        u_hi = sem("u_hi")
        u_lo = sem("u_lo")
        evac = sem("evac")
        glu = sem("glu")
        qsq = sem("qsq")
        qss = sem("qss")
        qsd = sem("qsd")
        qk_tok = sem("qk_tok")
        rope_tok = sem("rope_tok")
        qk_ps = sem("qk_ps")
        qk_T = sem("qk_T")
        s_ps = sem("s_ps")
        s_max = sem("s_max")
        s_exp = sem("s_exp")
        p_ok = sem("p_ok")
        p_ps = sem("p_ps")
        p_T = sem("p_T")
        o_ps = sem("o_ps")
        o_hi = sem("o_hi")
        o_lo = sem("o_lo")
        conv_dve = sem("conv_dve")
        conv_pool = sem("conv_pool")
        ln_mu = sem("ln_mu")
        ln_xc = sem("ln_xc")
        ln_sq = sem("ln_sq")
        ln_var = sem("ln_var")
        ln_sd = sem("ln_sd")
        ln_y = sem("ln_y")
        ln_e = sem("ln_e")
        c_ok = sem("c_ok")
        c_hi = sem("c_hi")
        c_lo = sem("c_lo")
        idx_tok = sem("idx_tok")
        idx_ps = sem("idx_ps")
        idx_T = sem("idx_T")
        lgt_ps = sem("lgt_ps")
        lgt_sb = sem("lgt_sb")
        lg_ok = sem("lg_ok")
        mask_ok = sem("mask_ok")
        merge_rd = sem("merge_rd")
        g_hi = sem("g_hi")
        g_lo = sem("g_lo")
        ff_exp = sem("ff_exp")
        ff_ok = sem("ff_ok")
        ff_hi = sem("ff_hi")
        ff_lo = sem("ff_lo")
        fin = sem("fin")
        dve_chain = sem("dve_chain")
        act_chain = sem("act_chain")
        pool_chain = sem("pool_chain")

        def whi_v(u, n=COLS):
            return whi[:, u.buf, :].rearrange("p (k n) -> p k n", n=n)

        def wlo_v(u, n=COLS):
            return wlo[:, u.buf, :].rearrange("p (k n) -> p k n", n=n)

        def ikw_v(buf):
            return buf[:, 0:KD * IKW].rearrange("p (k n) -> p k n", n=IKW)

        def unit_size(layer, j):
            if layer and j == 1:
                return KD * IKW
            return KA * COLS if layer and L_CONV <= j < L_MIX else UNIT

        def a_unit(j, turns=0):
            return Unit(j, turns)

        def l_unit(l, j, turns=0):
            return Unit(A_UNITS + j, L_UNITS // RING * l + turns)

        def rotate(eng, link, v, nh, tmp):
            x1, x2 = v[:, :, :, 0:ROPE_HALF], v[:, :, :, ROPE_HALF:2 * ROPE_HALF]
            cos = rope[:, :, 0:ROPE_HALF].unsqueeze(2).broadcast_to([P, NT, nh, ROPE_HALF])
            sin = rope[:, :, ROPE_HALF:2 * ROPE_HALF].unsqueeze(2).broadcast_to([P, NT, nh, ROPE_HALF])
            x1c, x2s, x2c, x1s = (tmp[:, r, 0:NT * nh * ROPE_HALF].rearrange("p (t h r) -> p t h r", t=NT, h=nh)
                                  for r in range(4))
            eng.tensor_tensor(x1c, x1, cos, ALU.mult)
            eng.tensor_tensor(x2s, x2, sin, ALU.mult)
            eng.tensor_tensor(x2c, x2, cos, ALU.mult)
            link(eng.tensor_tensor(x1s, x1, sin, ALU.mult))
            eng.tensor_tensor(x1, x1c, x2s, ALU.subtract)
            return eng.tensor_tensor(x2, x2c, x1s, ALU.add)

        def mid(buf, s):
            return buf[:, 2 * s:2 * s + 2, :]

        block = ctx.enter_context(nc.Block())

        @block.sync
        def _(sp):
            def load(u, src, size=UNIT, free=...):
                free = u if free is ... else free
                if free is not None and not (isinstance(u.turns, int) and u.st < RING):
                    sp.wait_ge(w_lo, free.upto(RING))
                dst = raw[:, u.slot, 0:size].rearrange("p (k n) -> p k n", n=src.shape[-1])
                sp.dma_start(dst, src).then_inc(landed[u.slot], 16)

            sp.dma_start(x[:], d["x"][0].rearrange("(t p) n -> p t n", p=P)).then_inc(x_in, 16)
            load(a_unit(0), w_in[:, :, A_COLS[0]:A_COLS[0] + COLS])
            rows = [("norm1_g", G_N1), ("norm2_g", G_N2), ("dw_bias", G_DWB), ("conv_ln_g", G_LNG), ("conv_ln_b", G_LNB)]
            for name, at in rows:
                n = d[name].shape[1] // P
                sp.dma_start(grow[at:at + n, :], d[name][0].rearrange("(k p) -> k p", p=P)).then_inc(par_in, 16)
            for name, at in (("q_norm_g", G_QG), ("k_norm_g", G_KG)):
                for half in range(2):
                    sp.dma_start(grow[at:at + 1, half * DH:half * DH + DH], d[name]).then_inc(par_in, 16)
            for l in range(LAYERS):
                at = G_LAYER + l * LG_N
                sp.dma_start(grow[at:at + 8, :], d["norm_mix_2"][l].rearrange("(k p) -> k p", p=P)).then_inc(par_in, 16)
                sp.dma_start(grow[at + 8:at + 16, :], d["norm_mlp_2"][l].rearrange("(k p) -> k p", p=P)).then_inc(par_in, 16)
                sp.dma_start(grow[at + 16:at + 28, :], d["conv_w_2"][l].rearrange("w (c p) -> (w c) p", p=P)).then_inc(par_in, 16)
            sp.dma_start(krow[0:TAPS * KA, :], d["dw_kernel"][0].rearrange("w (c p) -> (w c) p", p=P)).then_inc(par_in, 16)
            for j in range(1, A_OUT):
                load(a_unit(j), w_in[:, :, A_COLS[j]:A_COLS[j] + COLS])
                if j == 2:
                    sp.dma_start(rope[:], d["rope"].rearrange("(t p) n -> p t n", p=P)).then_inc(rope_in, 16)
            for i, r in enumerate(A_OUT_ROWS):
                load(a_unit(A_OUT + i), w_out[:, 2 * r:2 * r + 2, :])
            load(a_unit(A_FF), w_gate[:, :, 0:COLS])
            load(a_unit(A_FF + 1), w_up[:, :, 0:COLS])
            with sp.Fori(0, LOOPS) as i:
                for q in range(2):
                    at = i * (2 * COLS) + (1 + q) * COLS
                    load(a_unit(A_FF + 2 + 3 * q, i), w_gate[:, :, bass.ds(at, COLS)])
                    load(a_unit(A_FF + 3 + 3 * q, i), w_up[:, :, bass.ds(at, COLS)])
                    load(a_unit(A_FF + 4 + 3 * q, i), w_down[:, bass.ds(i * 4 + 2 * q, 2), :])
            load(a_unit(A_UNITS - 1), w_down[:, 2 * FF_BLOCKS - 2:2 * FF_BLOCKS, :])

            with sp.Fori(0, LAYERS) as l:
                def of(w):
                    return w[:, bass.ds(l, 1)].rearrange("p l k n -> p (l k) n")
                for j in range(L_CONV):
                    n = IKW if j == 1 else COLS
                    load(l_unit(l, j), of(w_in2)[:, :, L_COLS[j]:L_COLS[j] + n], KD * n,
                         None if j == 2 else l_unit(l, 2 if j == 1 else j))
                for at, w in ((L_CONV, w_conv2), (L_ATTN, w_attn2)):
                    for i in range(4):
                        load(l_unit(l, at + i), of(w)[:, :, COLS * i:COLS * i + COLS], KA * COLS)
                for i in range(4):
                    load(l_unit(l, L_MIX + i), of(w_mix2)[:, 2 * i:2 * i + 2, :])
                load(l_unit(l, L_MLP), of(w_mup2)[:, :, 0:COLS])
                with sp.Fori(0, LOOPS) as i:
                    for q in range(3):
                        load(l_unit(l, L_MLP + 1 + 2 * q, i), of(w_mup2)[:, :, bass.ds(i * (3 * COLS) + (1 + q) * COLS, COLS)])
                        load(l_unit(l, L_MLP + 2 + 2 * q, i), of(w_mdown2)[:, bass.ds(i * 6 + 2 * q, 2), :])
                load(l_unit(l, L_UNITS - 1), of(w_mdown2)[:, 2 * MLP_BLOCKS - 2:2 * MLP_BLOCKS, :])
            sp.wait_ge(w_lo, A_UNITS + LAYERS * L_UNITS - 2)
            sp.dma_start(gfin, d["norm_final_2"].partition_broadcast(P)).then_inc(gfin_in, 16)
            for t in range(NT):
                sp.wait_ge(fin, t + 1)
                sp.dma_start(d["out"][0, t * P:(t + 1) * P, :], xnt[:, t, :]).then_inc(out_done, 16)
            sp.wait_ge(out_done, 16 * NT)

        PAR_DMAS = 5 + 4 + 3 * LAYERS + 1

        @block.tensor
        def _(pe):
            def mm3(out, l_hi, l_lo, r_hi, r_lo, start, stop):
                pe.matmul(out, l_hi, r_hi, start=start, stop=False)
                pe.matmul(out, l_hi, r_lo, start=False, stop=False)
                return pe.matmul(out, l_lo, r_hi, start=False, stop=stop)

            def col_tokens(u, bank, w=COLS, norm=None):
                hi, lo = (ikw_v(whi[:, u.buf, :]), ikw_v(wlo[:, u.buf, :])) if w == IKW else (whi_v(u), wlo_v(u))
                for t in range(NT):
                    for k in range(KD):
                        if norm is not None and t == 0:
                            pe.wait_ge(u_lo, norm * KD + k + 1)
                        tok = slice(t * P, t * P + P)
                        mm = mm3(bank[:, t * w:t * w + w], uhi[:, k, tok], ulo[:, k, tok], hi[:, k, :], lo[:, k, :],
                                 k == 0, k == KD - 1)
                mm.then_inc(used, 1)

            def col_features(u, bank, hi_in, lo_in, kc=KD, norm=None):
                for c in range(COLS // P):
                    for k in range(kc):
                        if norm is not None and c == 0:
                            pe.wait_ge(u_lo, norm * KD + k + 1)
                        cs = slice(c * P, c * P + P)
                        mm = mm3(bank[:, c * T:c * T + T], whi_v(u)[:, k, cs], wlo_v(u)[:, k, cs],
                                 hi_in[:, k, :], lo_in[:, k, :], k == 0, k == kc - 1)
                mm.then_inc(used, 1)

            def rows(u, hi_in, lo_in, start, stop):
                for t in range(NT):
                    for h in range(2):
                        for c in range(2):
                            tok = slice(t * P, t * P + P)
                            cs = slice(h * 512, h * 512 + 512)
                            mm = mm3(acc[2 * t + h][:], hi_in[:, c, tok], lo_in[:, c, tok],
                                     whi_v(u, D)[:, c, cs], wlo_v(u, D)[:, c, cs], start and c == 0, stop and c == 1)
                mm.then_inc(used, 1)

            def norm_transposes(k):
                for t in range(NT):
                    pe.wait_ge(xn_ok, NT * k + t + 1)
                    for b in range(4):
                        for c in range(2):
                            f = 2 * b + c
                            tr = pe.transpose(acc[b][:, c * T + t * P:c * T + t * P + P], xnt[:, t, f * P:f * P + P], ident[:])
                        if t == NT - 1:
                            tr.then_inc(u_ps, 1)

            def turn(tok, n):
                for b in range(2):
                    bank = acc[2 * n + b]
                    for c in range(2):
                        for t in range(NT):
                            f = 2 * b + c
                            tr = pe.transpose(bank[:, c * T + t * P:c * T + t * P + P], tok[:, t, f * P:f * P + P], ident[:])
                    tr.then_inc(qk_ps, 1)

            def scores(a, h):
                pe.wait_ge(qk_T, 4 * a + 4)
                if h >= 2:
                    pe.wait_ge(s_max, HEADS * a + h - 1)
                off = DH * (h % 2)
                for t in range(NT):
                    mm = pe.matmul(S_BANK[h % 2][:, t * T:t * T + T], qT[off:off + DH, h // 2, t * P:t * P + P],
                                   kT[off:off + DH, h // 2, :], start=True, stop=True)
                mm.then_inc(s_ps, 1)

            def turn_probs(a, h):
                pe.wait_ge(p_ok, HEADS * a + h + 1)
                if h >= 1:
                    pe.wait_ge(p_T, HEADS * a + h)
                for kt in range(NT):
                    for t in range(NT):
                        tr = pe.transpose(T_BANK[:, kt * T + t * P:kt * T + t * P + P],
                                          expo[h % 2][:, t, kt * P:kt * P + P], ident[:])
                tr.then_inc(p_ps, 1)

            def values(a, h):
                pe.wait_ge(p_T, HEADS * a + h + 1)
                if h % 2 == 0 and h >= 2:
                    pe.wait_ge(o_lo, HEADS // 2 * a + h // 2)
                off = DH * (h % 2)
                for kt in range(NT):
                    mm = pe.matmul(O_BANK[off:off + DH, 0:T], vtok[:, kt, h * DH:h * DH + DH],
                                   prob[:, h % 2, kt * T:kt * T + T], start=kt == 0, stop=kt == NT - 1)
                mm.then_inc(o_ps, 1)

            pe.wait_ge(consts, 4)
            pe.wait_ge(par_in, 16 * PAR_DMAS)
            pe.transpose(col[2][:, 0:G_N], grow[0:G_N, :], ident[0:G_N, 0:G_N])
            pe.transpose(col[3][:, 0:TAPS * KA], krow[0:TAPS * KA, :], ident[0:TAPS * KA, 0:TAPS * KA]).then_inc(par_ps, 1)

            norm_transposes(0)
            for j in range(A_OUT):
                u = a_unit(j)
                pe.wait_ge(w_lo, u.upto())
                if j >= 4:
                    pe.wait_ge(evac, j - 3)
                if j < 4:
                    col_features(u, col[j % 4], uhi, ulo, norm=0 if j == 0 else None)
                else:
                    col_tokens(u, col[j % 4])
                if j == 6:
                    pe.wait_ge(qk_tok, 1)
                    turn(qtok, 0)
                if j == 8:
                    pe.wait_ge(qk_tok, 2)
                    turn(ktok, 1)
            pe.wait_ge(evac, A_OUT)
            scores(0, 0)
            for h in range(HEADS):
                if h + 1 < HEADS:
                    scores(0, h + 1)
                turn_probs(0, h)
                if h >= 1:
                    values(0, h - 1)
            values(0, HEADS - 1)
            pe.wait_ge(conv_dve, 1)
            pe.wait_ge(conv_pool, 1)
            for c in range(KA):
                mm = pe.matmul(MU[:, 0:T], ones[:], y[:, c, :], start=c == 0, stop=c == KA - 1)
            mm.then_inc(ln_mu, 1)
            pe.wait_ge(ln_sq, 1)
            for c in range(KA):
                mm = pe.matmul(VAR[:, 0:T], ones[:], lnsq[:, c, :], start=c == 0, stop=c == KA - 1)
            mm.then_inc(ln_var, 1)
            for i, r in enumerate(A_OUT_ROWS):
                u = a_unit(A_OUT + i)
                pe.wait_ge(w_lo, u.upto())
                if i == 0:
                    pe.wait_ge(o_lo, HEADS // 2)
                if i == 2:
                    pe.wait_ge(c_lo, 1)
                rows(u, mhi[:, 2 * r:2 * r + 2, :], mlo[:, 2 * r:2 * r + 2, :], i == 0, i == 3)

            def open_acc():
                for bank in acc:
                    pe.matmul(bank[:], zeros[:, 0:P], zeros[:], start=True, stop=False)

            norm_transposes(1)
            pe.wait_ge(w_lo, a_unit(A_FF).upto())
            col_features(a_unit(A_FF), col[0], uhi, ulo, norm=1)
            pe.wait_ge(w_lo, a_unit(A_FF + 1).upto())
            col_features(a_unit(A_FF + 1), col[1], uhi, ulo)
            pe.wait_ge(u_lo, 2 * KD)
            open_acc()
            with pe.Fori(0, LOOPS) as i:
                for q in range(2):
                    gate, up, down = (a_unit(A_FF + 2 + 3 * q + r, i) for r in range(3))
                    bank = 2 * ((1 + q) % 2)
                    pe.wait_ge(w_lo, gate.upto())
                    col_features(gate, col[bank], uhi, ulo)
                    pe.wait_ge(w_lo, up.upto())
                    col_features(up, col[bank + 1], uhi, ulo)
                    pe.wait_ge(w_lo, down.upto())
                    pe.wait_ge(ff_lo, 2 * i + q + 1)
                    rows(down, mid(mhi, q), mid(mlo, q), False, False)
            pe.wait_ge(w_lo, a_unit(A_UNITS - 1).upto())
            pe.wait_ge(ff_lo, FF_BLOCKS)
            rows(a_unit(A_UNITS - 1), mid(mhi, 0), mid(mlo, 0), False, True)

            with pe.Fori(0, LAYERS) as l:
                norm_transposes(2 + 2 * l)
                for j in range(L_CONV):
                    u = l_unit(l, j)
                    pe.wait_ge(w_lo, u.upto())
                    if j >= 4:
                        pe.wait_ge(evac, A_OUT + L_CONV * l + j - 3)
                    if j < 8:
                        col_tokens(u, col[j % 4], IKW if j == 1 else COLS, norm=2 + 2 * l if j == 0 else None)
                    else:
                        col_features(u, col[j % 4], uhi, ulo)
                    if j == 3:
                        pe.wait_ge(idx_tok, 2 * l + 2)
                        for c in range(2):
                            for t in range(NT):
                                pe.transpose(acc[0][:, c * T + t * P:c * T + t * P + P],
                                             iqtok[:, t, c * P:c * P + P], ident[:])
                        for t in range(NT):
                            tr = pe.transpose(acc[1][:, t * P:t * P + P], iktok[:, t, :], ident[:])
                        tr.then_inc(idx_ps, 1)
                    if j == 4:
                        pe.wait_ge(idx_T, 2 * l + 2)
                        for h in range(IDX_HEADS):
                            off = 64 * (h % 2)
                            for t in range(NT):
                                mm = pe.matmul(acc[h][:, t * T:t * T + T], iqT[off:off + 64, h // 2, t * P:t * P + P],
                                               ikT[off:off + 64, :], start=True, stop=True)
                        mm.then_inc(lgt_ps, 1)
                    if j == 6:
                        pe.wait_ge(lgt_sb, IDX_HEADS * l + IDX_HEADS)
                        pe.wait_ge(rope_tok, 2 * l + 1)
                        turn(qtok, 0)
                    if j == 7:
                        pe.wait_ge(rope_tok, 2 * l + 2)
                        turn(ktok, 1)
                    if j == 13:
                        scores(1 + l, 0)
                    if j >= 14:
                        h = j - 14
                        if h + 1 < HEADS:
                            scores(1 + l, h + 1)
                        turn_probs(1 + l, h)
                        if h >= 1:
                            values(1 + l, h - 1)
                for i in range(4):
                    u = l_unit(l, L_CONV + i)
                    pe.wait_ge(w_lo, u.upto())
                    pe.wait_ge(evac, A_OUT + L_CONV * l + 19 + i)
                    if i == 0:
                        pe.wait_ge(c_lo, 2 + l)
                    col_features(u, col[i], mhi[:, 0:KA, :], mlo[:, 0:KA, :], KA)
                    if i == 0:
                        values(1 + l, HEADS - 1)
                for i in range(4):
                    u = l_unit(l, L_ATTN + i)
                    pe.wait_ge(w_lo, u.upto())
                    pe.wait_ge(merge_rd, 8 * l + i + 1)
                    if i == 0:
                        pe.wait_ge(o_lo, HEADS // 2 * (2 + l))
                    col_features(u, col[i], mhi[:, KA:KD, :], mlo[:, KA:KD, :], KA)
                for i in range(4):
                    u = l_unit(l, L_MIX + i)
                    pe.wait_ge(w_lo, u.upto())
                    pe.wait_ge(g_lo, 4 * l + i + 1)
                    rows(u, uhi[:, 2 * i:2 * i + 2, :], ulo[:, 2 * i:2 * i + 2, :], i == 0, i == 3)

                norm_transposes(3 + 2 * l)
                u = l_unit(l, L_MLP)
                pe.wait_ge(w_lo, u.upto())
                col_features(u, col[0], uhi, ulo, norm=3 + 2 * l)
                open_acc()
                with pe.Fori(0, LOOPS) as i:
                    for q in range(3):
                        up, down = l_unit(l, L_MLP + 1 + 2 * q, i), l_unit(l, L_MLP + 2 + 2 * q, i)
                        done = FF_BLOCKS + MLP_BLOCKS * l + 3 * i + q
                        pe.wait_ge(w_lo, up.upto())
                        col_features(up, col[(1 + q) % 3], uhi, ulo)
                        pe.wait_ge(w_lo, down.upto())
                        pe.wait_ge(ff_lo, done + 1)
                        rows(down, mid(mhi, q), mid(mlo, q), False, False)
                pe.wait_ge(w_lo, l_unit(l, L_UNITS - 1).upto())
                pe.wait_ge(ff_lo, FF_BLOCKS + MLP_BLOCKS * l + MLP_BLOCKS)
                rows(l_unit(l, L_UNITS - 1), mid(mhi, 0), mid(mlo, 0), False, True)

        @block.scalar
        def _(act):
            chain = Chain(act, act_chain)

            def split(u, size=UNIT):
                act.wait_ge(landed[u.slot], u.landed)
                if not (isinstance(u.turns, int) and u.st < SPLIT):
                    act.wait_ge(used, u.upto(SPLIT))
                act.activation(whi[:, u.buf, 0:size], raw[:, u.slot, 0:size], ACT.Copy).then_inc(w_hi, 1)

            def squares(r):
                for t in range(NT):
                    if isinstance(r, int) and r == 0:
                        act.wait_ge(x_in, 16)
                    else:
                        act.wait_ge(x_new, NT * (r - 1) + t + 1)
                    act.activation(xnt[:, t, :], x[:, t, :], ACT.Square, accum_out=ss[:, t:t + 1]).then_inc(sq_done, 1)
                    act.wait_ge(sq_done, NT * r + t + 1)
                    act.activation(sd[:, t:t + 1], ss[:, t:t + 1], ACT.Sqrt, bias=eps[:, 0:1], scale=1.0 / D)\
                        .then_inc(sd_done, 1)

            def u_split(k, gain, at):
                for b in range(4):
                    act.wait_ge(u_ps, 4 * k + b + 1)
                    for c in range(2):
                        f = 2 * b + c
                        act.activation(uhi[:, f, :], acc[b][:, c * T:c * T + T], ACT.Copy,
                                       scale=gain[:, at + f:at + f + 1]).then_inc(u_hi, 1)

            def exps(a, h):
                act.wait_ge(s_max, HEADS * a + h + 1)
                if h >= 2:
                    act.wait_ge(p_ps, HEADS * a + h - 1)
                for t in range(NT):
                    act.activation(expo[h % 2][:, t, :], score[h % 2][:, t, :], ACT.Exp, bias=nmx[:, h % 2, t:t + 1],
                                   accum_out=den[:, h % 2, t:t + 1]).then_inc(s_exp, 1)

            def copy_probs(a, h):
                act.wait_ge(p_ps, HEADS * a + h + 1)
                if h >= 2:
                    act.wait_ge(o_ps, HEADS * a + h - 1)
                act.activation(prob[:, h % 2, :], T_BANK[:], ACT.Copy).then_inc(p_T, 1)

            def o_split(a, p):
                act.wait_ge(o_ps, HEADS * a + 2 * p + 2)
                act.activation(mhi[:, KA + p, :], O_BANK[:, 0:T], ACT.Copy).then_inc(o_hi, 1)

            def evacuate(n, j, dst, w=COLS):
                act.wait_ge(used, n.upto())
                act.activation(dst, col[j % 4][:, 0:NT * w].rearrange("p (t c) -> p t c", t=NT), ACT.Copy)\
                    .then_inc(evac, 1)

            def half(tok, i):
                return tok[:, :, COLS * i:COLS * i + COLS]

            def copy_turned(a, n, dst, gain=1.0):
                for b in range(2):
                    act.wait_ge(qk_ps, 4 * a + 2 * n + b + 1)
                    act.activation(dst[:, 2 * b:2 * b + 2, :], acc[2 * n + b][:].rearrange("p (c t) -> p c t", c=2),
                                   ACT.Copy, scale=gain).then_inc(qk_T, 1)

            act.wait_ge(par_ps, 1)
            act.activation(gcol[:], col[2][:, 0:G_N], ACT.Copy).then_inc(par_sb, 1)
            act.activation(kcol[:], col[3][:, 0:TAPS * KA], ACT.Copy).then_inc(par_sb, 1)
            act.wait_ge(consts, 4)
            squares(0)
            split(a_unit(0))
            act.wait_ge(par_sb, 2)
            u_split(0, gcol, G_N1)
            split(a_unit(1))
            for j in range(A_OUT):
                u = a_unit(j)
                split(a_unit(j + 2))
                if j == 6 or j == 8:
                    n = (j - 6) // 2
                    act.wait_ge(evac, j)
                    act.activation(xn[:, 0:2, :], (qtok, ktok)[n][:], ACT.Square).then_inc(qsq, 1)
                    act.wait_ge(qss, n + 1)
                    act.activation(sd[:], ss[:], ACT.Sqrt, bias=eps[:, 0:1], scale=1.0 / DH).then_inc(qsd, 1)
                if j == 7:
                    copy_turned(0, 0, qT, gcol[:, G_QG:G_QG + 1])
                if j == 9:
                    copy_turned(0, 1, kT, gcol[:, G_KG:G_KG + 1])
                if j in (0, 2):
                    if j == 2:
                        act.wait_ge(glu, 1)
                    act.wait_ge(used, u.upto())
                    act.activation(vtok[:, 0, :], col[j % 4][:], ACT.Exp, scale=-1.0).then_inc(evac, 1)
                elif j in (1, 3):
                    act.wait_ge(used, u.upto())
                    act.activation(vtok[:, 1, :], col[j % 4][:], ACT.Copy).then_inc(evac, 1)
                else:
                    if j == 8:
                        act.wait_ge(glu, 2)
                    evacuate(u, j, half((qtok, ktok, vtok)[(j - 4) // 2], j % 2))
            for h in range(HEADS):
                exps(0, h)
                copy_probs(0, h)
                if h % 2 == 0 and h >= 2:
                    o_split(0, h // 2 - 1)
            o_split(0, 3)
            act.wait_ge(ln_xc, 1)
            act.activation(lnsq, y[:], ACT.Square).then_inc(ln_sq, 1)
            act.wait_ge(ln_var, 1)
            act.activation(xn[:, 0, 0:T], VAR[:, 0:T], ACT.Sqrt, bias=eps[:, 0:1]).then_inc(ln_sd, 1)
            act.wait_ge(ln_y, 1)
            for c in range(KA):
                chain.link(act.activation(y[:, c, :], y[:, c, :], ACT.Identity, bias=gcol[:, G_LNB + c:G_LNB + c + 1],
                                          scale=gcol[:, G_LNG + c:G_LNG + c + 1]))
            act.activation(lne, y[:], ACT.Exp, scale=-1.0).then_inc(ln_e, 1)
            act.wait_ge(c_ok, 1)
            act.activation(mhi[:, 0:KA, :], y[:], ACT.Copy).then_inc(c_hi, 1)
            for j in range(A_OUT, A_FF):
                split(a_unit(j + 2))
            squares(1)
            u_split(1, gcol, G_N2)

            def ff_gate(b, q, n, bank):
                act.wait_ge(used, n.upto())
                act.activation(ff_e[q], col[bank][:], ACT.Exp, scale=-1.0).then_inc(ff_exp, 1)

            def ff_split(h, s, count):
                act.wait_ge(ff_ok, count)
                act.activation(mid(mhi, s), h.rearrange("p (c t) -> p c t", c=2), ACT.Copy).then_inc(ff_hi, 1)

            split(a_unit(A_FF + 2))
            ff_gate(0, 0, a_unit(A_FF), 0)
            ff_split(ff_h[0], 0, 1)
            with act.Fori(0, LOOPS) as i:
                for q in range(2):
                    j = A_FF + 2 + 3 * q
                    b = (1 + q) % 2
                    split(a_unit(j + 1, i))
                    split(a_unit(j + 2, i))
                    ff_gate(None, b, a_unit(j, i), 2 * b)
                    split(a_unit(j + 3, i))
                    ff_split(ff_h[b], b, 2 * i + q + 2)

            with act.Fori(0, LAYERS) as l:
                n0 = A_OUT + L_CONV * l
                split(l_unit(l, 0))
                squares(2 + 2 * l)
                act.wait_ge(lg_ok, l + 1)
                u_split(2 + 2 * l, lg, LG_MIX)
                split(l_unit(l, 1), KD * IKW)
                for j in range(L_CONV):
                    u = l_unit(l, j)
                    split(l_unit(l, j + 2), unit_size(True, j + 2))
                    if j == 4:
                        act.wait_ge(idx_ps, l + 1)
                        act.activation(iqT, acc[0][:].rearrange("p (c t) -> p c t", c=2), ACT.Copy).then_inc(idx_T, 1)
                        act.activation(ikT, acc[1][:, 0:T], ACT.Copy).then_inc(idx_T, 1)
                    if j == 5:
                        act.wait_ge(lgt_ps, l + 1)
                        for h in range(IDX_HEADS):
                            act.activation(big[:, 2 * h:2 * h + 2, :], acc[h][:].rearrange("p (t k) -> p t k", t=NT),
                                           ACT.Relu).then_inc(lgt_sb, 1)
                    if j == 7:
                        copy_turned(1 + l, 0, qT)
                    if j == 8:
                        copy_turned(1 + l, 1, kT)
                    if j >= 14:
                        exps(1 + l, j - 14)
                        if j % 2 == 1 and j >= 17:
                            o_split(1 + l, (j - 17) // 2)
                    if j == 0:
                        evacuate(u, j, iqtok)
                    elif j == 1:
                        act.wait_ge(used, u.upto())
                        ikw = col[1][:, 0:NT * IKW].rearrange("p (t c) -> p t c", t=NT)
                        act.activation(iktok[:, :, 0:64], ikw[:, :, 0:64], ACT.Copy)
                        act.activation(iw[:], ikw[:, :, 64:68], ACT.Copy, scale=IDX_SCALE).then_inc(evac, 1)
                    elif j < 8:
                        evacuate(u, j, half((qtok, ktok, vtok)[(j - 2) // 2], j % 2))
                    elif j < 14:
                        i = (j - 8) % 2
                        evacuate(u, j, (cC, cH, cB)[(j - 8) // 2][:, 2 * i:2 * i + 2, :])
                    else:
                        act.wait_ge(used, u.upto())
                        act.activation(big[:, 2 * (j - 14):2 * (j - 14) + 2, :],
                                       col[j % 4][:].rearrange("p (c t) -> p c t", c=2), ACT.Exp, scale=-1.0)\
                            .then_inc(evac, 1)
                    if j == 16:
                        act.wait_ge(c_ok, 2 + l)
                        act.activation(mhi[:, 0:KA, :], y[:], ACT.Copy).then_inc(c_hi, 1)
                    if j >= 14:
                        copy_probs(1 + l, j - 14)
                for j in range(L_CONV, L_MLP):
                    if j < L_MLP - 1:
                        split(l_unit(l, j + 2), unit_size(True, j + 2))
                    if j == L_CONV:
                        o_split(1 + l, 3)
                    if j > L_ATTN and j <= L_MIX:
                        i = j - L_ATTN - 1
                        act.wait_ge(merge_rd, 8 * l + 4 + i + 1)
                        act.activation(uhi[:, 2 * i:2 * i + 2, :], big[:, 2 * i:2 * i + 2, :], ACT.Copy).then_inc(g_hi, 1)
                squares(3 + 2 * l)
                u_split(3 + 2 * l, lg, LG_MLP)
                done = FF_BLOCKS + MLP_BLOCKS * l

                def relu(s, up):
                    act.wait_ge(used, up.upto())
                    act.activation(mlp_h[s], col[s][:], ACT.Relu).then_inc(ff_exp, 1)

                split(l_unit(l, L_MLP + 1))
                relu(0, l_unit(l, L_MLP))
                ff_split(mlp_h[0], 0, done + 1)
                with act.Fori(0, LOOPS) as i:
                    for q in range(3):
                        s = (1 + q) % 3
                        split(l_unit(l, L_MLP + 2 + 2 * q, i))
                        split(l_unit(l, L_MLP + 3 + 2 * q, i))
                        relu(s, l_unit(l, L_MLP + 1 + 2 * q, i))
                        ff_split(mlp_h[s], s, done + 3 * i + q + 2)

            squares(2 + 2 * LAYERS)

        @block.vector
        def _(dve):
            chain = Chain(dve, dve_chain)
            link = chain.link

            def split(u, size=UNIT):
                dve.wait_ge(w_hi, u.upto())
                dve.tensor_tensor(wlo[:, u.buf, 0:size], raw[:, u.slot, 0:size], whi[:, u.buf, 0:size].bitcast(F32),
                                  ALU.subtract).then_inc(w_lo, 1)

            def normalise(k):
                for t in range(NT):
                    dve.wait_ge(sd_done, NT * k + t + 1)
                    link(dve.reciprocal(rn[:, t:t + 1], sd[:, t:t + 1]))
                    dve.tensor_scalar(xnt[:, t, :], x[:, t, :], rn[:, t:t + 1], None, ALU.mult).then_inc(xn_ok, 1)

            def u_split(k, gain, at):
                for b in range(4):
                    dve.wait_ge(u_hi, KD * k + 2 * b + 2)
                    for c in range(2):
                        f = 2 * b + c
                        dve.scalar_tensor_tensor(ulo[:, f, :], acc[b][:, c * T:c * T + T], gain[:, at + f:at + f + 1],
                                                 uhi[:, f, :].bitcast(F32), ALU.mult, ALU.subtract).then_inc(u_lo, 1)

            def residual(unit):
                dve.wait_ge(used, unit.upto())
                for t in range(NT):
                    for h in range(2):
                        cs = slice(h * 512, h * 512 + 512)
                        add = dve.tensor_tensor(x[:, t, cs], acc[2 * t + h][:], x[:, t, cs], ALU.add)
                        if h == 0:
                            link(add)
                    add.then_inc(x_new, 1)

            def softmax_max(a, h):
                dve.wait_ge(s_ps, HEADS * a + h + 1)
                if h >= 2:
                    dve.wait_ge(s_exp, NT * (HEADS * a + h - 1))
                dve.memset(apart[:], 0.0)
                for t in range(NT):
                    add = bias[:, t, h, :] if isinstance(a, int) else wk[:, t, :]
                    ins = dve.tensor_tensor_reduce(score[h % 2][:, t, :], S_BANK[h % 2][:, t * T:t * T + T], add, SCALE,
                                                   OUTSIDE * 1e6, ALU.add, ALU.max, mx[:, h % 2, t:t + 1])
                    if t == NT - 1:
                        link(ins)
                dve.tensor_scalar(nmx[:, h % 2, :], mx[:, h % 2, :], -1.0, None, ALU.mult).then_inc(s_max, 1)

            def softmax_norm(a, h):
                dve.wait_ge(s_exp, NT * (HEADS * a + h + 1))
                link(dve.reciprocal(rden[:, h % 2, :], den[:, h % 2, :]))
                for t in range(NT):
                    ins = dve.tensor_scalar(expo[h % 2][:, t, :], expo[h % 2][:, t, :], rden[:, h % 2, t:t + 1], None,
                                            ALU.mult)
                    if t == 0:
                        link(ins)
                ins.then_inc(p_ok, 1)

            def o_split(a, p):
                dve.wait_ge(o_hi, HEADS // 2 * a + p + 1)
                dve.tensor_tensor(mlo[:, KA + p, :], O_BANK[:, 0:T], mhi[:, KA + p, :].bitcast(F32), ALU.subtract)\
                    .then_inc(o_lo, 1)

            def conv_taps():
                for c in range(KA):
                    if c == POOL_CHUNK:
                        continue
                    for w in range(TAPS):
                        tap = kcol[:, w * KA + c:w * KA + c + 1]
                        if w == 0:
                            ins = dve.tensor_scalar(y[:, c, :], cu[:, c, 0:T], tap, gcol[:, G_DWB + c:G_DWB + c + 1],
                                                    ALU.mult, ALU.add)
                        else:
                            ins = dve.scalar_tensor_tensor(y[:, c, :], cu[:, c, w:w + T], tap, y[:, c, :],
                                                           ALU.mult, ALU.add)
                        link(ins)
                        yield c
            taps = conv_taps()

            def convolve(n):
                for _ in range(n):
                    next(taps, None)

            dve.memset(zeros[:], 0.0).then_inc(consts, 1)
            dve.memset(eps[:], EPS).then_inc(consts, 1)
            dve.memset(ones[:], 1.0 / DA).then_inc(consts, 1)
            link(dve.memset(cu[:], 0.0))
            normalise(0)
            split(a_unit(0))
            u_split(0, gcol, G_N1)
            split(a_unit(1))
            dve.wait_ge(par_sb, 2)
            for j in range(A_OUT):
                split(a_unit(j + 2))
                if j in (2, 4):
                    i = j // 2 - 1
                    dve.wait_ge(evac, j)
                    link(dve.tensor_scalar(vtok[:, 0, :], vtok[:, 0, :], 1.0, None, ALU.add))
                    link(dve.reciprocal(vtok[:, 0, :], vtok[:, 0, :]))
                    dve.tensor_tensor(cu[:, 2 * i:2 * i + 2, PAD:PAD + T], vtok[:, 0, :].rearrange("p (c t) -> p c t", c=2),
                                      vtok[:, 1, :].rearrange("p (c t) -> p c t", c=2), ALU.mult).then_inc(glu, 1)
                    dve.wait_ge(glu, i + 1)
                if j in (3, 5, 7, 9):
                    convolve(8)
                if j in (6, 8):
                    n = (j - 6) // 2
                    tok = (qtok, ktok)[n][:].rearrange("p t (h d) -> p (t h) d", d=DH)
                    dve.wait_ge(qsq, n + 1)
                    dve.tensor_reduce(ss[:], xn[:, 0:2, :].rearrange("p t (h d) -> p (t h) d", d=DH), AX_X, ALU.add)\
                        .then_inc(qss, 1)
                    dve.wait_ge(qsd, n + 1)
                    link(dve.reciprocal(rn[:], sd[:]))
                    dve.tensor_tensor(tok, tok, rn[:].unsqueeze(2).broadcast_to([P, NT * HEADS, DH]), ALU.mult)\
                        .then_inc(qk_tok, 1)
            dve.wait_ge(bias_ok, 8)
            softmax_max(0, 0)
            for h in range(HEADS):
                if h + 1 < HEADS:
                    softmax_max(0, h + 1)
                softmax_norm(0, h)
                convolve(8)
                if h % 2 == 0 and h >= 2:
                    o_split(0, h // 2 - 1)
            convolve(3 * TAPS)
            dve.memset(m8[:], 0.0).then_inc(conv_dve, 1)
            o_split(0, 3)
            dve.wait_ge(ln_mu, 1)
            dve.tensor_tensor(y[:], y[:], MU[:, 0:T].unsqueeze(1).broadcast_to([P, KA, T]), ALU.subtract).then_inc(ln_xc, 1)
            dve.wait_ge(ln_sd, 1)
            link(dve.reciprocal(xn[:, 1, 0:T], xn[:, 0, 0:T]))
            dve.tensor_tensor(y[:], y[:], xn[:, 1, 0:T].unsqueeze(1).broadcast_to([P, KA, T]), ALU.mult).then_inc(ln_y, 1)
            dve.wait_ge(ln_e, 1)
            link(dve.tensor_scalar(lne, lne, 1.0, None, ALU.add))
            link(dve.reciprocal(lne, lne))
            dve.tensor_tensor(y[:], y[:], lne, ALU.mult).then_inc(c_ok, 1)
            dve.wait_ge(c_hi, 1)
            dve.tensor_tensor(mlo[:, 0:KA, :], y[:], mhi[:, 0:KA, :].bitcast(F32), ALU.subtract).then_inc(c_lo, 1)
            for j in range(A_OUT, A_FF):
                split(a_unit(j + 2))
            residual(a_unit(A_FF - 1))
            normalise(1)
            u_split(1, gcol, G_N2)

            def swiglu(b, q, up, count):
                e, h = ff_e[q], ff_h[q]
                dve.wait_ge(ff_exp, count)
                link(dve.tensor_scalar(e, e, 1.0, None, ALU.add))
                link(dve.reciprocal(e, e))
                link(dve.tensor_tensor(e, col[2 * q][:], e, ALU.mult))
                dve.wait_ge(used, up.upto())
                dve.tensor_tensor(h, col[2 * q + 1][:], e, ALU.mult).then_inc(ff_ok, 1)

            def ff_split(h, s, count):
                dve.wait_ge(ff_hi, count)
                dve.tensor_tensor(mid(mlo, s), h.rearrange("p (c t) -> p c t", c=2), mid(mhi, s).bitcast(F32),
                                  ALU.subtract).then_inc(ff_lo, 1)

            split(a_unit(A_FF + 2))
            swiglu(0, 0, a_unit(A_FF + 1), 1)
            ff_split(ff_h[0], 0, 1)
            with chain.loop(LOOPS, 6) as i:
                for q in range(2):
                    j = A_FF + 2 + 3 * q
                    b = (1 + q) % 2
                    split(a_unit(j + 1, i))
                    split(a_unit(j + 2, i))
                    swiglu(None, b, a_unit(j + 1, i), 2 * i + q + 2)
                    split(a_unit(j + 3, i))
                    ff_split(ff_h[b], b, 2 * i + q + 2)
            residual(a_unit(A_UNITS - 1))

            def select(t, rounds):
                v = wk[:, t, 0:P * (t + 1)]
                for _ in range(rounds):
                    chain.link_apart(dve.max(m8[:], v), apart[:])
                    chain.link_apart(dve.match_replace(v, m8[:], v, TAKEN), apart[:])

            dve.wait_ge(rope_in, 16)

            def gates(l, i):
                v = big[:, 2 * i:2 * i + 2, :]
                dve.wait_ge(evac, A_OUT + L_CONV * l + 15 + i)
                link(dve.tensor_scalar(v, v, 1.0, None, ALU.add))
                link(dve.reciprocal(v, v))

            with chain.loop(LAYERS, LAYER_LINKS) as l:
                n0 = A_OUT + L_CONV * l
                dve.tensor_copy(lg[:], gcol[:, bass.ds(l * LG_N + G_LAYER, LG_N)]).then_inc(lg_ok, 1)
                normalise(2 + 2 * l)
                split(l_unit(l, 0))
                u_split(2 + 2 * l, lg, LG_MIX)
                split(l_unit(l, 1), KD * IKW)
                for j in range(L_CONV):
                    split(l_unit(l, j + 2), unit_size(True, j + 2))
                    if j == 1:
                        dve.wait_ge(evac, n0 + 1)
                        rotate(dve, link, iqtok.rearrange("p t (h d) -> p t h d", d=64), IDX_HEADS, itmp).then_inc(idx_tok, 1)
                        dve.wait_ge(idx_tok, 2 * l + 1)
                    if j == 2:
                        dve.wait_ge(evac, n0 + 2)
                        link(rotate(dve, link, iktok[:, :, 0:64].rearrange("p t (h d) -> p t h d", d=64), 1, itmp))
                        dve.tensor_copy(iktok[:, :, 64:128], iktok[:, :, 0:64]).then_inc(idx_tok, 1)
                    if j == 5:
                        for h in range(IDX_HEADS):
                            dve.wait_ge(lgt_sb, IDX_HEADS * l + h + 1)
                            for t in range(NT):
                                n = P * (t + 1)
                                out, lgt, wt = wk[:, t, 0:n], big[:, 2 * h + t, 0:n], iw[:, t, h:h + 1]
                                if h == 0:
                                    link(dve.tensor_scalar(out, lgt, wt, None, ALU.mult))
                                else:
                                    link(dve.scalar_tensor_tensor(out, lgt, wt, out, ALU.mult, ALU.add))
                        dve.memset(wk[0:CHUNK, 0, CHUNK:P], NOT_ADMISSIBLE)
                        dve.memset(wk[:, 0, P:T], NOT_ADMISSIBLE)
                        link(dve.memset(wk[0:CHUNK, 1, P + CHUNK:T], NOT_ADMISSIBLE))
                    if 6 <= j < 10:
                        select(0, 2)
                        select(1, 1)
                    if 10 <= j < 12:
                        select(1, 2)
                    if j == 12:
                        dve.tensor_scalar(wk[:], wk[:], -2e38, OUTSIDE, ALU.is_ge, ALU.mult).then_inc(mask_ok, 1)
                        dve.wait_ge(mask_ok, l + 1)
                    if j >= 14:
                        softmax_max(1 + l, j - 14)
                        softmax_norm(1 + l, j - 14)
                        if j % 2 == 1 and j >= 17:
                            o_split(1 + l, (j - 17) // 2)
                    if j >= 15:
                        gates(l, j - 15)
                    if j == 17:
                        dve.wait_ge(c_hi, 2 + l)
                        dve.tensor_tensor(mlo[:, 0:KA, :], y[:], mhi[:, 0:KA, :].bitcast(F32), ALU.subtract).then_inc(c_lo, 1)
                gates(l, 7)
                for j in range(L_CONV, L_MLP):
                    if j < L_MLP - 1:
                        split(l_unit(l, j + 2), unit_size(True, j + 2))
                    if j == L_CONV:
                        o_split(1 + l, 3)
                    if L_ATTN < j <= L_MIX:
                        i = j - L_ATTN - 1
                        f = slice(2 * i, 2 * i + 2)
                        dve.wait_ge(g_hi, 4 * l + i + 1)
                        dve.tensor_tensor(ulo[:, f, :], big[:, f, :], uhi[:, f, :].bitcast(F32), ALU.subtract)\
                            .then_inc(g_lo, 1)
                    if j < L_ATTN:
                        i = j - L_CONV
                        g = big[:, KD + 2 * i:KD + 2 * i + 2, :]
                        dve.wait_ge(used, l_unit(l, j).upto())
                        dve.tensor_tensor(g, col[i][:].rearrange("p (c t) -> p c t", c=2), g, ALU.mult).then_inc(merge_rd, 1)
                    elif j < L_MIX:
                        i = j - L_ATTN
                        m = big[:, 2 * i:2 * i + 2, :]
                        dve.wait_ge(used, l_unit(l, j).upto())
                        link(dve.tensor_tensor(m, col[i][:].rearrange("p (c t) -> p c t", c=2), m, ALU.mult))
                        dve.tensor_tensor(m, m, big[:, KD + 2 * i:KD + 2 * i + 2, :], ALU.add).then_inc(merge_rd, 1)
                residual(l_unit(l, L_MLP - 1))
                normalise(3 + 2 * l)
                u_split(3 + 2 * l, lg, LG_MLP)

                def square(s, count):
                    dve.wait_ge(ff_exp, count)
                    dve.tensor_tensor(mlp_h[s], mlp_h[s], mlp_h[s], ALU.mult).then_inc(ff_ok, 1)

                done = FF_BLOCKS + MLP_BLOCKS * l
                split(l_unit(l, L_MLP + 1))
                square(0, done + 1)
                ff_split(mlp_h[0], 0, done + 1)
                with chain.loop(LOOPS, 0) as i:
                    for q in range(3):
                        s = (1 + q) % 3
                        split(l_unit(l, L_MLP + 2 + 2 * q, i))
                        split(l_unit(l, L_MLP + 3 + 2 * q, i))
                        square(s, done + 3 * i + q + 2)
                        ff_split(mlp_h[s], s, done + 3 * i + q + 2)
                residual(l_unit(l, L_UNITS - 1))

            last = 2 + 2 * LAYERS
            normalise(last)
            dve.wait_ge(gfin_in, 16)
            for t in range(NT):
                dve.wait_ge(xn_ok, NT * last + t + 1)
                dve.tensor_tensor(xnt[:, t, :], xnt[:, t, :], gfin, ALU.mult).then_inc(fin, 1)

        @block.gpsimd
        def _(pool):
            chain = Chain(pool, pool_chain)
            link = chain.link
            tmp = [rtmp[:, 0:2, :].rearrange("p a b -> p (a b)"), rtmp[:, 2:4, :].rearrange("p a b -> p (a b)")]
            link(pool.memset(ident[:], 0.0))
            pool.affine_select(out=ident[:], in_=ident[:], compare_op=ALU.not_equal, fill=1.0, base=0,
                               pattern=[[-1, P]], channel_multiplier=1).then_inc(consts, 1)

            rh, rw = d["rpb"].shape[2:]
            skew = bass.AP(tensor=d["rpb"].tensor, offset=(NA_ROWS - GRID_ROWS) * rw + NA_COLS - 1,
                           ap=[[rh * rw, HEADS], [-1, GRID_W], [1, d["skew"].shape[2]]])
            pool.dma_start(d["skew"], skew).then_inc(skew_in, 16)
            pool.wait_ge(skew_in, 16)
            for qr in range(GRID_ROWS):
                p0 = qr % 2 * GRID_W
                for h in range(HEADS):
                    at = (GRID_ROWS - 1 - qr) * rw
                    n = d["skew"].shape[2]
                    src = bass.AP(tensor=d["skew"].tensor, offset=h * GRID_W * n + at,
                                  ap=[[n, GRID_W], [rw, GRID_ROWS], [1, GRID_W]])
                    dst = bias[p0:p0 + GRID_W, qr // 2, h, :].rearrange("p (r c) -> p r c", c=GRID_W)
                    pool.dma_start(dst, src).then_inc(bias_in, 16)
            pool.wait_ge(bias_in, 16 * GRID_ROWS * HEADS)
            link(pool.tensor_scalar(big[:], big[:], 1.0 / SCALE, None, ALU.mult))
            rows_k, half = T // GRID_W, NA_COLS // 2
            for t in range(NT):
                for p0 in (0, GRID_W):
                    v = bias[p0:p0 + GRID_W, t, :, :].rearrange("p h (r c) -> p h r c", c=GRID_W)
                    left, right = v[:, :, :, 0:GRID_W - NA_COLS], v[:, :, :, NA_COLS:GRID_W]
                    n = GRID_W - NA_COLS
                    pool.wait_ge(pool_chain, chain.n)
                    pool.affine_select(out=left, in_=left, compare_op=ALU.is_ge, fill=OUTSIDE, base=half,
                                       pattern=[[0, HEADS], [0, rows_k], [1, n]], channel_multiplier=-1).then_inc(bias_ok, 1)
                    pool.wait_ge(bias_ok, 4 * t + p0 // GRID_W * 2 + 1)
                    pool.affine_select(out=right, in_=right, compare_op=ALU.is_ge, fill=OUTSIDE, base=half - 1 - NA_COLS,
                                       pattern=[[0, HEADS], [0, rows_k], [-1, n]], channel_multiplier=1).then_inc(bias_ok, 1)
                    pool.wait_ge(bias_ok, 4 * t + p0 // GRID_W * 2 + 2)

            c = POOL_CHUNK
            pool.wait_ge(par_sb, 2)
            pool.wait_ge(glu, c // 2 + 1)
            link(pool.tensor_scalar(y[:, c, :], cu[:, c, 0:T], kcol[:, c:c + 1], gcol[:, G_DWB + c:G_DWB + c + 1],
                                    ALU.mult, ALU.add))
            for w in range(1, TAPS):
                link(pool.tensor_scalar(tmp[w % 2], cu[:, c, w:w + T], kcol[:, w * KA + c:w * KA + c + 1], None, ALU.mult))
                add = pool.tensor_tensor(y[:, c, :], y[:, c, :], tmp[w % 2], ALU.add)
                if w < TAPS - 1:
                    link(add)
            add.then_inc(conv_pool, 1)

            pool.wait_ge(rope_in, 16)
            with chain.loop(LAYERS, POOL_LINKS) as l:
                n0 = A_OUT + L_CONV * l
                for n, tok in enumerate((qtok, ktok)):
                    pool.wait_ge(evac, n0 + 4 + 2 * n)
                    rotate(pool, link, tok[:].rearrange("p t (h d) -> p t h d", d=DH), HEADS, rtmp).then_inc(rope_tok, 1)
                    pool.wait_ge(rope_tok, 2 * l + n + 1)
                pool.wait_ge(lg_ok, l + 1)
                pool.wait_ge(evac, n0 + 12)
                link(pool.tensor_tensor(cu[:, :, CONV_K - 1:CONV_K - 1 + T], cC, cH, ALU.mult))
                for w in range(CONV_K):
                    for c in range(KA):
                        tap = lg[:, LG_CONV + w * KA + c:LG_CONV + w * KA + c + 1]
                        out = y[:, c, :] if w == 0 else tmp[c % 2]
                        link(pool.tensor_tensor(out, cu[:, c, w:w + T], tap.broadcast_to([P, T]), ALU.mult))
                        if w:
                            link(pool.tensor_tensor(y[:, c, :], y[:, c, :], out, ALU.add))
                pool.wait_ge(evac, n0 + 14)
                pool.tensor_tensor(y[:], y[:], cB[:], ALU.mult).then_inc(c_ok, 1)


_INS = ["x", "norm1_g", "w_in", "q_norm_g", "k_norm_g", "rpb", "dw_kernel", "dw_bias", "conv_ln_g", "conv_ln_b",
        "w_out", "norm2_g", "w_gate", "w_up", "w_down", "norm_mix_2", "w_in_2", "conv_w_2", "w_attn_out_2",
        "w_conv_out_2", "w_mix_out_2", "norm_mlp_2", "w_mlp_up_2", "w_mlp_down_2", "norm_final_2"]


def rope_table():
    inv = 1.0 / (np.float32(500000.0) ** (np.arange(0, 16, 2, dtype=np.float32) / np.float32(16)))
    ang = np.arange(T, dtype=np.float32)[:, None] * inv[None, :].astype(np.float32)
    return np.concatenate([np.cos(ang), np.sin(ang)], axis=1).astype(np.float32)


def kernel(**inputs):
    import concourse.bacc as bacc
    from concourse.bass_utils import run_bass_kernel_spmd as run

    nc = bacc.Bacc("TRN2", target_bir_lowering=False, num_devices=1)
    arrays, d = {}, {}
    for name in _INS:
        a = np.ascontiguousarray(inputs[name])
        arrays[f"in_{name}"] = a
        d[name] = nc.dram_tensor(f"in_{name}", a.shape, F32, kind="ExternalInput").ap()
    arrays["in_rope"] = rope_table()
    d["rope"] = nc.dram_tensor("in_rope", arrays["in_rope"].shape, F32, kind="ExternalInput").ap()
    d["out"] = nc.dram_tensor("out", (1, T, D), F32, kind="ExternalOutput").ap()
    d["skew"] = nc.dram_tensor("skew", (HEADS, GRID_W, (2 * GRID_ROWS - 2) * (2 * NA_COLS - 1) + GRID_W), F32).ap()
    build(nc, d)
    return run(nc, [arrays], core_ids=[0]).results[0]["out"]
```

```python
from contextlib import ExitStack, contextmanager

import numpy as np
import concourse.bass as bass
from concourse import mybir

F32 = mybir.dt.float32
F32R = mybir.dt.float32r
ALU = mybir.AluOpType
ACT = mybir.ActivationFunctionType
AX_X = mybir.AxisListType.X

P = 128
D = 1024
T = 256
NT = T // P
KD = D // P
HEADS, DH = 8, 64
DA = HEADS * DH
KA = DA // P
GRID_W, NA_ROWS, NA_COLS = 64, 8, 16
GRID_ROWS = T // GRID_W
TAPS = 31
PAD = TAPS // 2
D_FF = 2816
D_MLP = 4096
LAYERS = 2
IDX_HEADS = 4
CHUNK, TOPK = 64, 64
CONV_K = 3
ROPE_HALF = 8
EPS = 1e-6
SCALE = DH ** -0.5
IDX_SCALE = (64 ** -0.5) * (IDX_HEADS ** -0.5)
OUTSIDE = -1e30
NOT_ADMISSIBLE = -1e38
TAKEN = -3e38

COLS = 256
UNIT = 2048
RING, SPLIT = 6, 3
FF_BLOCKS, MLP_BLOCKS = D_FF // COLS, D_MLP // COLS
A_OUT, A_FF = 10, 14
A_UNITS = A_FF + 3 * FF_BLOCKS
L_CONV, L_ATTN, L_MIX, L_MLP = 22, 26, 30, 34
L_UNITS = L_MLP + 2 * MLP_BLOCKS
LOOPS = 5
IQ0, IK0, CB0, CC0, CH0, G0 = 1536, 1792, 1860, 2372, 2884, 3396
IKW = 68
L_COLS = [IQ0, IK0, 0, 256, 512, 768, 1024, 1280, CC0, CC0 + 256, CH0, CH0 + 256, CB0, CB0 + 256] \
    + [G0 + COLS * i for i in range(8)]
A_COLS = [512, 0, 768, 256, 1024, 1280, 1536, 1792, 2048, 2304]
A_OUT_ROWS = [2, 3, 0, 1]

G_N1, G_N2, G_DWB, G_LNG, G_LNB, G_QG, G_KG, G_LAYER = 0, 8, 16, 20, 24, 28, 29, 30
LG_MIX, LG_MLP, LG_CONV, LG_N = 0, 8, 16, 28
G_N = G_LAYER + LAYERS * LG_N
LAYER_LINKS = 76
POOL_LINKS = 23
POOL_CHUNK = 0


class Unit:
    def __init__(self, st, turns=0):
        self.st, self.turns = st, turns
        self.slot, self.buf = st % RING, st % SPLIT
        self.landed = 16 * (st // RING + 1) + 16 * turns

    def upto(self, back=0):
        return self.st - back + 1 + RING * self.turns


class Chain:
    def __init__(self, eng, sem):
        self.eng, self.sem, self.n, self.run = eng, sem, 0, 0

    def link(self, ins):
        self.n += 1
        ins.then_inc(self.sem, 1)
        self.eng.wait_ge(self.sem, self.n + self.run)

    def link_apart(self, ins, scratch):
        self.link(ins)
        self.eng.memset(scratch, 0.0)

    @contextmanager
    def loop(self, turns, per):
        with self.eng.Fori(0, turns) as i:
            n, run = self.n, self.run
            self.run = run + per * i
            yield i
            assert self.n - n == per, (self.n - n, per)
            self.n, self.run = n + per * turns, run


def build(nc, d):
    w_in = d["w_in"][0].rearrange("(k p) n -> p k n", p=P)
    w_out = d["w_out"][0].rearrange("(k p) n -> p k n", p=P)
    w_gate = d["w_gate"][0].rearrange("(k p) n -> p k n", p=P)
    w_up = d["w_up"][0].rearrange("(k p) n -> p k n", p=P)
    w_down = d["w_down"][0].rearrange("(k p) n -> p k n", p=P)

    def per_layer(name):
        return d[name].rearrange("l (k p) n -> p l k n", p=P)

    w_in2, w_attn2, w_conv2 = per_layer("w_in_2"), per_layer("w_attn_out_2"), per_layer("w_conv_out_2")
    w_mix2, w_mup2, w_mdown2 = per_layer("w_mix_out_2"), per_layer("w_mlp_up_2"), per_layer("w_mlp_down_2")

    with ExitStack() as ctx:
        def sb(name, shape, dt=F32):
            return ctx.enter_context(nc.sbuf_tensor(name, shape, dt))

        def sem(name):
            return ctx.enter_context(nc.semaphore(name))

        raw = sb("raw", [P, RING, UNIT])
        whi = sb("whi", [P, SPLIT, UNIT], F32R)
        wlo = sb("wlo", [P, SPLIT, UNIT], F32R)
        x = sb("x", [P, NT, D])
        xn = sb("xn", [P, 4, 512])
        uhi = sb("uhi", [P, KD, T], F32R)
        ulo = sb("ulo", [P, KD, T], F32R)
        mhi = sb("mhi", [P, KD, T], F32R)
        mlo = sb("mlo", [P, KD, T], F32R)
        big = sb("big", [P, 16, T])
        qtok = sb("qtok", [P, NT, DA])
        ktok = sb("ktok", [P, NT, DA])
        vtok = sb("vtok", [P, NT, DA])
        qT = sb("qT", [P, KA, T])
        kT = sb("kT", [P, KA, T])
        prob = sb("prob", [P, 2, NT * T])
        wk = sb("wk", [P, NT, T])
        cu = sb("cu", [P, KA, T + 2 * PAD])
        y = sb("y", [P, KA, T])
        cB = sb("cB", [P, KA, T])
        ident = sb("ident", [P, P])
        ones = sb("ones", [P, P])
        grow = sb("grow", [P, P])
        krow = sb("krow", [P, P])
        gcol = sb("gcol", [P, G_N])
        kcol = sb("kcol", [P, TAPS * KA])
        lg = sb("lg", [P, LG_N])
        rope = sb("rope", [P, NT, 2 * ROPE_HALF])
        iw = sb("iw", [P, NT, IDX_HEADS])
        ss = sb("ss", [P, 16])
        sd = sb("sd", [P, 16])
        rn = sb("rn", [P, 16])
        mx = sb("mx", [P, 2, NT])
        nmx = sb("nmx", [P, 2, NT])
        den = sb("den", [P, 2, NT])
        rden = sb("rden", [P, 2, NT])
        m8 = sb("m8", [P, 8])
        apart = sb("apart", [P, 1])
        eps = sb("eps", [P, 1])
        qg = sb("qg", [P, 1])
        zeros = sb("zeros", [P, 512], mybir.dt.bfloat16)
        rtmp = sb("rtmp", [P, 4, NT * HEADS * ROPE_HALF])
        itmp = sb("itmp", [P, 4, NT * IDX_HEADS * ROPE_HALF])
        xnt = xn[:].rearrange("p (t a) b -> p t (a b)", t=NT)
        score = [xn[:, 0, :].rearrange("p (t k) -> p t k", t=NT), xn[:, 1, :].rearrange("p (t k) -> p t k", t=NT)]
        expo = [xn[:, 2, :].rearrange("p (t k) -> p t k", t=NT), xn[:, 3, :].rearrange("p (t k) -> p t k", t=NT)]
        iqtok = y[:, 0:2, :]
        iktok = y[:, 2, :].rearrange("p (t c) -> p t c", t=NT)
        iqT = prob[:, 0, :].rearrange("p (c t) -> p c t", c=2)
        ikT = prob[:, 1, 0:T]
        cC = qtok[:].rearrange("p a (b t) -> p (a b) t", t=T)
        cH = ktok[:].rearrange("p a (b t) -> p (a b) t", t=T)
        lnsq, lne = cC, cH
        gfin = qT[:].rearrange("p a b -> p (a b)")
        ff_e = [xn[:, 0, :], xn[:, 1, :]]
        ff_h = [xn[:, 2, :], xn[:, 3, :]]
        mlp_h = [xn[:, 0, :], xn[:, 1, :], xn[:, 2, :]]
        bias = big[:].rearrange("p (t h) k -> p t h k", t=NT)

        acc = [ctx.enter_context(nc.psum_tensor(f"acc{i}", [P, 512], F32)) for i in range(4)]
        col = [ctx.enter_context(nc.psum_tensor(f"col{i}", [P, 512], F32)) for i in range(4)]
        S_BANK, T_BANK, O_BANK = (acc[0], acc[1]), acc[2], acc[3]
        MU, VAR = col[0], col[1]

        landed = [sem(f"landed{i}") for i in range(RING)]
        w_hi = sem("w_hi")
        w_lo = sem("w_lo")
        used = sem("used")
        x_in = [sem(f"x_in{t}") for t in range(NT)]
        par_in = sem("par_in")
        rope_in = sem("rope_in")
        skew_in = sem("skew_in")
        bias_in = sem("bias_in")
        gfin_in = sem("gfin_in")
        out_done = sem("out_done")
        consts = sem("consts")
        par_ps = sem("par_ps")
        par_sb = sem("par_sb")
        bias_ok = sem("bias_ok")
        acc_ok = sem("acc_ok")
        x_new = sem("x_new")
        sq_done = sem("sq_done")
        sd_done = sem("sd_done")
        xn_ok = sem("xn_ok")
        u_ps = sem("u_ps")
        u_hi = sem("u_hi")
        u_lo = sem("u_lo")
        evac = sem("evac")
        glu = sem("glu")
        qsq = sem("qsq")
        qss = sem("qss")
        qsd = sem("qsd")
        qk_tok = sem("qk_tok")
        rope_tok = sem("rope_tok")
        qk_ps = sem("qk_ps")
        qk_T = sem("qk_T")
        s_ps = sem("s_ps")
        s_max = sem("s_max")
        s_exp = sem("s_exp")
        p_ok = sem("p_ok")
        p_ps = sem("p_ps")
        p_T = sem("p_T")
        o_ps = sem("o_ps")
        o_hi = sem("o_hi")
        o_lo = sem("o_lo")
        conv_dve = sem("conv_dve")
        conv_pool = sem("conv_pool")
        ln_mu = sem("ln_mu")
        ln_xc = sem("ln_xc")
        ln_sq = sem("ln_sq")
        ln_var = sem("ln_var")
        ln_sd = sem("ln_sd")
        ln_y = sem("ln_y")
        ln_e = sem("ln_e")
        c_ok = sem("c_ok")
        c_hi = sem("c_hi")
        c_lo = sem("c_lo")
        idx_tok = sem("idx_tok")
        idx_ps = sem("idx_ps")
        idx_T = sem("idx_T")
        lgt_ps = sem("lgt_ps")
        lgt_sb = sem("lgt_sb")
        lg_ok = sem("lg_ok")
        mask_ok = sem("mask_ok")
        gate_ok = sem("gate_ok")
        merge_rd = sem("merge_rd")
        g_hi = sem("g_hi")
        g_lo = sem("g_lo")
        ff_act = sem("ff_act")
        ff_ok = sem("ff_ok")
        ff_hi = sem("ff_hi")
        ff_lo = sem("ff_lo")
        fin = sem("fin")
        dve_chain = sem("dve_chain")
        act_chain = sem("act_chain")
        pool_chain = sem("pool_chain")

        def whi_v(u, n=COLS):
            return whi[:, u.buf, :].rearrange("p (k n) -> p k n", n=n)

        def wlo_v(u, n=COLS):
            return wlo[:, u.buf, :].rearrange("p (k n) -> p k n", n=n)

        def ikw_v(buf):
            return buf[:, 0:KD * IKW].rearrange("p (k n) -> p k n", n=IKW)

        def unit_size(layer, j):
            if layer and j == 1:
                return KD * IKW
            return KA * COLS if layer and L_CONV <= j < L_MIX else UNIT

        def a_unit(j, turns=0):
            return Unit(j, turns)

        def l_unit(l, j, turns=0):
            return Unit(A_UNITS + j, L_UNITS // RING * l + turns)

        def rotate(eng, link, v, nh, tmp):
            x1, x2 = v[:, :, :, 0:ROPE_HALF], v[:, :, :, ROPE_HALF:2 * ROPE_HALF]
            cos = rope[:, :, 0:ROPE_HALF].unsqueeze(2).broadcast_to([P, NT, nh, ROPE_HALF])
            sin = rope[:, :, ROPE_HALF:2 * ROPE_HALF].unsqueeze(2).broadcast_to([P, NT, nh, ROPE_HALF])
            x1c, x2s, x2c, x1s = (tmp[:, r, 0:NT * nh * ROPE_HALF].rearrange("p (t h r) -> p t h r", t=NT, h=nh)
                                  for r in range(4))
            eng.tensor_tensor(x1c, x1, cos, ALU.mult)
            eng.tensor_tensor(x2s, x2, sin, ALU.mult)
            eng.tensor_tensor(x2c, x2, cos, ALU.mult)
            link(eng.tensor_tensor(x1s, x1, sin, ALU.mult))
            eng.tensor_tensor(x1, x1c, x2s, ALU.subtract)
            return eng.tensor_tensor(x2, x2c, x1s, ALU.add)

        def mid(buf, s):
            return buf[:, 2 * s:2 * s + 2, :]

        block = ctx.enter_context(nc.Block())

        @block.sync
        def _(sp):
            def load(u, src, size=UNIT, free=...):
                free = u if free is ... else free
                if free is not None and not (isinstance(u.turns, int) and u.st < RING):
                    sp.wait_ge(w_lo, free.upto(RING))
                dst = raw[:, u.slot, 0:size].rearrange("p (k n) -> p k n", n=src.shape[-1])
                sp.dma_start(dst, src).then_inc(landed[u.slot], 16)

            for t in range(NT):
                sp.dma_start(x[:, t, :], d["x"][0, t * P:(t + 1) * P, :]).then_inc(x_in[t], 16)
            load(a_unit(0), w_in[:, :, A_COLS[0]:A_COLS[0] + COLS])
            for j in range(1, A_OUT):
                load(a_unit(j), w_in[:, :, A_COLS[j]:A_COLS[j] + COLS])
                if j == 3:
                    n, (rh, rw) = 2 * GRID_ROWS - 1, d["rpb"].shape[2:]
                    for h in range(HEADS):
                        skew = bass.AP(tensor=d["rpb"].tensor, offset=(h * rh + NA_ROWS - GRID_ROWS) * rw + NA_COLS - 1,
                                       ap=[[rw, n], [-1, GRID_W], [1, GRID_W]])
                        sp.dma_start(d["skew"][h], skew).then_inc(skew_in, 16)
                if j == 5:
                    sp.wait_ge(skew_in, 16 * HEADS)
                    for qr in range(GRID_ROWS):
                        r0, p0 = GRID_ROWS - 1 - qr, qr % 2 * GRID_W
                        for r in range(GRID_ROWS):
                            dst = bias[p0:p0 + GRID_W, qr // 2, :, r * GRID_W:(r + 1) * GRID_W]
                            sp.dma_start(dst, d["skew"][:, r0 + r, :, :].rearrange("h q c -> q h c")).then_inc(bias_in, 16)
                    sp.dma_start(rope[:], d["rope"].rearrange("(t p) n -> p t n", p=P)).then_inc(rope_in, 16)
            for i, r in enumerate(A_OUT_ROWS):
                load(a_unit(A_OUT + i), w_out[:, 2 * r:2 * r + 2, :])
            load(a_unit(A_FF), w_gate[:, :, 0:COLS])
            load(a_unit(A_FF + 1), w_up[:, :, 0:COLS])
            with sp.Fori(0, LOOPS) as i:
                for q in range(2):
                    at = i * (2 * COLS) + (1 + q) * COLS
                    load(a_unit(A_FF + 2 + 3 * q, i), w_gate[:, :, bass.ds(at, COLS)])
                    load(a_unit(A_FF + 3 + 3 * q, i), w_up[:, :, bass.ds(at, COLS)])
                    load(a_unit(A_FF + 4 + 3 * q, i), w_down[:, bass.ds(i * 4 + 2 * q, 2), :])
            load(a_unit(A_UNITS - 1), w_down[:, 2 * FF_BLOCKS - 2:2 * FF_BLOCKS, :])

            with sp.Fori(0, LAYERS) as l:
                def of(w):
                    return w[:, bass.ds(l, 1)].rearrange("p l k n -> p (l k) n")
                for j in range(L_CONV):
                    n = IKW if j == 1 else COLS
                    load(l_unit(l, j), of(w_in2)[:, :, L_COLS[j]:L_COLS[j] + n], KD * n,
                         None if j == 2 else l_unit(l, 2 if j == 1 else j))
                for at, w in ((L_CONV, w_conv2), (L_ATTN, w_attn2)):
                    for i in range(4):
                        load(l_unit(l, at + i), of(w)[:, :, COLS * i:COLS * i + COLS], KA * COLS)
                for i in range(4):
                    load(l_unit(l, L_MIX + i), of(w_mix2)[:, 2 * i:2 * i + 2, :])
                load(l_unit(l, L_MLP), of(w_mup2)[:, :, 0:COLS])
                with sp.Fori(0, LOOPS) as i:
                    for q in range(3):
                        load(l_unit(l, L_MLP + 1 + 2 * q, i), of(w_mup2)[:, :, bass.ds(i * (3 * COLS) + (1 + q) * COLS, COLS)])
                        load(l_unit(l, L_MLP + 2 + 2 * q, i), of(w_mdown2)[:, bass.ds(i * 6 + 2 * q, 2), :])
                load(l_unit(l, L_UNITS - 1), of(w_mdown2)[:, 2 * MLP_BLOCKS - 2:2 * MLP_BLOCKS, :])
            sp.wait_ge(w_lo, A_UNITS + LAYERS * L_UNITS - 2)
            sp.dma_start(gfin, d["norm_final_2"].partition_broadcast(P)).then_inc(gfin_in, 16)
            for t in range(NT):
                sp.wait_ge(fin, t + 1)
                sp.dma_start(d["out"][0, t * P:(t + 1) * P, :], xnt[:, t, :]).then_inc(out_done, 16)
            sp.wait_ge(out_done, 16 * NT)


        @block.tensor
        def _(pe):
            def mm3(out, l_hi, l_lo, r_hi, r_lo, start, stop):
                pe.matmul(out, l_hi, r_hi, start=start, stop=False)
                pe.matmul(out, l_hi, r_lo, start=False, stop=False)
                return pe.matmul(out, l_lo, r_hi, start=False, stop=stop)

            def col_tokens(u, bank, w=COLS, norm=None):
                hi, lo = (ikw_v(whi[:, u.buf, :]), ikw_v(wlo[:, u.buf, :])) if w == IKW else (whi_v(u), wlo_v(u))
                for t in range(NT):
                    for k in range(KD):
                        if norm is not None and k % 4 == 0:
                            pe.wait_ge(u_lo, 4 * norm + 2 * t + k // 4 + 1)
                        tok = slice(t * P, t * P + P)
                        mm = mm3(bank[:, t * w:t * w + w], uhi[:, k, tok], ulo[:, k, tok], hi[:, k, :], lo[:, k, :],
                                 k == 0, k == KD - 1)
                mm.then_inc(used, 1)

            def col_features(u, bank, hi_in, lo_in, kc=KD, norm=None):
                for c in range(COLS // P):
                    for k in range(kc):
                        if norm is not None and c == 0 and k % 4 == 0:
                            pe.wait_ge(u_lo, 4 * norm + 2 + k // 4 + 1)
                        cs = slice(c * P, c * P + P)
                        mm = mm3(bank[:, c * T:c * T + T], whi_v(u)[:, k, cs], wlo_v(u)[:, k, cs],
                                 hi_in[:, k, :], lo_in[:, k, :], k == 0, k == kc - 1)
                mm.then_inc(used, 1)

            def rows(u, hi_in, lo_in, start, stop):
                for t in range(NT):
                    for h in range(2):
                        for c in range(2):
                            tok = slice(t * P, t * P + P)
                            cs = slice(h * 512, h * 512 + 512)
                            mm = mm3(acc[2 * t + h][:], hi_in[:, c, tok], lo_in[:, c, tok],
                                     whi_v(u, D)[:, c, cs], wlo_v(u, D)[:, c, cs], start and c == 0, stop and c == 1)
                    if stop and t == 0:
                        mm.then_inc(acc_ok, 1)
                mm.then_inc(used, 1)

            def norm_transposes(k):
                for t in range(NT):
                    pe.wait_ge(xn_ok, NT * k + t + 1)
                    for f in range(KD):
                        tr = pe.transpose(col[2 * t + f // 4][:, f % 4 * P:f % 4 * P + P], xnt[:, t, f * P:f * P + P], ident[:])
                        if f % 4 == 3:
                            tr.then_inc(u_ps, 1)

            def turn(tok, n):
                for b in range(2):
                    bank = acc[2 * n + b]
                    for c in range(2):
                        for t in range(NT):
                            f = 2 * b + c
                            tr = pe.transpose(bank[:, c * T + t * P:c * T + t * P + P], tok[:, t, f * P:f * P + P], ident[:])
                    tr.then_inc(qk_ps, 1)

            def scores(a, h):
                pe.wait_ge(qk_T, 4 * a + 4)
                if h >= 2:
                    pe.wait_ge(s_max, HEADS * a + h - 1)
                off = DH * (h % 2)
                for t in range(NT):
                    mm = pe.matmul(S_BANK[h % 2][:, t * T:t * T + T], qT[off:off + DH, h // 2, t * P:t * P + P],
                                   kT[off:off + DH, h // 2, :], start=True, stop=True)
                mm.then_inc(s_ps, 1)

            def turn_probs(a, h):
                pe.wait_ge(p_ok, HEADS * a + h + 1)
                if h >= 1:
                    pe.wait_ge(p_T, HEADS * a + h)
                for kt in range(NT):
                    for t in range(NT):
                        tr = pe.transpose(T_BANK[:, kt * T + t * P:kt * T + t * P + P],
                                          expo[h % 2][:, t, kt * P:kt * P + P], ident[:])
                tr.then_inc(p_ps, 1)

            def values(a, h):
                pe.wait_ge(p_T, HEADS * a + h + 1)
                if h % 2 == 0 and h >= 2:
                    pe.wait_ge(o_lo, HEADS // 2 * a + h // 2)
                off = DH * (h % 2)
                for kt in range(NT):
                    mm = pe.matmul(O_BANK[off:off + DH, 0:T], vtok[:, kt, h * DH:h * DH + DH],
                                   prob[:, h % 2, kt * T:kt * T + T], start=kt == 0, stop=kt == NT - 1)
                mm.then_inc(o_ps, 1)

            pe.wait_ge(consts, 4)
            norm_transposes(0)
            pe.wait_ge(par_in, 16 * 2)
            pe.transpose(acc[0][:, 0:G_N], grow[0:G_N, :], ident[0:G_N, 0:G_N])
            pe.transpose(acc[1][:, 0:TAPS * KA], krow[0:TAPS * KA, :], ident[0:TAPS * KA, 0:TAPS * KA]).then_inc(par_ps, 1)

            for j in range(A_OUT):
                u = a_unit(j)
                pe.wait_ge(w_lo, u.upto())
                if j >= 4:
                    pe.wait_ge(evac, j - 3)
                if j < 4:
                    col_features(u, col[j % 4], uhi, ulo, norm=0 if j == 0 else None)
                else:
                    col_tokens(u, col[j % 4])
                if j == 6:
                    pe.wait_ge(qk_tok, 1)
                    turn(qtok, 0)
                if j == 8:
                    pe.wait_ge(qk_tok, 2)
                    turn(ktok, 1)
            pe.wait_ge(evac, A_OUT)
            scores(0, 0)
            for h in range(HEADS):
                if h + 1 < HEADS:
                    scores(0, h + 1)
                turn_probs(0, h)
                if h >= 1:
                    values(0, h - 1)
            values(0, HEADS - 1)
            pe.wait_ge(conv_dve, 1)
            pe.wait_ge(conv_pool, 1)
            for c in range(KA):
                mm = pe.matmul(MU[:, 0:T], ones[:], y[:, c, :], start=c == 0, stop=c == KA - 1)
            mm.then_inc(ln_mu, 1)
            pe.wait_ge(ln_sq, 1)
            for c in range(KA):
                mm = pe.matmul(VAR[:, 0:T], ones[:], lnsq[:, c, :], start=c == 0, stop=c == KA - 1)
            mm.then_inc(ln_var, 1)
            for i, r in enumerate(A_OUT_ROWS):
                u = a_unit(A_OUT + i)
                pe.wait_ge(w_lo, u.upto())
                if i == 0:
                    pe.wait_ge(o_lo, HEADS // 2)
                if i == 2:
                    pe.wait_ge(c_lo, 1)
                rows(u, mhi[:, 2 * r:2 * r + 2, :], mlo[:, 2 * r:2 * r + 2, :], i == 0, i == 3)

            def open_acc():
                for bank in acc:
                    pe.matmul(bank[:], zeros[:, 0:P], zeros[:], start=True, stop=False)

            norm_transposes(1)
            pe.wait_ge(w_lo, a_unit(A_FF).upto())
            col_features(a_unit(A_FF), col[0], uhi, ulo, norm=1)
            pe.wait_ge(w_lo, a_unit(A_FF + 1).upto())
            col_features(a_unit(A_FF + 1), col[1], uhi, ulo)
            open_acc()
            with pe.Fori(0, LOOPS) as i:
                for q in range(2):
                    gate, up, down = (a_unit(A_FF + 2 + 3 * q + r, i) for r in range(3))
                    bank = 2 * ((1 + q) % 2)
                    pe.wait_ge(w_lo, gate.upto())
                    col_features(gate, col[bank], uhi, ulo)
                    pe.wait_ge(w_lo, up.upto())
                    col_features(up, col[bank + 1], uhi, ulo)
                    pe.wait_ge(w_lo, down.upto())
                    pe.wait_ge(ff_lo, 2 * i + q + 1)
                    rows(down, mid(mhi, q), mid(mlo, q), False, False)
            pe.wait_ge(w_lo, a_unit(A_UNITS - 1).upto())
            pe.wait_ge(ff_lo, FF_BLOCKS)
            rows(a_unit(A_UNITS - 1), mid(mhi, 0), mid(mlo, 0), False, True)

            with pe.Fori(0, LAYERS) as l:
                norm_transposes(2 + 2 * l)
                for j in range(L_CONV):
                    u = l_unit(l, j)
                    pe.wait_ge(w_lo, u.upto())
                    if j >= 4:
                        pe.wait_ge(evac, A_OUT + L_CONV * l + j - 3)
                    if j < 8:
                        col_tokens(u, col[j % 4], IKW if j == 1 else COLS, norm=2 + 2 * l if j == 0 else None)
                    else:
                        col_features(u, col[j % 4], uhi, ulo)
                    if j == 3:
                        pe.wait_ge(idx_tok, 2 * l + 2)
                        for c in range(2):
                            for t in range(NT):
                                pe.transpose(acc[0][:, c * T + t * P:c * T + t * P + P],
                                             iqtok[:, t, c * P:c * P + P], ident[:])
                        for t in range(NT):
                            tr = pe.transpose(acc[1][:, t * P:t * P + P], iktok[:, t, :], ident[:])
                        tr.then_inc(idx_ps, 1)
                    if j == 4:
                        pe.wait_ge(idx_T, 2 * l + 2)
                        for h in range(IDX_HEADS):
                            off = 64 * (h % 2)
                            for t in range(NT):
                                mm = pe.matmul(acc[h][:, t * T:t * T + T], iqT[off:off + 64, h // 2, t * P:t * P + P],
                                               ikT[off:off + 64, :], start=True, stop=True)
                        mm.then_inc(lgt_ps, 1)
                    if j == 6:
                        pe.wait_ge(lgt_sb, IDX_HEADS * l + IDX_HEADS)
                        pe.wait_ge(rope_tok, 2 * l + 1)
                        turn(qtok, 0)
                    if j == 7:
                        pe.wait_ge(rope_tok, 2 * l + 2)
                        turn(ktok, 1)
                    if j == 13:
                        scores(1 + l, 0)
                    if j >= 14:
                        h = j - 14
                        if h + 1 < HEADS:
                            scores(1 + l, h + 1)
                        turn_probs(1 + l, h)
                        if h >= 1:
                            values(1 + l, h - 1)
                for i in range(4):
                    u = l_unit(l, L_CONV + i)
                    pe.wait_ge(w_lo, u.upto())
                    pe.wait_ge(evac, A_OUT + L_CONV * l + 19 + i)
                    if i == 0:
                        pe.wait_ge(c_lo, 2 + l)
                    col_features(u, col[i], mhi[:, 0:KA, :], mlo[:, 0:KA, :], KA)
                    if i == 0:
                        values(1 + l, HEADS - 1)
                for i in range(4):
                    u = l_unit(l, L_ATTN + i)
                    pe.wait_ge(w_lo, u.upto())
                    pe.wait_ge(merge_rd, 8 * l + i + 1)
                    if i == 0:
                        pe.wait_ge(o_lo, HEADS // 2 * (2 + l))
                    col_features(u, col[i], mhi[:, KA:KD, :], mlo[:, KA:KD, :], KA)
                for i in range(4):
                    u = l_unit(l, L_MIX + i)
                    pe.wait_ge(w_lo, u.upto())
                    pe.wait_ge(g_lo, 4 * l + i + 1)
                    rows(u, uhi[:, 2 * i:2 * i + 2, :], ulo[:, 2 * i:2 * i + 2, :], i == 0, i == 3)

                norm_transposes(3 + 2 * l)
                u = l_unit(l, L_MLP)
                pe.wait_ge(w_lo, u.upto())
                col_features(u, col[0], uhi, ulo, norm=3 + 2 * l)
                open_acc()
                with pe.Fori(0, LOOPS) as i:
                    for q in range(3):
                        up, down = l_unit(l, L_MLP + 1 + 2 * q, i), l_unit(l, L_MLP + 2 + 2 * q, i)
                        done = FF_BLOCKS + MLP_BLOCKS * l + 3 * i + q
                        pe.wait_ge(w_lo, up.upto())
                        col_features(up, col[(1 + q) % 3], uhi, ulo)
                        pe.wait_ge(w_lo, down.upto())
                        pe.wait_ge(ff_lo, done + 1)
                        rows(down, mid(mhi, q), mid(mlo, q), False, False)
                pe.wait_ge(w_lo, l_unit(l, L_UNITS - 1).upto())
                pe.wait_ge(ff_lo, FF_BLOCKS + MLP_BLOCKS * l + MLP_BLOCKS)
                rows(l_unit(l, L_UNITS - 1), mid(mhi, 0), mid(mlo, 0), False, True)

        @block.scalar
        def _(act):
            chain = Chain(act, act_chain)

            def split(u, size=UNIT):
                act.wait_ge(landed[u.slot], u.landed)
                if not (isinstance(u.turns, int) and u.st < SPLIT):
                    act.wait_ge(used, u.upto(SPLIT))
                act.activation(whi[:, u.buf, 0:size], raw[:, u.slot, 0:size], ACT.Copy).then_inc(w_hi, 1)

            def norm(k, gain, at, pause=None):
                act.activation(sd[:, 2:3], eps[:, 0:1], ACT.Sqrt)

                def mean(t):
                    if isinstance(k, int) and k == 0:
                        act.wait_ge(x_in[t], 16)
                    else:
                        act.wait_ge(x_new, NT * (k - 1) + t + 1)
                    act.activation(xnt[:, t, :], x[:, t, :], ACT.Square, accum_out=ss[:, t:t + 1]).then_inc(sq_done, 1)
                    act.wait_ge(sq_done, NT * k + t + 1)
                    act.activation(sd[:, t:t + 1], ss[:, t:t + 1], ACT.Sqrt, bias=eps[:, 0:1], scale=1.0 / D)\
                        .then_inc(sd_done, 1)

                def hi(t, b):
                    act.wait_ge(u_ps, 4 * k + 2 * t + b + 1)
                    for c in range(4):
                        f = 4 * b + c
                        out = act.activation(uhi[:, f, t * P:t * P + P], col[2 * t + b][:, c * P:c * P + P], ACT.Copy,
                                             scale=gain[:, at + f:at + f + 1])
                    out.then_inc(u_hi, 1)

                mean(0)
                if gain is None:
                    mean(1)
                    return
                if pause:
                    mean(1)
                    pause()
                    hi(0, 0)
                else:
                    hi(0, 0)
                    mean(1)
                hi(0, 1)
                hi(1, 0)
                hi(1, 1)

            def exps(a, h):
                act.wait_ge(s_max, HEADS * a + h + 1)
                if h >= 2:
                    act.wait_ge(p_ps, HEADS * a + h - 1)
                for t in range(NT):
                    act.activation(expo[h % 2][:, t, :], score[h % 2][:, t, :], ACT.Exp, bias=nmx[:, h % 2, t:t + 1],
                                   accum_out=den[:, h % 2, t:t + 1]).then_inc(s_exp, 1)

            def copy_probs(a, h):
                act.wait_ge(p_ps, HEADS * a + h + 1)
                if h >= 2:
                    act.wait_ge(o_ps, HEADS * a + h - 1)
                act.activation(prob[:, h % 2, :], T_BANK[:], ACT.Copy).then_inc(p_T, 1)

            def o_split(a, p):
                act.wait_ge(o_ps, HEADS * a + 2 * p + 2)
                act.activation(mhi[:, KA + p, :], O_BANK[:, 0:T], ACT.Copy).then_inc(o_hi, 1)

            def evacuate(n, j, dst, w=COLS):
                act.wait_ge(used, n.upto())
                act.activation(dst, col[j % 4][:, 0:NT * w].rearrange("p (t c) -> p t c", t=NT), ACT.Copy)\
                    .then_inc(evac, 1)

            def half(tok, i):
                return tok[:, :, COLS * i:COLS * i + COLS]

            def copy_turned(a, n, dst, gain=1.0):
                for b in range(2):
                    act.wait_ge(qk_ps, 4 * a + 2 * n + b + 1)
                    act.activation(dst[:, 2 * b:2 * b + 2, :], acc[2 * n + b][:].rearrange("p (c t) -> p c t", c=2),
                                   ACT.Copy, scale=gain).then_inc(qk_T, 1)

            act.dma_start(grow[0:G_N, :], d["params"][0:G_N, :]).then_inc(par_in, 16)
            act.dma_start(krow[0:TAPS * KA, :], d["params"][G_N:G_N + TAPS * KA, :]).then_inc(par_in, 16)

            def parameters():
                split(a_unit(0))
                act.wait_ge(par_ps, 1)
                act.activation(gcol[:], acc[0][:, 0:G_N], ACT.Copy).then_inc(par_sb, 1)
                act.activation(qg[:], acc[0][:, G_QG:G_QG + 1], ACT.Copy, scale=SCALE).then_inc(par_sb, 1)
                act.activation(kcol[:], acc[1][:, 0:TAPS * KA], ACT.Copy).then_inc(par_sb, 1)
                act.wait_ge(par_sb, 3)

            act.wait_ge(consts, 4)
            norm(0, gcol, G_N1, parameters)
            split(a_unit(1))
            for j in range(A_OUT):
                u = a_unit(j)
                split(a_unit(j + 2))
                if j == 6 or j == 8:
                    n = (j - 6) // 2
                    act.wait_ge(evac, j)
                    act.activation(xn[:, 0:2, :], (qtok, ktok)[n][:], ACT.Square).then_inc(qsq, 1)
                    act.wait_ge(qss, n + 1)
                    act.activation(sd[:], ss[:], ACT.Sqrt, bias=eps[:, 0:1], scale=1.0 / DH).then_inc(qsd, 1)
                if j == 7:
                    copy_turned(0, 0, qT, qg[:])
                if j == 9:
                    copy_turned(0, 1, kT, gcol[:, G_KG:G_KG + 1])
                if j in (0, 2):
                    if j == 2:
                        act.wait_ge(glu, 1)
                    act.wait_ge(used, u.upto())
                    act.activation(vtok[:, 0, :], col[j % 4][:], ACT.Sigmoid).then_inc(evac, 1)
                elif j in (1, 3):
                    act.wait_ge(used, u.upto())
                    act.activation(vtok[:, 1, :], col[j % 4][:], ACT.Copy).then_inc(evac, 1)
                else:
                    if j == 8:
                        act.wait_ge(glu, 2)
                    evacuate(u, j, half((qtok, ktok, vtok)[(j - 4) // 2], j % 2))
            for h in range(HEADS):
                exps(0, h)
                copy_probs(0, h)
                if h % 2 == 0 and h >= 2:
                    o_split(0, h // 2 - 1)
            o_split(0, 3)
            act.wait_ge(ln_xc, 1)
            act.activation(lnsq, y[:], ACT.Square).then_inc(ln_sq, 1)
            act.wait_ge(ln_var, 1)
            act.activation(xn[:, 0, 0:T], VAR[:, 0:T], ACT.Sqrt, bias=eps[:, 0:1]).then_inc(ln_sd, 1)
            act.wait_ge(ln_y, 1)
            for c in range(KA):
                z = act.activation(y[:, c, :], y[:, c, :], ACT.Identity, bias=gcol[:, G_LNB + c:G_LNB + c + 1],
                                   scale=gcol[:, G_LNG + c:G_LNG + c + 1])
            chain.link(z)
            act.activation(lne, y[:], ACT.Sigmoid).then_inc(ln_e, 1)
            act.wait_ge(c_ok, 1)
            act.activation(mhi[:, 0:KA, :], y[:], ACT.Copy).then_inc(c_hi, 1)
            for j in range(A_OUT, A_FF):
                split(a_unit(j + 2))
            norm(1, gcol, G_N2)

            def ff_gate(b, q, n, bank):
                act.wait_ge(used, n.upto())
                act.activation(ff_e[q], col[bank][:], ACT.Sigmoid).then_inc(ff_act, 1)

            def ff_split(h, s, count):
                act.wait_ge(ff_ok, count)
                act.activation(mid(mhi, s), h.rearrange("p (c t) -> p c t", c=2), ACT.Copy).then_inc(ff_hi, 1)

            split(a_unit(A_FF + 2))
            ff_gate(0, 0, a_unit(A_FF), 0)
            ff_split(ff_h[0], 0, 1)
            with act.Fori(0, LOOPS) as i:
                for q in range(2):
                    j = A_FF + 2 + 3 * q
                    b = (1 + q) % 2
                    split(a_unit(j + 1, i))
                    split(a_unit(j + 2, i))
                    ff_gate(None, b, a_unit(j, i), 2 * b)
                    split(a_unit(j + 3, i))
                    ff_split(ff_h[b], b, 2 * i + q + 2)

            with act.Fori(0, LAYERS) as l:
                n0 = A_OUT + L_CONV * l
                split(l_unit(l, 0))
                act.wait_ge(lg_ok, l + 1)
                norm(2 + 2 * l, lg, LG_MIX)
                split(l_unit(l, 1), KD * IKW)
                for j in range(L_CONV):
                    u = l_unit(l, j)
                    if j >= 14:
                        exps(1 + l, j - 14)
                    split(l_unit(l, j + 2), unit_size(True, j + 2))
                    if j == 4:
                        act.wait_ge(idx_ps, l + 1)
                        act.activation(iqT, acc[0][:].rearrange("p (c t) -> p c t", c=2), ACT.Copy).then_inc(idx_T, 1)
                        act.activation(ikT, acc[1][:, 0:T], ACT.Copy).then_inc(idx_T, 1)
                    if j == 5:
                        act.wait_ge(lgt_ps, l + 1)
                        for h in range(IDX_HEADS):
                            act.activation(big[:, 2 * h:2 * h + 2, :], acc[h][:].rearrange("p (t k) -> p t k", t=NT),
                                           ACT.Relu).then_inc(lgt_sb, 1)
                    if j == 7:
                        copy_turned(1 + l, 0, qT, SCALE)
                    if j == 8:
                        copy_turned(1 + l, 1, kT)
                    if j % 2 == 1 and j >= 17:
                        o_split(1 + l, (j - 17) // 2)
                    if j == 0:
                        evacuate(u, j, iqtok)
                    elif j == 1:
                        act.wait_ge(used, u.upto())
                        ikw = col[1][:, 0:NT * IKW].rearrange("p (t c) -> p t c", t=NT)
                        act.activation(iktok[:, :, 0:64], ikw[:, :, 0:64], ACT.Copy)
                        act.activation(iw[:], ikw[:, :, 64:68], ACT.Copy, scale=IDX_SCALE).then_inc(evac, 1)
                    elif j < 8:
                        evacuate(u, j, half((qtok, ktok, vtok)[(j - 2) // 2], j % 2))
                    elif j < 14:
                        i = (j - 8) % 2
                        evacuate(u, j, (cC, cH, cB)[(j - 8) // 2][:, 2 * i:2 * i + 2, :])
                    else:
                        act.wait_ge(used, u.upto())
                        act.activation(big[:, 2 * (j - 14):2 * (j - 14) + 2, :],
                                       col[j % 4][:].rearrange("p (c t) -> p c t", c=2), ACT.Copy)\
                            .then_inc(evac, 1)
                    if j == 16:
                        act.wait_ge(c_ok, 2 + l)
                        act.activation(mhi[:, 0:KA, :], y[:], ACT.Copy).then_inc(c_hi, 1)
                    if j >= 14:
                        copy_probs(1 + l, j - 14)
                for j in range(L_CONV, L_MLP):
                    if j < L_MLP - 1:
                        split(l_unit(l, j + 2), unit_size(True, j + 2))
                    if j == L_CONV:
                        o_split(1 + l, 3)
                        act.wait_ge(evac, A_OUT + L_CONV * l + L_CONV)
                    if j < L_MIX:
                        f = 2 * (j - L_CONV) + (KD if j < L_ATTN else -KD)
                        act.activation(big[:, f:f + 2, :], big[:, f:f + 2, :], ACT.Sigmoid).then_inc(gate_ok, 1)
                    if j > L_ATTN and j <= L_MIX:
                        i = j - L_ATTN - 1
                        act.wait_ge(merge_rd, 8 * l + 4 + i + 1)
                        act.activation(uhi[:, 2 * i:2 * i + 2, :], big[:, 2 * i:2 * i + 2, :], ACT.Copy).then_inc(g_hi, 1)
                norm(3 + 2 * l, lg, LG_MLP)
                done = FF_BLOCKS + MLP_BLOCKS * l

                def relu(s, up):
                    act.wait_ge(used, up.upto())
                    act.activation(mlp_h[s], col[s][:], ACT.Relu).then_inc(ff_act, 1)

                split(l_unit(l, L_MLP + 1))
                relu(0, l_unit(l, L_MLP))
                ff_split(mlp_h[0], 0, done + 1)
                with act.Fori(0, LOOPS) as i:
                    for q in range(3):
                        s = (1 + q) % 3
                        split(l_unit(l, L_MLP + 2 + 2 * q, i))
                        split(l_unit(l, L_MLP + 3 + 2 * q, i))
                        relu(s, l_unit(l, L_MLP + 1 + 2 * q, i))
                        ff_split(mlp_h[s], s, done + 3 * i + q + 2)

            norm(2 + 2 * LAYERS, None, None)

        @block.vector
        def _(dve):
            chain = Chain(dve, dve_chain)
            link = chain.link

            def split(u, size=UNIT):
                dve.wait_ge(w_hi, u.upto())
                dve.tensor_tensor(wlo[:, u.buf, 0:size], raw[:, u.slot, 0:size], whi[:, u.buf, 0:size].bitcast(F32),
                                  ALU.subtract).then_inc(w_lo, 1)

            def norm(k, gain, at, unit=None):
                def residual(t):
                    if unit is None:
                        return
                    if t == 0:
                        dve.wait_ge(acc_ok, k)
                    else:
                        dve.wait_ge(used, unit.upto())
                    for h in range(2):
                        cs = slice(h * 512, h * 512 + 512)
                        add = dve.tensor_tensor(x[:, t, cs], acc[2 * t + h][:], x[:, t, cs], ALU.add)
                    add.then_inc(x_new, 1)

                def scale(t):
                    dve.wait_ge(sd_done, NT * k + t + 1)
                    link(dve.reciprocal(rn[:, t:t + 1], sd[:, t:t + 1]))
                    dve.tensor_scalar(xnt[:, t, :], x[:, t, :], rn[:, t:t + 1], None, ALU.mult).then_inc(xn_ok, 1)

                def lo(t, b):
                    dve.wait_ge(u_hi, 4 * k + 2 * t + b + 1)
                    for c in range(4):
                        f = 4 * b + c
                        tok = slice(t * P, t * P + P)
                        out = dve.scalar_tensor_tensor(ulo[:, f, tok], col[2 * t + b][:, c * P:c * P + P],
                                                       gain[:, at + f:at + f + 1], uhi[:, f, tok].bitcast(F32),
                                                       ALU.mult, ALU.subtract)
                    out.then_inc(u_lo, 1)

                residual(0)
                scale(0)
                residual(1)
                if gain is None or unit is None:
                    scale(1)
                if gain is not None:
                    lo(0, 0)
                    if unit is not None:
                        scale(1)
                    lo(0, 1)
                    lo(1, 0)
                    lo(1, 1)

            def softmax_max(a, h):
                dve.wait_ge(s_ps, HEADS * a + h + 1)
                if h >= 2:
                    dve.wait_ge(s_exp, NT * (HEADS * a + h - 1))
                dve.memset(apart[:], 0.0)
                for t in range(NT):
                    add = bias[:, t, h, :] if isinstance(a, int) else wk[:, t, :]
                    ins = dve.tensor_tensor_reduce(score[h % 2][:, t, :], S_BANK[h % 2][:, t * T:t * T + T], add, 1.0,
                                                   OUTSIDE * 1e6, ALU.add, ALU.max, mx[:, h % 2, t:t + 1])
                    if t == NT - 1:
                        link(ins)
                dve.tensor_scalar(nmx[:, h % 2, :], mx[:, h % 2, :], -1.0, None, ALU.mult).then_inc(s_max, 1)

            def softmax_norm(a, h):
                dve.wait_ge(s_exp, NT * (HEADS * a + h + 1))
                link(dve.reciprocal(rden[:, h % 2, :], den[:, h % 2, :]))
                for t in range(NT):
                    ins = dve.tensor_scalar(expo[h % 2][:, t, :], expo[h % 2][:, t, :], rden[:, h % 2, t:t + 1], None,
                                            ALU.mult)
                    if t == 0:
                        link(ins)
                ins.then_inc(p_ok, 1)

            def o_split(a, p):
                dve.wait_ge(o_hi, HEADS // 2 * a + p + 1)
                dve.tensor_tensor(mlo[:, KA + p, :], O_BANK[:, 0:T], mhi[:, KA + p, :].bitcast(F32), ALU.subtract)\
                    .then_inc(o_lo, 1)

            def conv_taps():
                for c in range(KA):
                    if c == POOL_CHUNK:
                        continue
                    for w in range(TAPS):
                        tap = kcol[:, w * KA + c:w * KA + c + 1]
                        if w == 0:
                            ins = dve.tensor_scalar(y[:, c, :], cu[:, c, 0:T], tap, gcol[:, G_DWB + c:G_DWB + c + 1],
                                                    ALU.mult, ALU.add)
                        else:
                            ins = dve.scalar_tensor_tensor(y[:, c, :], cu[:, c, w:w + T], tap, y[:, c, :],
                                                           ALU.mult, ALU.add)
                        link(ins)
                        yield c
            taps = conv_taps()

            def convolve(n):
                for _ in range(n):
                    next(taps, None)

            dve.memset(zeros[:], 0.0).then_inc(consts, 1)
            dve.memset(eps[:], EPS).then_inc(consts, 1)
            dve.memset(ones[:], 1.0 / DA).then_inc(consts, 1)
            link(dve.memset(cu[:], 0.0))
            norm(0, gcol, G_N1)
            split(a_unit(0))
            split(a_unit(1))
            for j in range(A_OUT):
                split(a_unit(j + 2))
                if j in (2, 4):
                    i = j // 2 - 1
                    dve.wait_ge(evac, j)
                    dve.tensor_tensor(cu[:, 2 * i:2 * i + 2, PAD:PAD + T], vtok[:, 0, :].rearrange("p (c t) -> p c t", c=2),
                                      vtok[:, 1, :].rearrange("p (c t) -> p c t", c=2), ALU.mult).then_inc(glu, 1)
                    dve.wait_ge(glu, i + 1)
                if j in (3, 5, 7, 9):
                    convolve(8)
                if j in (6, 8):
                    n = (j - 6) // 2
                    tok = (qtok, ktok)[n][:].rearrange("p t (h d) -> p (t h) d", d=DH)
                    dve.wait_ge(qsq, n + 1)
                    dve.tensor_reduce(ss[:], xn[:, 0:2, :].rearrange("p t (h d) -> p (t h) d", d=DH), AX_X, ALU.add)\
                        .then_inc(qss, 1)
                    dve.wait_ge(qsd, n + 1)
                    link(dve.reciprocal(rn[:], sd[:]))
                    dve.tensor_tensor(tok, tok, rn[:].unsqueeze(2).broadcast_to([P, NT * HEADS, DH]), ALU.mult)\
                        .then_inc(qk_tok, 1)
            dve.wait_ge(bias_ok, 8)
            softmax_max(0, 0)
            for h in range(HEADS):
                if h + 1 < HEADS:
                    softmax_max(0, h + 1)
                softmax_norm(0, h)
                convolve(8)
                if h % 2 == 0 and h >= 2:
                    o_split(0, h // 2 - 1)
            convolve(3 * TAPS)
            dve.memset(m8[:], 0.0).then_inc(conv_dve, 1)
            o_split(0, 3)
            dve.wait_ge(ln_mu, 1)
            dve.tensor_tensor(y[:], y[:], MU[:, 0:T].unsqueeze(1).broadcast_to([P, KA, T]), ALU.subtract).then_inc(ln_xc, 1)
            dve.wait_ge(ln_sd, 1)
            link(dve.reciprocal(xn[:, 1, 0:T], xn[:, 0, 0:T]))
            dve.tensor_tensor(y[:], y[:], xn[:, 1, 0:T].unsqueeze(1).broadcast_to([P, KA, T]), ALU.mult).then_inc(ln_y, 1)
            dve.wait_ge(ln_e, 1)
            dve.tensor_tensor(y[:], y[:], lne, ALU.mult).then_inc(c_ok, 1)
            dve.wait_ge(c_hi, 1)
            dve.tensor_tensor(mlo[:, 0:KA, :], y[:], mhi[:, 0:KA, :].bitcast(F32), ALU.subtract).then_inc(c_lo, 1)
            for j in range(A_OUT, A_FF):
                split(a_unit(j + 2))
            norm(1, gcol, G_N2, a_unit(A_FF - 1))

            def swiglu(b, q, up, count):
                e, h = ff_e[q], ff_h[q]
                dve.wait_ge(ff_act, count)
                link(dve.tensor_tensor(e, col[2 * q][:], e, ALU.mult))
                dve.wait_ge(used, up.upto())
                dve.tensor_tensor(h, col[2 * q + 1][:], e, ALU.mult).then_inc(ff_ok, 1)

            def ff_split(h, s, count):
                dve.wait_ge(ff_hi, count)
                dve.tensor_tensor(mid(mlo, s), h.rearrange("p (c t) -> p c t", c=2), mid(mhi, s).bitcast(F32),
                                  ALU.subtract).then_inc(ff_lo, 1)

            split(a_unit(A_FF + 2))
            swiglu(0, 0, a_unit(A_FF + 1), 1)
            ff_split(ff_h[0], 0, 1)
            with chain.loop(LOOPS, 2) as i:
                for q in range(2):
                    j = A_FF + 2 + 3 * q
                    b = (1 + q) % 2
                    split(a_unit(j + 1, i))
                    split(a_unit(j + 2, i))
                    swiglu(None, b, a_unit(j + 1, i), 2 * i + q + 2)
                    split(a_unit(j + 3, i))
                    ff_split(ff_h[b], b, 2 * i + q + 2)

            def select(t, rounds):
                v = wk[:, t, 0:P * (t + 1)]
                for _ in range(rounds):
                    chain.link_apart(dve.max(m8[:], v), apart[:])
                    chain.link_apart(dve.match_replace(v, m8[:], v, TAKEN), apart[:])

            dve.wait_ge(rope_in, 16)

            with chain.loop(LAYERS, LAYER_LINKS) as l:
                n0 = A_OUT + L_CONV * l
                dve.tensor_copy(lg[:], gcol[:, bass.ds(l * LG_N + G_LAYER, LG_N)]).then_inc(lg_ok, 1)
                split(l_unit(l, 0))
                norm(2 + 2 * l, lg, LG_MIX, l_unit(l, -1))
                split(l_unit(l, 1), KD * IKW)
                for j in range(L_CONV):
                    if j >= 14:
                        softmax_max(1 + l, j - 14)
                        softmax_norm(1 + l, j - 14)
                    split(l_unit(l, j + 2), unit_size(True, j + 2))
                    if j == 1:
                        dve.wait_ge(evac, n0 + 1)
                        rotate(dve, link, iqtok.rearrange("p t (h d) -> p t h d", d=64), IDX_HEADS, itmp).then_inc(idx_tok, 1)
                        dve.wait_ge(idx_tok, 2 * l + 1)
                    if j == 2:
                        dve.wait_ge(evac, n0 + 2)
                        link(rotate(dve, link, iktok[:, :, 0:64].rearrange("p t (h d) -> p t h d", d=64), 1, itmp))
                        dve.tensor_copy(iktok[:, :, 64:128], iktok[:, :, 0:64]).then_inc(idx_tok, 1)
                    if j == 5:
                        for h in range(IDX_HEADS):
                            dve.wait_ge(lgt_sb, IDX_HEADS * l + h + 1)
                            for t in range(NT):
                                n = P * (t + 1)
                                out, lgt, wt = wk[:, t, 0:n], big[:, 2 * h + t, 0:n], iw[:, t, h:h + 1]
                                if h == 0:
                                    link(dve.tensor_scalar(out, lgt, wt, None, ALU.mult))
                                else:
                                    link(dve.scalar_tensor_tensor(out, lgt, wt, out, ALU.mult, ALU.add))
                        dve.memset(wk[0:CHUNK, 0, CHUNK:P], NOT_ADMISSIBLE)
                        dve.memset(wk[:, 0, P:T], NOT_ADMISSIBLE)
                        link(dve.memset(wk[0:CHUNK, 1, P + CHUNK:T], NOT_ADMISSIBLE))
                    if 6 <= j < 10:
                        select(0, 2)
                        select(1, 1)
                    if 10 <= j < 12:
                        select(1, 2)
                    if j == 12:
                        dve.tensor_scalar(wk[:], wk[:], -2e38, OUTSIDE, ALU.is_ge, ALU.mult).then_inc(mask_ok, 1)
                        dve.wait_ge(mask_ok, l + 1)
                    if j % 2 == 1 and j >= 17:
                        o_split(1 + l, (j - 17) // 2)
                    if j == 17:
                        dve.wait_ge(c_hi, 2 + l)
                        dve.tensor_tensor(mlo[:, 0:KA, :], y[:], mhi[:, 0:KA, :].bitcast(F32), ALU.subtract).then_inc(c_lo, 1)
                for j in range(L_CONV, L_MLP):
                    if j < L_MLP - 1:
                        split(l_unit(l, j + 2), unit_size(True, j + 2))
                    if j == L_CONV:
                        o_split(1 + l, 3)
                    if L_ATTN < j <= L_MIX:
                        i = j - L_ATTN - 1
                        f = slice(2 * i, 2 * i + 2)
                        dve.wait_ge(g_hi, 4 * l + i + 1)
                        dve.tensor_tensor(ulo[:, f, :], big[:, f, :], uhi[:, f, :].bitcast(F32), ALU.subtract)\
                            .then_inc(g_lo, 1)
                    if j < L_ATTN:
                        i = j - L_CONV
                        g = big[:, KD + 2 * i:KD + 2 * i + 2, :]
                        dve.wait_ge(gate_ok, 8 * l + i + 1)
                        dve.wait_ge(used, l_unit(l, j).upto())
                        dve.tensor_tensor(g, col[i][:].rearrange("p (c t) -> p c t", c=2), g, ALU.mult).then_inc(merge_rd, 1)
                    elif j < L_MIX:
                        i = j - L_ATTN
                        m = big[:, 2 * i:2 * i + 2, :]
                        dve.wait_ge(gate_ok, 8 * l + 4 + i + 1)
                        dve.wait_ge(used, l_unit(l, j).upto())
                        link(dve.tensor_tensor(m, col[i][:].rearrange("p (c t) -> p c t", c=2), m, ALU.mult))
                        dve.tensor_tensor(m, m, big[:, KD + 2 * i:KD + 2 * i + 2, :], ALU.add).then_inc(merge_rd, 1)
                norm(3 + 2 * l, lg, LG_MLP, l_unit(l, L_MLP - 1))

                def square(s, count):
                    dve.wait_ge(ff_act, count)
                    dve.tensor_tensor(mlp_h[s], mlp_h[s], mlp_h[s], ALU.mult).then_inc(ff_ok, 1)

                done = FF_BLOCKS + MLP_BLOCKS * l
                split(l_unit(l, L_MLP + 1))
                square(0, done + 1)
                ff_split(mlp_h[0], 0, done + 1)
                with chain.loop(LOOPS, 0) as i:
                    for q in range(3):
                        s = (1 + q) % 3
                        split(l_unit(l, L_MLP + 2 + 2 * q, i))
                        split(l_unit(l, L_MLP + 3 + 2 * q, i))
                        square(s, done + 3 * i + q + 2)
                        ff_split(mlp_h[s], s, done + 3 * i + q + 2)

            last = 2 + 2 * LAYERS
            norm(last, None, None, l_unit(LAYERS - 1, L_UNITS - 1))
            dve.wait_ge(gfin_in, 16)
            for t in range(NT):
                dve.wait_ge(xn_ok, NT * last + t + 1)
                dve.tensor_tensor(xnt[:, t, :], xnt[:, t, :], gfin, ALU.mult).then_inc(fin, 1)

        @block.gpsimd
        def _(pool):
            chain = Chain(pool, pool_chain)
            link = chain.link
            tmp = [rtmp[:, 0:2, :].rearrange("p a b -> p (a b)"), rtmp[:, 2:4, :].rearrange("p a b -> p (a b)")]
            link(pool.memset(ident[:], 0.0))
            pool.affine_select(out=ident[:], in_=ident[:], compare_op=ALU.not_equal, fill=1.0, base=0,
                               pattern=[[-1, P]], channel_multiplier=1).then_inc(consts, 1)

            pool.wait_ge(bias_in, 16 * GRID_ROWS * GRID_ROWS)
            rows_k, half = T // GRID_W, NA_COLS // 2
            for t in range(NT):
                for p0 in (0, GRID_W):
                    v = bias[p0:p0 + GRID_W, t, :, :].rearrange("p h (r c) -> p h r c", c=GRID_W)
                    left, right = v[:, :, :, 0:GRID_W - NA_COLS], v[:, :, :, NA_COLS:GRID_W]
                    n = GRID_W - NA_COLS
                    pool.affine_select(out=left, in_=left, compare_op=ALU.is_ge, fill=OUTSIDE, base=half,
                                       pattern=[[0, HEADS], [0, rows_k], [1, n]], channel_multiplier=-1).then_inc(bias_ok, 1)
                    pool.wait_ge(bias_ok, 4 * t + p0 // GRID_W * 2 + 1)
                    pool.affine_select(out=right, in_=right, compare_op=ALU.is_ge, fill=OUTSIDE, base=half - 1 - NA_COLS,
                                       pattern=[[0, HEADS], [0, rows_k], [-1, n]], channel_multiplier=1).then_inc(bias_ok, 1)
                    pool.wait_ge(bias_ok, 4 * t + p0 // GRID_W * 2 + 2)

            c = POOL_CHUNK
            pool.wait_ge(par_sb, 3)
            pool.wait_ge(glu, c // 2 + 1)
            link(pool.tensor_scalar(y[:, c, :], cu[:, c, 0:T], kcol[:, c:c + 1], gcol[:, G_DWB + c:G_DWB + c + 1],
                                    ALU.mult, ALU.add))
            for w in range(1, TAPS):
                link(pool.tensor_scalar(tmp[w % 2], cu[:, c, w:w + T], kcol[:, w * KA + c:w * KA + c + 1], None, ALU.mult))
                add = pool.tensor_tensor(y[:, c, :], y[:, c, :], tmp[w % 2], ALU.add)
                if w < TAPS - 1:
                    link(add)
            add.then_inc(conv_pool, 1)

            pool.wait_ge(rope_in, 16)
            with chain.loop(LAYERS, POOL_LINKS) as l:
                n0 = A_OUT + L_CONV * l
                for n, tok in enumerate((qtok, ktok)):
                    pool.wait_ge(evac, n0 + 4 + 2 * n)
                    rotate(pool, link, tok[:].rearrange("p t (h d) -> p t h d", d=DH), HEADS, rtmp).then_inc(rope_tok, 1)
                    pool.wait_ge(rope_tok, 2 * l + n + 1)
                pool.wait_ge(lg_ok, l + 1)
                pool.wait_ge(evac, n0 + 12)
                link(pool.tensor_tensor(cu[:, :, CONV_K - 1:CONV_K - 1 + T], cC, cH, ALU.mult))
                for w in range(CONV_K):
                    for c in range(KA):
                        tap = lg[:, LG_CONV + w * KA + c:LG_CONV + w * KA + c + 1]
                        out = y[:, c, :] if w == 0 else tmp[c % 2]
                        link(pool.tensor_tensor(out, cu[:, c, w:w + T], tap.broadcast_to([P, T]), ALU.mult))
                        if w:
                            link(pool.tensor_tensor(y[:, c, :], y[:, c, :], out, ALU.add))
                pool.wait_ge(evac, n0 + 14)
                pool.tensor_tensor(y[:], y[:], cB[:], ALU.mult).then_inc(c_ok, 1)


_MATRICES = ["x", "w_in", "rpb", "w_out", "w_gate", "w_up", "w_down", "w_in_2", "w_attn_out_2", "w_conv_out_2",
             "w_mix_out_2", "w_mlp_up_2", "w_mlp_down_2", "norm_final_2"]


def rope_table():
    inv = 1.0 / (np.float32(500000.0) ** (np.arange(0, 16, 2, dtype=np.float32) / np.float32(16)))
    ang = np.arange(T, dtype=np.float32)[:, None] * inv[None, :].astype(np.float32)
    return np.concatenate([np.cos(ang), np.sin(ang)], axis=1).astype(np.float32)


def parameter_rows(inputs):
    def rows(a):
        return np.asarray(a).reshape(-1, P)
    qk = [np.tile(np.asarray(inputs[name])[0], P // DH)[None] for name in ("q_norm_g", "k_norm_g")]
    first = [rows(inputs[name]) for name in ("norm1_g", "norm2_g", "dw_bias", "conv_ln_g", "conv_ln_b")]
    layers = [rows(inputs[name][l]) for l in range(LAYERS) for name in ("norm_mix_2", "norm_mlp_2", "conv_w_2")]
    return np.concatenate(first + qk + layers + [rows(inputs["dw_kernel"])])


def kernel(**inputs):
    import concourse.bacc as bacc
    from concourse.bass_utils import run_bass_kernel_spmd as run

    nc = bacc.Bacc("TRN2", target_bir_lowering=False, num_devices=1)
    arrays, d = {}, {}
    for name in _MATRICES:
        a = np.ascontiguousarray(inputs[name])
        arrays[f"in_{name}"] = a
        d[name] = nc.dram_tensor(f"in_{name}", a.shape, F32, kind="ExternalInput").ap()
    arrays["in_rope"] = rope_table()
    d["rope"] = nc.dram_tensor("in_rope", arrays["in_rope"].shape, F32, kind="ExternalInput").ap()
    arrays["in_params"] = parameter_rows(inputs)
    d["params"] = nc.dram_tensor("in_params", arrays["in_params"].shape, F32, kind="ExternalInput").ap()
    d["out"] = nc.dram_tensor("out", (1, T, D), F32, kind="ExternalOutput").ap()
    d["skew"] = nc.dram_tensor("skew", (HEADS, 2 * GRID_ROWS - 1, GRID_W, GRID_W), F32).ap()
    build(nc, d)
    return run(nc, [arrays], core_ids=[0]).results[0]["out"]
```

```python
from contextlib import ExitStack, contextmanager

import numpy as np
import concourse.bass as bass
from concourse import mybir

F32 = mybir.dt.float32
F32R = mybir.dt.float32r
ALU = mybir.AluOpType
ACT = mybir.ActivationFunctionType
AX_X = mybir.AxisListType.X

P = 128
D = 1024
T = 256
NT = T // P
KD = D // P
HEADS, DH = 8, 64
DA = HEADS * DH
KA = DA // P
GRID_W, NA_ROWS, NA_COLS = 64, 8, 16
GRID_ROWS = T // GRID_W
TAPS = 31
PAD = TAPS // 2
D_FF = 2816
D_MLP = 4096
LAYERS = 2
IDX_HEADS = 4
CHUNK, TOPK = 64, 64
CONV_K = 3
ROPE_HALF = 8
EPS = 1e-6
SCALE = DH ** -0.5
IDX_SCALE = (64 ** -0.5) * (IDX_HEADS ** -0.5)
OUTSIDE = -1e30
NOT_ADMISSIBLE = -1e38
TAKEN = -3e38

COLS = 256
UNIT = 2048
RING, SPLIT = 6, 3
FF_BLOCKS, MLP_BLOCKS = D_FF // COLS, D_MLP // COLS
A_OUT, A_FF = 10, 14
A_UNITS = A_FF + 3 * FF_BLOCKS
L_CONV, L_ATTN, L_MIX, L_MLP = 22, 26, 30, 34
L_UNITS = L_MLP + 2 * MLP_BLOCKS
LOOPS = 5
IQ0, IK0, CB0, CC0, CH0, G0 = 1536, 1792, 1860, 2372, 2884, 3396
IKW = 68
L_COLS = [IK0, IQ0, 0, 256, 512, 768, 1024, 1280, CC0, CC0 + 256, CH0, CH0 + 256, CB0, CB0 + 256] \
    + [G0 + COLS * i for i in range(8)]
A_COLS = [512, 0, 768, 256, 1024, 1280, 1536, 1792, 2048, 2304]
A_OUT_ROWS = [2, 3, 0, 1]

G_N1, G_N2, G_DWB, G_LNG, G_LNB, G_QG, G_KG, G_LAYER = 0, 8, 16, 20, 24, 28, 29, 30
LG_MIX, LG_MLP, LG_CONV, LG_N = 0, 8, 16, 28
G_N = G_LAYER + LAYERS * LG_N
LAYER_LINKS = 76
POOL_LINKS = 23
FIRST_TAPS, GP_SUMS = 4, 27
TAPS_AT = (0, 0, 8, 0, 8, 8, 0, 1, 8, 4)
TAPS_AT_HEAD = 4
DVE_TAPS = KA * TAPS - 2 * GP_SUMS
WARM_START, WARM_HEAD = 10, 5
PARTS = 6
WARM = 10


class Unit:
    def __init__(self, st, turns=0):
        self.st, self.turns = st, turns
        self.slot, self.buf = st % RING, st % SPLIT
        self.landed = 16 * (st // RING + 1) + 16 * turns

    def upto(self, back=0):
        return self.st - back + 1 + RING * self.turns


class Chain:
    def __init__(self, eng, sem):
        self.eng, self.sem, self.n, self.run = eng, sem, 0, 0

    def link(self, ins):
        self.n += 1
        ins.then_inc(self.sem, 1)
        self.eng.wait_ge(self.sem, self.n + self.run)

    def link_apart(self, ins, scratch):
        self.link(ins)
        self.eng.memset(scratch, 0.0)

    @contextmanager
    def loop(self, turns, per):
        with self.eng.Fori(0, turns) as i:
            n, run = self.n, self.run
            self.run = run + per * i
            yield i
            assert self.n - n == per, (self.n - n, per)
            self.n, self.run = n + per * turns, run


def build(nc, d):
    w_in = d["w_in"][0].rearrange("(k p) n -> p k n", p=P)
    w_out = d["w_out"][0].rearrange("(k p) n -> p k n", p=P)
    w_gate = d["w_gate"][0].rearrange("(k p) n -> p k n", p=P)
    w_up = d["w_up"][0].rearrange("(k p) n -> p k n", p=P)
    w_down = d["w_down"][0].rearrange("(k p) n -> p k n", p=P)

    def per_layer(name):
        return d[name].rearrange("l (k p) n -> p l k n", p=P)

    w_in2, w_attn2, w_conv2 = per_layer("w_in_2"), per_layer("w_attn_out_2"), per_layer("w_conv_out_2")
    w_mix2, w_mup2, w_mdown2 = per_layer("w_mix_out_2"), per_layer("w_mlp_up_2"), per_layer("w_mlp_down_2")

    with ExitStack() as ctx:
        def sb(name, shape, dt=F32):
            return ctx.enter_context(nc.sbuf_tensor(name, shape, dt))

        def sem(name):
            return ctx.enter_context(nc.semaphore(name))

        raw = sb("raw", [P, RING, UNIT])
        whi = sb("whi", [P, SPLIT, UNIT], F32R)
        wlo = sb("wlo", [P, SPLIT, UNIT], F32R)
        x = sb("x", [P, NT, D])
        xn = sb("xn", [P, 4, 512])
        uhi = sb("uhi", [P, KD, T], F32R)
        ulo = sb("ulo", [P, KD, T], F32R)
        mhi = sb("mhi", [P, KD, T], F32R)
        mlo = sb("mlo", [P, KD, T], F32R)
        big = sb("big", [P, 16, T])
        qtok = sb("qtok", [P, NT, DA])
        ktok = sb("ktok", [P, NT, DA])
        vtok = sb("vtok", [P, NT, DA])
        qT = sb("qT", [P, KA, T])
        kT = sb("kT", [P, KA, T])
        prob = sb("prob", [P, 2, NT * T])
        wk = sb("wk", [P, NT, T])
        cu = sb("cu", [P, KA, T + 2 * PAD])
        y = sb("y", [P, KA, T])
        cB = sb("cB", [P, KA, T])
        ident = sb("ident", [P, P])
        ones = sb("ones", [P, P])
        grow = sb("grow", [P, P])
        krow = sb("krow", [P, P])
        gcol = sb("gcol", [P, G_N])
        kcol = sb("kcol", [P, TAPS * KA])
        lg = sb("lg", [P, LG_N])
        rope = sb("rope", [P, NT, 2 * ROPE_HALF])
        iw = sb("iw", [P, NT, IDX_HEADS])
        ss = sb("ss", [P, 16])
        sd = sb("sd", [P, 16])
        rn = sb("rn", [P, 16])
        mx = sb("mx", [P, 2, NT])
        nmx = sb("nmx", [P, 2, NT])
        den = sb("den", [P, 2, NT])
        rden = sb("rden", [P, 2, NT])
        m8 = sb("m8", [P, 8])
        apart = sb("apart", [P, 1])
        eps = sb("eps", [P, 1])
        qg = sb("qg", [P, 1])
        zeros = sb("zeros", [P, 512], mybir.dt.bfloat16)
        wmask = sb("wmask", [P, GRID_ROWS, GRID_W], mybir.dt.bfloat16)
        ident16 = sb("ident16", [P, P], mybir.dt.bfloat16)
        rtmp = sb("rtmp", [P, 4, NT * HEADS * ROPE_HALF])
        itmp = sb("itmp", [P, 4, NT * IDX_HEADS * ROPE_HALF])
        xnt = xn[:].rearrange("p (t a) b -> p t (a b)", t=NT)
        score = [xn[:, 0, :].rearrange("p (t k) -> p t k", t=NT), xn[:, 1, :].rearrange("p (t k) -> p t k", t=NT)]
        expo = [xn[:, 2, :].rearrange("p (t k) -> p t k", t=NT), xn[:, 3, :].rearrange("p (t k) -> p t k", t=NT)]
        iqtok = y[:, 0:2, :]
        iktok = y[:, 2, :].rearrange("p (t c) -> p t c", t=NT)
        iqT = prob[:, 0, :].rearrange("p (c t) -> p c t", c=2)
        ikT = prob[:, 1, 0:T]
        ikf = prob[:, 1, T:2 * T]
        cC = qtok[:].rearrange("p a (b t) -> p (a b) t", t=T)
        cH = ktok[:].rearrange("p a (b t) -> p (a b) t", t=T)
        lnsq, lne, lnz = cC, cH, cC
        lnsd, lnr = xn[:, 0, 0:T], xn[:, 1, 0:T]
        gfin = qT[:].rearrange("p a b -> p (a b)")
        ff_e = [xn[:, 0, :], xn[:, 1, :]]
        ff_h = [xn[:, 2, :], xn[:, 3, :]]
        mlp_h = [xn[:, 0, :], xn[:, 1, :], xn[:, 2, :]]
        bias = big[:].rearrange("p (t h) k -> p t h k", t=NT)

        acc = [ctx.enter_context(nc.psum_tensor(f"acc{i}", [P, 512], F32)) for i in range(4)]
        col = [ctx.enter_context(nc.psum_tensor(f"col{i}", [P, 512], F32)) for i in range(4)]
        S_BANK, T_BANK, O_BANK = (acc[0], acc[1]), acc[2], acc[3]
        MU, VAR = col[0], col[1]

        landed = [sem(f"landed{i}") for i in range(RING)]
        w_hi = sem("w_hi")
        w_lo = sem("w_lo")
        used = sem("used")
        x_in = [sem(f"x_in{t}") for t in range(NT)]
        par_in = sem("par_in")
        rope_in = sem("rope_in")
        skew_in = sem("skew_in")
        bias_in = sem("bias_in")
        gfin_in = sem("gfin_in")
        out_done = sem("out_done")
        consts = sem("consts")
        par_ps = sem("par_ps")
        par_sb = sem("par_sb")
        wmask_ok = sem("wmask_ok")
        acc_ok = sem("acc_ok")
        x_new = sem("x_new")
        sq_done = sem("sq_done")
        sd_done = sem("sd_done")
        xn_ok = sem("xn_ok")
        u_ps = sem("u_ps")
        u_hi = sem("u_hi")
        u_lo = sem("u_lo")
        evac = sem("evac")
        glu = sem("glu")
        qsq = sem("qsq")
        qss = sem("qss")
        qsd = sem("qsd")
        qk_tok = sem("qk_tok")
        rope_tok = sem("rope_tok")
        qk_ps = sem("qk_ps")
        qk_T = sem("qk_T")
        s_ps = sem("s_ps")
        s_max = sem("s_max")
        s_exp = sem("s_exp")
        p_ok = sem("p_ok")
        p_ps = sem("p_ps")
        p_T = sem("p_T")
        o_ps = sem("o_ps")
        o_hi = sem("o_hi")
        o_lo = sem("o_lo")
        conv_prod = sem("conv_prod")
        conv_pool = sem("conv_pool")
        conv_dve = sem("conv_dve")
        rden_ok = sem("rden_ok")
        ln_mu = sem("ln_mu")
        ln_xc = sem("ln_xc")
        ln_sq = sem("ln_sq")
        ln_var = sem("ln_var")
        ln_sd = sem("ln_sd")
        ln_y = sem("ln_y")
        ln_e = sem("ln_e")
        c_ok = sem("c_ok")
        c_hi = sem("c_hi")
        c_lo = sem("c_lo")
        ik_sb = sem("ik_sb")
        ik_ps = sem("ik_ps")
        idx_tok = sem("idx_tok")
        idx_ps = sem("idx_ps")
        idx_T = sem("idx_T")
        lgt_ps = sem("lgt_ps")
        lgt_sb = sem("lgt_sb")
        lg_ok = sem("lg_ok")
        mask_ok = sem("mask_ok")
        gate_ok = sem("gate_ok")
        merge_rd = sem("merge_rd")
        g_hi = sem("g_hi")
        g_lo = sem("g_lo")
        ff_act = sem("ff_act")
        ff_ok = sem("ff_ok")
        ff_hi = sem("ff_hi")
        ff_lo = sem("ff_lo")
        fin = sem("fin")
        dve_chain = sem("dve_chain")
        act_chain = sem("act_chain")
        pool_chain = sem("pool_chain")

        def whi_v(u, n=COLS):
            return whi[:, u.buf, :].rearrange("p (k n) -> p k n", n=n)

        def wlo_v(u, n=COLS):
            return wlo[:, u.buf, :].rearrange("p (k n) -> p k n", n=n)

        def ikw_v(buf):
            return buf[:, 0:KD * IKW].rearrange("p (k n) -> p k n", n=IKW)

        def unit_size(layer, j):
            if layer and j == 0:
                return KD * IKW
            return KA * COLS if layer and L_CONV <= j < L_MIX else UNIT

        def a_unit(j, turns=0):
            return Unit(j, turns)

        def l_unit(l, j, turns=0):
            return Unit(A_UNITS + j, L_UNITS // RING * l + turns)

        def rotate(eng, link, v, nh, tmp):
            x1, x2 = v[:, :, :, 0:ROPE_HALF], v[:, :, :, ROPE_HALF:2 * ROPE_HALF]
            cos = rope[:, :, 0:ROPE_HALF].unsqueeze(2).broadcast_to([P, NT, nh, ROPE_HALF])
            sin = rope[:, :, ROPE_HALF:2 * ROPE_HALF].unsqueeze(2).broadcast_to([P, NT, nh, ROPE_HALF])
            x1c, x2s, x2c, x1s = (tmp[:, r, 0:NT * nh * ROPE_HALF].rearrange("p (t h r) -> p t h r", t=NT, h=nh)
                                  for r in range(4))
            eng.tensor_tensor(x1c, x1, cos, ALU.mult)
            eng.tensor_tensor(x2s, x2, sin, ALU.mult)
            eng.tensor_tensor(x2c, x2, cos, ALU.mult)
            link(eng.tensor_tensor(x1s, x1, sin, ALU.mult))
            eng.tensor_tensor(x1, x1c, x2s, ALU.subtract)
            return eng.tensor_tensor(x2, x2c, x1s, ALU.add)

        part_a, part_b = [(0, range(4 * b, 4 * b + 4), acc[b]) for b in range(2)]
        second = [(1, range(2 * b, 2 * b + 2), (acc[2], acc[3], col[2], col[3])[b]) for b in range(4)]

        def norm_parts(k):
            if isinstance(k, int) and k == 0:
                return [part_a] + second[0:2] + [part_b] + second[2:4]
            return [part_a, part_b] + second

        def norm_count(k, t, f):
            at = [i for i, (pt, fs, _) in enumerate(norm_parts(k)) if pt == t and f in fs][0]
            return PARTS * k + at + 1

        def mid(buf, s):
            return buf[:, 2 * s:2 * s + 2, :]

        def keys(a, t):
            return T if isinstance(a, int) else P * (t + 1)

        block = ctx.enter_context(nc.Block())

        @block.sync
        def _(sp):
            def load(u, src, size=UNIT, free=...):
                free = u if free is ... else free
                if free is not None and not (isinstance(u.turns, int) and u.st < RING):
                    sp.wait_ge(w_lo, free.upto(RING))
                dst = raw[:, u.slot, 0:size].rearrange("p (k n) -> p k n", n=src.shape[-1])
                sp.dma_start(dst, src).then_inc(landed[u.slot], 16)

            for t in range(NT):
                sp.dma_start(x[:, t, :], d["x"][0, t * P:(t + 1) * P, :]).then_inc(x_in[t], 16)
            load(a_unit(0), w_in[:, :, A_COLS[0]:A_COLS[0] + COLS])
            for j in range(1, A_OUT):
                load(a_unit(j), w_in[:, :, A_COLS[j]:A_COLS[j] + COLS])
                if j == 3:
                    n, (rh, rw) = 2 * GRID_ROWS - 1, d["rpb"].shape[2:]
                    for h in range(HEADS):
                        skew = bass.AP(tensor=d["rpb"].tensor, offset=(h * rh + NA_ROWS - GRID_ROWS) * rw + NA_COLS - 1,
                                       ap=[[rw, n], [-1, GRID_W], [1, GRID_W]])
                        sp.dma_start(d["skew"][h], skew).then_inc(skew_in, 16)
                if j == 5:
                    sp.wait_ge(skew_in, 16 * HEADS)
                    for qr in range(GRID_ROWS):
                        r0, p0 = GRID_ROWS - 1 - qr, qr % 2 * GRID_W
                        for r in range(GRID_ROWS):
                            dst = bias[p0:p0 + GRID_W, qr // 2, :, r * GRID_W:(r + 1) * GRID_W]
                            sp.dma_start(dst, d["skew"][:, r0 + r, :, :].rearrange("h q c -> q h c")).then_inc(bias_in, 16)
                    sp.dma_start(rope[:], d["rope"].rearrange("(t p) n -> p t n", p=P)).then_inc(rope_in, 16)
            for i, r in enumerate(A_OUT_ROWS):
                load(a_unit(A_OUT + i), w_out[:, 2 * r:2 * r + 2, :])
            load(a_unit(A_FF), w_gate[:, :, 0:COLS])
            load(a_unit(A_FF + 1), w_up[:, :, 0:COLS])
            with sp.Fori(0, LOOPS) as i:
                for q in range(2):
                    at = i * (2 * COLS) + (1 + q) * COLS
                    load(a_unit(A_FF + 2 + 3 * q, i), w_gate[:, :, bass.ds(at, COLS)])
                    load(a_unit(A_FF + 3 + 3 * q, i), w_up[:, :, bass.ds(at, COLS)])
                    load(a_unit(A_FF + 4 + 3 * q, i), w_down[:, bass.ds(i * 4 + 2 * q, 2), :])
            load(a_unit(A_UNITS - 1), w_down[:, 2 * FF_BLOCKS - 2:2 * FF_BLOCKS, :])

            with sp.Fori(0, LAYERS) as l:
                def of(w):
                    return w[:, bass.ds(l, 1)].rearrange("p l k n -> p (l k) n")
                for j in range(L_CONV):
                    n = IKW if j == 0 else COLS
                    load(l_unit(l, j), of(w_in2)[:, :, L_COLS[j]:L_COLS[j] + n], KD * n,
                         None if j == 2 else l_unit(l, 2 if j == 1 else j))
                for at, w in ((L_CONV, w_conv2), (L_ATTN, w_attn2)):
                    for i in range(4):
                        load(l_unit(l, at + i), of(w)[:, :, COLS * i:COLS * i + COLS], KA * COLS)
                for i in range(4):
                    load(l_unit(l, L_MIX + i), of(w_mix2)[:, 2 * i:2 * i + 2, :])
                load(l_unit(l, L_MLP), of(w_mup2)[:, :, 0:COLS])
                with sp.Fori(0, LOOPS) as i:
                    for q in range(3):
                        load(l_unit(l, L_MLP + 1 + 2 * q, i), of(w_mup2)[:, :, bass.ds(i * (3 * COLS) + (1 + q) * COLS, COLS)])
                        load(l_unit(l, L_MLP + 2 + 2 * q, i), of(w_mdown2)[:, bass.ds(i * 6 + 2 * q, 2), :])
                load(l_unit(l, L_UNITS - 1), of(w_mdown2)[:, 2 * MLP_BLOCKS - 2:2 * MLP_BLOCKS, :])
            sp.wait_ge(w_lo, A_UNITS + LAYERS * L_UNITS - 2)
            sp.dma_start(gfin, d["norm_final_2"].partition_broadcast(P)).then_inc(gfin_in, 16)
            for t in range(NT):
                sp.wait_ge(fin, t + 1)
                sp.dma_start(d["out"][0, t * P:(t + 1) * P, :], xnt[:, t, :]).then_inc(out_done, 16)
            sp.wait_ge(out_done, 16 * NT)


        @block.tensor
        def _(pe):
            def mm3(out, l_hi, l_lo, r_hi, r_lo, start, stop):
                pe.matmul(out, l_hi, r_hi, start=start, stop=False)
                pe.matmul(out, l_hi, r_lo, start=False, stop=False)
                return pe.matmul(out, l_lo, r_hi, start=False, stop=stop)

            def col_tokens(u, bank, between=None):
                for t in range(NT):
                    tok = slice(t * P, t * P + P)
                    for k in range(KD):
                        mm = mm3(bank[:, t * COLS:t * COLS + COLS], uhi[:, k, tok], ulo[:, k, tok],
                                 whi_v(u)[:, k, :], wlo_v(u)[:, k, :], k == 0, k == KD - 1)
                    if t == 0 and between:
                        between()
                mm.then_inc(used, 1)

            def col_features(u, bank, hi_in, lo_in, kc=KD, norm=None):
                for c in range(COLS // P):
                    for k in range(kc):
                        if norm is not None and c == 0:
                            pe.wait_ge(u_lo, norm_count(norm, 1, k))
                        cs = slice(c * P, c * P + P)
                        mm = mm3(bank[:, c * T:c * T + T], whi_v(u)[:, k, cs], wlo_v(u)[:, k, cs],
                                 hi_in[:, k, :], lo_in[:, k, :], k == 0, k == kc - 1)
                mm.then_inc(used, 1)

            def rows_half(u, t, hi_in, lo_in, start, stop):
                for h in range(2):
                    for c in range(2):
                        tok = slice(t * P, t * P + P)
                        cs = slice(h * 512, h * 512 + 512)
                        mm = mm3(acc[2 * t + h][:], hi_in[:, c, tok], lo_in[:, c, tok],
                                 whi_v(u, D)[:, c, cs], wlo_v(u, D)[:, c, cs], start and c == 0, stop and c == 1)
                return mm

            def rows(u, hi_in, lo_in, start, stop):
                mm = rows_half(u, 0, hi_in, lo_in, start, stop)
                if stop:
                    mm.then_inc(acc_ok, 1)
                rows_half(u, 1, hi_in, lo_in, start, stop).then_inc(used, 1)

            def last_rows(u, hi_u, lo_u, v, hi_v, lo_v):
                rows_half(u, 0, hi_u, lo_u, False, False)
                rows_half(v, 0, hi_v, lo_v, False, True).then_inc(acc_ok, 1)
                rows_half(u, 1, hi_u, lo_u, False, False).then_inc(used, 1)
                rows_half(v, 1, hi_v, lo_v, False, True).then_inc(used, 1)

            def keep_warm(n, bank=col[0]):
                for _ in range(n):
                    pe.matmul(bank[:], zeros[:, 0:P], zeros[:], start=True, stop=True)

            def parameter_transposes():
                pe.wait_ge(par_in, 16 * 2)
                pe.transpose(col[0][:, 0:G_N], grow[0:G_N, :], ident[0:G_N, 0:G_N])
                pe.transpose(col[1][:, 0:TAPS * KA], krow[0:TAPS * KA, :], ident[0:TAPS * KA, 0:TAPS * KA]).then_inc(par_ps, 1)

            def norm_transposes(k, between=None):
                for t in range(NT):
                    if t == 1:
                        if between:
                            between()
                        else:
                            keep_warm(WARM)
                    pe.wait_ge(xn_ok, NT * k + t + 1)
                    for _, fs, bank in (second if t else (part_a, part_b)):
                        for i, f in enumerate(fs):
                            tr = pe.transpose(bank[:, i * P:i * P + P], xnt[:, t, f * P:f * P + P], ident[:])
                        tr.then_inc(u_ps, 1)

            def turn(tok, n):
                for b in range(2):
                    bank = acc[2 * n + b]
                    for c in range(2):
                        for t in range(NT):
                            f = 2 * b + c
                            tr = pe.transpose(bank[:, c * T + t * P:c * T + t * P + P], tok[:, t, f * P:f * P + P], ident[:])
                    tr.then_inc(qk_ps, 1)

            def scores(a, h):
                pe.wait_ge(qk_T, 4 * a + 4)
                if h >= 2:
                    pe.wait_ge(s_max, HEADS * a + h - 1)
                off = DH * (h % 2)
                for t in range(NT):
                    out = S_BANK[h % 2][:, t * T:t * T + keys(a, t)]
                    windowed = isinstance(a, int)
                    mm = pe.matmul(out, qT[off:off + DH, h // 2, t * P:t * P + P], kT[off:off + DH, h // 2, 0:keys(a, t)],
                                   start=True, stop=not windowed)
                    if windowed:
                        mm = pe.matmul(out, ident16[:], wmask[:].rearrange("p r c -> p (r c)"), start=False, stop=True)
                mm.then_inc(s_ps, 1)

            def turn_probs(a, h):
                pe.wait_ge(p_ok, HEADS * a + h + 1)
                if h >= 1:
                    pe.wait_ge(p_T, HEADS * a + h)
                for kt in range(NT):
                    for t in range(NT):
                        if kt * P >= keys(a, t):
                            continue
                        tr = pe.transpose(T_BANK[:, kt * T + t * P:kt * T + t * P + P],
                                          expo[h % 2][:, t, kt * P:kt * P + P], ident[:])
                tr.then_inc(p_ps, 1)

            def values(a, h):
                pe.wait_ge(p_T, HEADS * a + h + 1)
                if h % 2 == 0 and h >= 2:
                    pe.wait_ge(o_lo, HEADS // 2 * a + h // 2)
                off = DH * (h % 2)
                for kt in range(NT):
                    t0 = 0 if kt * P < keys(a, 0) else P
                    mm = pe.matmul(O_BANK[off:off + DH, t0:T], vtok[:, kt, h * DH:h * DH + DH],
                                   prob[:, h % 2, kt * T + t0:kt * T + T], start=kt == 0, stop=kt == NT - 1)
                mm.then_inc(o_ps, 1)

            pe.wait_ge(consts, 4)
            keep_warm(WARM_START)
            norm_transposes(0, parameter_transposes)
            def first_scores():
                pe.wait_ge(wmask_ok, 5)
                scores(0, 0)

            for j in range(A_OUT):
                u = a_unit(j)
                pe.wait_ge(w_lo, u.upto())
                if j >= 4:
                    pe.wait_ge(evac, j - 3)
                if j < 4:
                    col_features(u, col[j % 4], uhi, ulo, norm=0 if j == 0 else None)
                else:
                    col_tokens(u, col[j % 4], between=first_scores if j == A_OUT - 1 else None)
                if j == 7 or j == 8:
                    n = j - 7
                    pe.wait_ge(qk_tok, n + 1)
                    turn((qtok, ktok)[n], n)
            for h in range(HEADS):
                if h + 1 < HEADS:
                    scores(0, h + 1)
                else:
                    pe.wait_ge(conv_dve, DVE_TAPS)
                    pe.wait_ge(conv_pool, GP_SUMS)
                    for c in range(KA):
                        mm = pe.matmul(MU[:, 0:T], ones[:], y[:, c, :], start=c == 0, stop=c == KA - 1)
                    mm.then_inc(ln_mu, 1)
                keep_warm(WARM_HEAD, col[3])
                turn_probs(0, h)
                if h == 1:
                    pe.wait_ge(evac, A_OUT)
                if h >= 1:
                    values(0, h - 1)
            values(0, HEADS - 1)
            pe.wait_ge(ln_sq, 2)
            for c in range(KA):
                mm = pe.matmul(VAR[:, 0:T], ones[:], lnsq[:, c, :], start=c == 0, stop=c == KA - 1)
            mm.then_inc(ln_var, 1)
            for i, r in enumerate(A_OUT_ROWS):
                u = a_unit(A_OUT + i)
                pe.wait_ge(w_lo, u.upto())
                if i == 0:
                    pe.wait_ge(o_lo, HEADS // 2)
                if i >= 2:
                    pe.wait_ge(c_lo, i - 1)
                if i < 2:
                    rows(u, mhi[:, 2 * r:2 * r + 2, :], mlo[:, 2 * r:2 * r + 2, :], i == 0, False)
            last_rows(a_unit(A_OUT + 2), mhi[:, 0:2, :], mlo[:, 0:2, :], a_unit(A_OUT + 3), mhi[:, 2:4, :], mlo[:, 2:4, :])

            def open_acc():
                for bank in acc:
                    pe.matmul(bank[:], zeros[:, 0:P], zeros[:], start=True, stop=False)

            norm_transposes(1)
            pe.wait_ge(w_lo, a_unit(A_FF).upto())
            col_features(a_unit(A_FF), col[0], uhi, ulo, norm=1)
            pe.wait_ge(w_lo, a_unit(A_FF + 1).upto())
            col_features(a_unit(A_FF + 1), col[1], uhi, ulo)
            open_acc()
            with pe.Fori(0, LOOPS) as i:
                for q in range(2):
                    gate, up, down = (a_unit(A_FF + 2 + 3 * q + r, i) for r in range(3))
                    bank = 2 * ((1 + q) % 2)
                    pe.wait_ge(w_lo, gate.upto())
                    col_features(gate, col[bank], uhi, ulo)
                    pe.wait_ge(w_lo, up.upto())
                    col_features(up, col[bank + 1], uhi, ulo)
                    pe.wait_ge(w_lo, down.upto())
                    pe.wait_ge(ff_lo, 2 * i + q + 1)
                    rows(down, mid(mhi, q), mid(mlo, q), False, False)
            pe.wait_ge(w_lo, a_unit(A_UNITS - 1).upto())
            pe.wait_ge(ff_lo, FF_BLOCKS)
            rows(a_unit(A_UNITS - 1), mid(mhi, 0), mid(mlo, 0), False, True)

            with pe.Fori(0, LAYERS) as l:
                norm_transposes(2 + 2 * l)
                u = l_unit(l, 0)
                pe.wait_ge(w_lo, u.upto())
                hi, lo = ikw_v(whi[:, u.buf, :]), ikw_v(wlo[:, u.buf, :])
                for k in range(KD):
                    pe.wait_ge(u_lo, norm_count(2 + 2 * l, 1, k))
                    mm = mm3(col[0][0:IKW, 0:T], hi[:, k, :], lo[:, k, :], uhi[:, k, :], ulo[:, k, :], k == 0, k == KD - 1)
                mm.then_inc(used, 1)
                for j in range(1, L_CONV):
                    u = l_unit(l, j)
                    pe.wait_ge(w_lo, u.upto())
                    if j >= 4:
                        pe.wait_ge(evac, A_OUT + L_CONV * l + j - 3)
                    if j < 8:
                        col_tokens(u, col[j % 4])
                    else:
                        col_features(u, col[j % 4], uhi, ulo)
                    if j == 1:
                        pe.wait_ge(ik_sb, l + 1)
                        for t in range(NT):
                            tr = pe.transpose(acc[1][:, t * IKW:t * IKW + IKW], ikf[0:IKW, t * P:t * P + P],
                                              ident[0:IKW, 0:IKW])
                        tr.then_inc(ik_ps, 1)
                    if j == 3:
                        pe.wait_ge(idx_tok, 2 * l + 2)
                        for c in range(2):
                            for t in range(NT):
                                pe.transpose(acc[0][:, c * T + t * P:c * T + t * P + P],
                                             iqtok[:, t, c * P:c * P + P], ident[:])
                        for t in range(NT):
                            tr = pe.transpose(acc[1][:, t * P:t * P + P], iktok[:, t, :], ident[:])
                        tr.then_inc(idx_ps, 1)
                    if j == 4:
                        pe.wait_ge(idx_T, 2 * l + 2)
                        for h in range(IDX_HEADS):
                            off = 64 * (h % 2)
                            for t in range(NT):
                                mm = pe.matmul(acc[h][:, t * T:t * T + T], iqT[off:off + 64, h // 2, t * P:t * P + P],
                                               ikT[off:off + 64, :], start=True, stop=True)
                        mm.then_inc(lgt_ps, 1)
                    if j == 6:
                        pe.wait_ge(lgt_sb, IDX_HEADS * l + IDX_HEADS)
                        pe.wait_ge(rope_tok, 2 * l + 1)
                        turn(qtok, 0)
                    if j == 7:
                        pe.wait_ge(rope_tok, 2 * l + 2)
                        turn(ktok, 1)
                    if j == 13:
                        scores(1 + l, 0)
                    if j >= 14:
                        h = j - 14
                        if h + 1 < HEADS:
                            scores(1 + l, h + 1)
                        turn_probs(1 + l, h)
                        if h >= 1:
                            values(1 + l, h - 1)
                for i in range(4):
                    u = l_unit(l, L_CONV + i)
                    pe.wait_ge(w_lo, u.upto())
                    pe.wait_ge(evac, A_OUT + L_CONV * l + 19 + i)
                    if i == 0:
                        pe.wait_ge(c_lo, 3 + l)
                    col_features(u, col[i], mhi[:, 0:KA, :], mlo[:, 0:KA, :], KA)
                    if i == 0:
                        values(1 + l, HEADS - 1)
                for i in range(4):
                    u = l_unit(l, L_ATTN + i)
                    pe.wait_ge(w_lo, u.upto())
                    pe.wait_ge(merge_rd, 8 * l + i + 1)
                    if i == 0:
                        pe.wait_ge(o_lo, HEADS // 2 * (2 + l))
                    col_features(u, col[i], mhi[:, KA:KD, :], mlo[:, KA:KD, :], KA)
                for i in range(4):
                    u = l_unit(l, L_MIX + i)
                    pe.wait_ge(w_lo, u.upto())
                    pe.wait_ge(g_lo, 4 * l + i + 1)
                    if i < 2:
                        rows(u, uhi[:, 2 * i:2 * i + 2, :], ulo[:, 2 * i:2 * i + 2, :], i == 0, False)
                last_rows(l_unit(l, L_MIX + 2), uhi[:, 4:6, :], ulo[:, 4:6, :], l_unit(l, L_MIX + 3), uhi[:, 6:8, :], ulo[:, 6:8, :])

                norm_transposes(3 + 2 * l)
                u = l_unit(l, L_MLP)
                pe.wait_ge(w_lo, u.upto())
                col_features(u, col[0], uhi, ulo, norm=3 + 2 * l)
                open_acc()
                with pe.Fori(0, LOOPS) as i:
                    for q in range(3):
                        up, down = l_unit(l, L_MLP + 1 + 2 * q, i), l_unit(l, L_MLP + 2 + 2 * q, i)
                        done = FF_BLOCKS + MLP_BLOCKS * l + 3 * i + q
                        pe.wait_ge(w_lo, up.upto())
                        col_features(up, col[(1 + q) % 3], uhi, ulo)
                        pe.wait_ge(w_lo, down.upto())
                        pe.wait_ge(ff_lo, done + 1)
                        rows(down, mid(mhi, q), mid(mlo, q), False, False)
                pe.wait_ge(w_lo, l_unit(l, L_UNITS - 1).upto())
                pe.wait_ge(ff_lo, FF_BLOCKS + MLP_BLOCKS * l + MLP_BLOCKS)
                rows(l_unit(l, L_UNITS - 1), mid(mhi, 0), mid(mlo, 0), False, True)

        @block.scalar
        def _(act):
            chain = Chain(act, act_chain)

            def split(u, size=UNIT):
                act.wait_ge(landed[u.slot], u.landed)
                if not (isinstance(u.turns, int) and u.st < SPLIT):
                    act.wait_ge(used, u.upto(SPLIT))
                act.activation(whi[:, u.buf, 0:size], raw[:, u.slot, 0:size], ACT.Copy).then_inc(w_hi, 1)

            def norm(k, gain, at, pause=None, early=1):
                act.activation(sd[:, 2:3], eps[:, 0:1], ACT.Sqrt)

                def mean(t):
                    if isinstance(k, int) and k == 0:
                        act.wait_ge(x_in[t], 16)
                    else:
                        act.wait_ge(x_new, NT * (k - 1) + t + 1)
                    act.activation(xnt[:, t, :], x[:, t, :], ACT.Square, accum_out=ss[:, t:t + 1]).then_inc(sq_done, 1)
                    act.wait_ge(sq_done, NT * k + t + 1)
                    act.activation(sd[:, t:t + 1], ss[:, t:t + 1], ACT.Sqrt, bias=eps[:, 0:1], scale=1.0 / D)\
                        .then_inc(sd_done, 1)

                def hi(t, fs, bank):
                    order = [part_a, part_b] + second
                    act.wait_ge(u_ps, PARTS * k + order.index((t, fs, bank)) + 1)
                    for i, f in enumerate(fs):
                        out = act.activation(uhi[:, f, t * P:t * P + P], bank[:, i * P:i * P + P], ACT.Copy,
                                             scale=gain[:, at + f:at + f + 1])
                    out.then_inc(u_hi, 1)

                mean(0)
                if gain is None or pause:
                    mean(1)
                if gain is None:
                    return
                if pause:
                    pause()
                for i, part in enumerate(norm_parts(k)):
                    if i == early and not pause:
                        mean(1)
                    hi(*part)

            def exps(a, h):
                act.wait_ge(s_max, HEADS * a + h + 1)
                if h >= 2:
                    act.wait_ge(p_ps, HEADS * a + h - 1)
                for t in range(NT):
                    act.activation(expo[h % 2][:, t, 0:keys(a, t)], score[h % 2][:, t, 0:keys(a, t)], ACT.Exp, bias=nmx[:, h % 2, t:t + 1],
                                   accum_out=den[:, h % 2, t:t + 1]).then_inc(s_exp, 1)

            def copy_probs(a, h):
                act.wait_ge(p_ps, HEADS * a + h + 1)
                if h >= 2:
                    act.wait_ge(o_ps, HEADS * a + h - 1)
                if isinstance(a, int):
                    act.activation(prob[:, h % 2, :], T_BANK[:], ACT.Copy).then_inc(p_T, 1)
                else:
                    act.activation(prob[:, h % 2, 0:T], T_BANK[:, 0:T], ACT.Copy)
                    act.activation(prob[:, h % 2, T + P:2 * T], T_BANK[:, T + P:2 * T], ACT.Copy).then_inc(p_T, 1)

            def o_split(a, p):
                act.wait_ge(o_ps, HEADS * a + 2 * p + 2)
                act.activation(mhi[:, KA + p, :], O_BANK[:, 0:T], ACT.Copy).then_inc(o_hi, 1)

            def evacuate(n, j, dst, w=COLS):
                act.wait_ge(used, n.upto())
                act.activation(dst, col[j % 4][:, 0:NT * w].rearrange("p (t c) -> p t c", t=NT), ACT.Copy)\
                    .then_inc(evac, 1)

            def half(tok, i):
                return tok[:, :, COLS * i:COLS * i + COLS]

            def copy_turned(a, n, dst, gain=1.0):
                for b in range(2):
                    act.wait_ge(qk_ps, 4 * a + 2 * n + b + 1)
                    act.activation(dst[:, 2 * b:2 * b + 2, :], acc[2 * n + b][:].rearrange("p (c t) -> p c t", c=2),
                                   ACT.Copy, scale=gain).then_inc(qk_T, 1)

            act.dma_start(grow[0:G_N, :], d["params"][0:G_N, :]).then_inc(par_in, 16)
            act.dma_start(krow[0:TAPS * KA, :], d["params"][G_N:G_N + TAPS * KA, :]).then_inc(par_in, 16)

            def parameters():
                split(a_unit(0))
                act.wait_ge(par_ps, 1)
                act.activation(gcol[:], col[0][:, 0:G_N], ACT.Copy).then_inc(par_sb, 1)
                act.activation(qg[:], col[0][:, G_QG:G_QG + 1], ACT.Copy, scale=SCALE).then_inc(par_sb, 1)
                act.activation(kcol[:], col[1][:, 0:TAPS * KA], ACT.Copy).then_inc(par_sb, 1)
                act.wait_ge(par_sb, 3)

            act.wait_ge(consts, 4)
            norm(0, gcol, G_N1, parameters)
            split(a_unit(1))
            for j in range(A_OUT):
                u = a_unit(j)
                n = (j - 6) // 2
                if j == 6 or j == 8:
                    act.wait_ge(evac, j)
                    act.activation(xn[:, 0:2, :], (qtok, ktok)[n][:], ACT.Square).then_inc(qsq, 1)
                split(a_unit(j + 2))
                if j == 6 or j == 8:
                    act.wait_ge(qss, n + 1)
                    act.activation(sd[:], ss[:], ACT.Sqrt, bias=eps[:, 0:1], scale=1.0 / DH).then_inc(qsd, 1)
                if j == 9:
                    copy_turned(0, 1, kT, gcol[:, G_KG:G_KG + 1])
                    exps(0, 0)
                if j == 8:
                    copy_turned(0, 0, qT, qg[:])
                if j in (0, 2):
                    if j == 2:
                        act.wait_ge(glu, 1)
                    act.wait_ge(used, u.upto())
                    act.activation(vtok[:, 0, :], col[j % 4][:], ACT.Sigmoid).then_inc(evac, 1)
                elif j in (1, 3):
                    act.wait_ge(used, u.upto())
                    act.activation(vtok[:, 1, :], col[j % 4][:], ACT.Copy).then_inc(evac, 1)
                else:
                    if j == 8:
                        act.wait_ge(glu, 2)
                    evacuate(u, j, half((qtok, ktok, vtok)[(j - 4) // 2], j % 2))
            for h in range(HEADS):
                act.wait_ge(s_exp, NT * (h + 1))
                act.wait_ge(rden_ok, h + 1)
                for t in range(NT):
                    norm_p = act.activation(expo[h % 2][:, t, :], expo[h % 2][:, t, :], ACT.Copy,
                                            scale=rden[:, h % 2, t:t + 1])
                norm_p.then_inc(p_ok, 1)
                if h == 0:
                    split(a_unit(A_OUT + 2))
                if h + 1 < HEADS:
                    exps(0, h + 1)
                else:
                    for p in range(2):
                        f = slice(2 * p, 2 * p + 2)
                        act.wait_ge(ln_xc, p + 1)
                        act.activation(lnsq[:, f, :], y[:, f, :], ACT.Square).then_inc(ln_sq, 1)
                copy_probs(0, h)
                if h % 2 == 0 and h >= 2:
                    o_split(0, h // 2 - 1)
            o_split(0, 3)
            act.activation(sd[:, 2:3], eps[:, 0:1], ACT.Sqrt)
            act.wait_ge(ln_var, 1)
            act.activation(lnsd, VAR[:, 0:T], ACT.Sqrt, bias=eps[:, 0:1]).then_inc(ln_sd, 1)
            act.activation(sd[:, 3:4], eps[:, 0:1], ACT.Sigmoid)
            for c in range(KA):
                act.wait_ge(ln_y, c + 1)
                act.activation(lne[:, c, :], y[:, c, :], ACT.Sigmoid, bias=gcol[:, G_LNB + c:G_LNB + c + 1],
                               scale=gcol[:, G_LNG + c:G_LNG + c + 1]).then_inc(ln_e, 1)
            for p in range(2):
                act.wait_ge(c_ok, p + 1)
                act.activation(mhi[:, 2 * p:2 * p + 2, :], y[:, 2 * p:2 * p + 2, :], ACT.Copy).then_inc(c_hi, 1)
            for j in range(A_OUT + 1, A_FF - 1):
                split(a_unit(j + 2))
            norm(1, gcol, G_N2)
            split(a_unit(A_FF + 1))

            def ff_gate(b, q, n, bank):
                act.wait_ge(used, n.upto())
                act.activation(ff_e[q], col[bank][:], ACT.Sigmoid).then_inc(ff_act, 1)

            def ff_split(h, s, count):
                act.wait_ge(ff_ok, count)
                act.activation(mid(mhi, s), h.rearrange("p (c t) -> p c t", c=2), ACT.Copy).then_inc(ff_hi, 1)

            split(a_unit(A_FF + 2))
            ff_gate(0, 0, a_unit(A_FF), 0)
            ff_split(ff_h[0], 0, 1)
            with act.Fori(0, LOOPS) as i:
                for q in range(2):
                    j = A_FF + 2 + 3 * q
                    b = (1 + q) % 2
                    split(a_unit(j + 1, i))
                    split(a_unit(j + 2, i))
                    ff_gate(None, b, a_unit(j, i), 2 * b)
                    split(a_unit(j + 3, i))
                    ff_split(ff_h[b], b, 2 * i + q + 2)

            with act.Fori(0, LAYERS) as l:
                n0 = A_OUT + L_CONV * l
                split(l_unit(l, 0), KD * IKW)
                act.wait_ge(lg_ok, l + 1)
                split(l_unit(l, 1))
                norm(2 + 2 * l, lg, LG_MIX)
                for j in range(L_CONV):
                    u = l_unit(l, j)
                    if j >= 14:
                        exps(1 + l, j - 14)
                    split(l_unit(l, j + 2), unit_size(True, j + 2))
                    if j == 4:
                        act.wait_ge(idx_ps, l + 1)
                        act.activation(iqT, acc[0][:].rearrange("p (c t) -> p c t", c=2), ACT.Copy).then_inc(idx_T, 1)
                        act.activation(ikT, acc[1][:, 0:T], ACT.Copy).then_inc(idx_T, 1)
                    if j == 5:
                        act.wait_ge(lgt_ps, l + 1)
                        for h in range(IDX_HEADS):
                            act.activation(big[:, 2 * h:2 * h + 2, :], acc[h][:].rearrange("p (t k) -> p t k", t=NT),
                                           ACT.Relu).then_inc(lgt_sb, 1)
                    if j == 7:
                        copy_turned(1 + l, 0, qT, SCALE)
                    if j == 8:
                        copy_turned(1 + l, 1, kT)
                    if j % 2 == 1 and j >= 17:
                        o_split(1 + l, (j - 17) // 2)
                    if j == 0:
                        act.wait_ge(used, u.upto())
                        act.activation(ikf[0:IKW, :], col[0][0:IKW, 0:T], ACT.Copy).then_inc(ik_sb, 1)
                    elif j == 1:
                        evacuate(u, j, iqtok)
                        act.wait_ge(ik_ps, l + 1)
                        ikw = acc[1][:, 0:NT * IKW].rearrange("p (t c) -> p t c", t=NT)
                        act.activation(iktok[:, :, 0:64], ikw[:, :, 0:64], ACT.Copy)
                        act.activation(iw[:], ikw[:, :, 64:68], ACT.Copy, scale=IDX_SCALE).then_inc(evac, 1)
                    elif j < 8:
                        evacuate(u, j, half((qtok, ktok, vtok)[(j - 2) // 2], j % 2))
                    elif j < 14:
                        i = (j - 8) % 2
                        evacuate(u, j, (cC, cH, cB)[(j - 8) // 2][:, 2 * i:2 * i + 2, :])
                    else:
                        act.wait_ge(used, u.upto())
                        act.activation(big[:, 2 * (j - 14):2 * (j - 14) + 2, :],
                                       col[j % 4][:].rearrange("p (c t) -> p c t", c=2), ACT.Copy)\
                            .then_inc(evac, 1)
                    if j == 16:
                        act.wait_ge(c_ok, 3 + l)
                        act.activation(mhi[:, 0:KA, :], y[:], ACT.Copy).then_inc(c_hi, 1)
                    if j >= 14:
                        copy_probs(1 + l, j - 14)
                for j in range(L_CONV, L_MLP):
                    if j < L_MLP - 1:
                        split(l_unit(l, j + 2), unit_size(True, j + 2))
                    if j == L_CONV:
                        o_split(1 + l, 3)
                        act.wait_ge(evac, A_OUT + L_CONV * l + L_CONV)
                    if j < L_MIX:
                        f = 2 * (j - L_CONV) + (KD if j < L_ATTN else -KD)
                        act.activation(big[:, f:f + 2, :], big[:, f:f + 2, :], ACT.Sigmoid).then_inc(gate_ok, 1)
                    if j > L_ATTN and j <= L_MIX:
                        i = j - L_ATTN - 1
                        act.wait_ge(merge_rd, 8 * l + 4 + i + 1)
                        act.activation(uhi[:, 2 * i:2 * i + 2, :], big[:, 2 * i:2 * i + 2, :], ACT.Copy).then_inc(g_hi, 1)
                norm(3 + 2 * l, lg, LG_MLP)
                done = FF_BLOCKS + MLP_BLOCKS * l

                def relu(s, up):
                    act.wait_ge(used, up.upto())
                    act.activation(mlp_h[s], col[s][:], ACT.Relu).then_inc(ff_act, 1)

                split(l_unit(l, L_MLP + 1))
                relu(0, l_unit(l, L_MLP))
                ff_split(mlp_h[0], 0, done + 1)
                with act.Fori(0, LOOPS) as i:
                    for q in range(3):
                        s = (1 + q) % 3
                        split(l_unit(l, L_MLP + 2 + 2 * q, i))
                        split(l_unit(l, L_MLP + 3 + 2 * q, i))
                        relu(s, l_unit(l, L_MLP + 1 + 2 * q, i))
                        ff_split(mlp_h[s], s, done + 3 * i + q + 2)

            norm(2 + 2 * LAYERS, None, None)

        @block.vector
        def _(dve):
            chain = Chain(dve, dve_chain)
            link = chain.link

            def split(u, size=UNIT):
                dve.wait_ge(w_hi, u.upto())
                dve.tensor_tensor(wlo[:, u.buf, 0:size], raw[:, u.slot, 0:size], whi[:, u.buf, 0:size].bitcast(F32),
                                  ALU.subtract).then_inc(w_lo, 1)

            def norm(k, gain, at, unit=None, pause=None, early=1):
                def residual(t):
                    if unit is None:
                        return
                    if t == 0:
                        dve.wait_ge(acc_ok, k)
                    else:
                        dve.wait_ge(used, unit.upto())
                    for h in range(2):
                        cs = slice(h * 512, h * 512 + 512)
                        add = dve.tensor_tensor(x[:, t, cs], acc[2 * t + h][:], x[:, t, cs], ALU.add)
                    add.then_inc(x_new, 1)

                def scale(t):
                    dve.wait_ge(sd_done, NT * k + t + 1)
                    link(dve.reciprocal(rn[:, t:t + 1], sd[:, t:t + 1]))
                    if gain is None:
                        dve.scalar_tensor_tensor(xnt[:, t, :], x[:, t, :], rn[:, t:t + 1], gfin, ALU.mult, ALU.mult)\
                            .then_inc(fin, 1)
                    else:
                        dve.tensor_scalar(xnt[:, t, :], x[:, t, :], rn[:, t:t + 1], None, ALU.mult).then_inc(xn_ok, 1)

                def lo(t, fs, bank):
                    dve.wait_ge(u_hi, norm_count(k, t, fs[0]))
                    for i, f in enumerate(fs):
                        tok = slice(t * P, t * P + P)
                        out = dve.scalar_tensor_tensor(ulo[:, f, tok], bank[:, i * P:i * P + P],
                                                       gain[:, at + f:at + f + 1], uhi[:, f, tok].bitcast(F32),
                                                       ALU.mult, ALU.subtract)
                    out.then_inc(u_lo, 1)

                residual(0)
                scale(0)
                residual(1)
                if pause or gain is None:
                    scale(1)
                if pause:
                    pause()
                for i, part in enumerate(norm_parts(k) if gain is not None else ()):
                    if i == early and not pause:
                        scale(1)
                    lo(*part)

            def softmax_max(a, h):
                dve.wait_ge(s_ps, HEADS * a + h + 1)
                if h >= 2:
                    dve.wait_ge(s_exp, NT * (HEADS * a + h - 1))
                dve.memset(apart[:], 0.0)
                for t in range(NT):
                    n = keys(a, t)
                    add = bias[:, t, h, :] if isinstance(a, int) else wk[:, t, 0:n]
                    ins = dve.tensor_tensor_reduce(score[h % 2][:, t, 0:n], S_BANK[h % 2][:, t * T:t * T + n], add, 1.0,
                                                   OUTSIDE * 1e6, ALU.add, ALU.max, mx[:, h % 2, t:t + 1])
                    if t == NT - 1:
                        link(ins)
                dve.tensor_scalar(nmx[:, h % 2, :], mx[:, h % 2, :], -1.0, None, ALU.mult).then_inc(s_max, 1)

            def softmax_norm(a, h):
                dve.wait_ge(s_exp, NT * (HEADS * a + h + 1))
                link(dve.reciprocal(rden[:, h % 2, :], den[:, h % 2, :]))
                for t in range(NT):
                    p = expo[h % 2][:, t, 0:keys(a, t)]
                    ins = dve.tensor_scalar(p, p, rden[:, h % 2, t:t + 1], None,
                                            ALU.mult)
                    if t == 0:
                        link(ins)
                ins.then_inc(p_ok, 1)

            def o_split(a, p):
                dve.wait_ge(o_hi, HEADS // 2 * a + p + 1)
                dve.tensor_tensor(mlo[:, KA + p, :], O_BANK[:, 0:T], mhi[:, KA + p, :].bitcast(F32), ALU.subtract)\
                    .then_inc(o_lo, 1)

            def conv_taps():
                n = 0
                for w0, w1, chunks in ((0, FIRST_TAPS, (0, 1)), (0, TAPS, (2, 3)), (FIRST_TAPS + GP_SUMS, TAPS, (0, 1))):
                    for w in range(w0, w1):
                        for c in chunks:
                            if w == w0 and w:
                                dve.wait_ge(conv_pool, GP_SUMS)
                            elif w > w0:
                                dve.wait_ge(conv_dve, n - 1)
                            tap = kcol[:, w * KA + c:w * KA + c + 1]
                            if w == 0:
                                ins = dve.tensor_scalar(y[:, c, :], cu[:, c, 0:T], tap,
                                                        gcol[:, G_DWB + c:G_DWB + c + 1], ALU.mult, ALU.add)
                            else:
                                ins = dve.scalar_tensor_tensor(y[:, c, :], cu[:, c, w:w + T], tap, y[:, c, :],
                                                               ALU.mult, ALU.add)
                            ins.then_inc(conv_dve, 1)
                            n += 1
                            yield c
            taps = conv_taps()

            def convolve(n):
                for _ in range(n):
                    next(taps, None)

            dve.memset(zeros[:], 0.0).then_inc(consts, 1)
            dve.memset(eps[:], EPS).then_inc(consts, 1)
            dve.memset(ones[:], 1.0 / DA).then_inc(consts, 1)
            link(dve.memset(cu[:], 0.0))
            norm(0, gcol, G_N1, pause=lambda: split(a_unit(0)))
            split(a_unit(1))
            for j in range(A_OUT):
                if j not in (6, 8):
                    split(a_unit(j + 2))
                if j in (2, 4):
                    i = j // 2 - 1
                    dve.wait_ge(evac, j)
                    dve.tensor_tensor(cu[:, 2 * i:2 * i + 2, PAD:PAD + T], vtok[:, 0, :].rearrange("p (c t) -> p c t", c=2),
                                      vtok[:, 1, :].rearrange("p (c t) -> p c t", c=2), ALU.mult).then_inc(glu, 1)
                    dve.wait_ge(glu, i + 1)
                if j in (6, 8):
                    n = (j - 6) // 2
                    tok = (qtok, ktok)[n][:].rearrange("p t (h d) -> p (t h) d", d=DH)
                    dve.wait_ge(qsq, n + 1)
                    dve.tensor_reduce(ss[:], xn[:, 0:2, :].rearrange("p t (h d) -> p (t h) d", d=DH), AX_X, ALU.add)\
                        .then_inc(qss, 1)
                    dve.wait_ge(qsd, n + 1)
                    link(dve.reciprocal(rn[:], sd[:]))
                    dve.tensor_tensor(tok, tok, rn[:].unsqueeze(2).broadcast_to([P, NT * HEADS, DH]), ALU.mult)\
                        .then_inc(qk_tok, 1)
                    split(a_unit(j + 2))
                convolve(TAPS_AT[j])
            dve.wait_ge(bias_in, 16 * GRID_ROWS * GRID_ROWS)
            softmax_max(0, 0)
            for h in range(HEADS):
                dve.wait_ge(s_exp, NT * (h + 1))
                dve.reciprocal(rden[:, h % 2, :], den[:, h % 2, :]).then_inc(rden_ok, 1)
                convolve(TAPS_AT_HEAD if h < HEADS - 2 else 4 * TAPS)
                if h + 1 < HEADS:
                    softmax_max(0, h + 1)
                if h % 2 == 1 and h >= 3:
                    o_split(0, (h - 3) // 2)
            dve.wait_ge(ln_mu, 1)
            for p in range(2):
                f = slice(2 * p, 2 * p + 2)
                dve.tensor_tensor(y[:, f, :], y[:, f, :], MU[:, 0:T].unsqueeze(1).broadcast_to([P, 2, T]), ALU.subtract)\
                    .then_inc(ln_xc, 1)
            split(a_unit(A_OUT + 2))
            o_split(0, 3)
            dve.wait_ge(ln_sd, 1)
            link(dve.reciprocal(lnr, lnsd))
            for c in range(KA):
                dve.tensor_tensor(y[:, c, :], y[:, c, :], lnr, ALU.mult).then_inc(ln_y, 1)
            for c in range(KA):
                dve.wait_ge(ln_y, c + 1)
                z = dve.tensor_scalar(lnz[:, c, :], y[:, c, :], gcol[:, G_LNG + c:G_LNG + c + 1],
                                      gcol[:, G_LNB + c:G_LNB + c + 1], ALU.mult, ALU.add)
            link(z)
            for p in range(2):
                f = slice(2 * p, 2 * p + 2)
                dve.wait_ge(ln_e, 2 * p + 2)
                dve.tensor_tensor(y[:, f, :], lnz[:, f, :], lne[:, f, :], ALU.mult).then_inc(c_ok, 1)
            for p in range(2):
                f = slice(2 * p, 2 * p + 2)
                dve.wait_ge(c_hi, p + 1)
                dve.tensor_tensor(mlo[:, f, :], y[:, f, :], mhi[:, f, :].bitcast(F32), ALU.subtract).then_inc(c_lo, 1)
            for j in range(A_OUT + 1, A_FF - 1):
                split(a_unit(j + 2))
            norm(1, gcol, G_N2, a_unit(A_FF - 1))
            split(a_unit(A_FF + 1))

            def swiglu(b, q, up, count):
                e, h = ff_e[q], ff_h[q]
                dve.wait_ge(ff_act, count)
                link(dve.tensor_tensor(e, col[2 * q][:], e, ALU.mult))
                dve.wait_ge(used, up.upto())
                dve.tensor_tensor(h, col[2 * q + 1][:], e, ALU.mult).then_inc(ff_ok, 1)

            def ff_split(h, s, count):
                dve.wait_ge(ff_hi, count)
                dve.tensor_tensor(mid(mlo, s), h.rearrange("p (c t) -> p c t", c=2), mid(mhi, s).bitcast(F32),
                                  ALU.subtract).then_inc(ff_lo, 1)

            split(a_unit(A_FF + 2))
            swiglu(0, 0, a_unit(A_FF + 1), 1)
            ff_split(ff_h[0], 0, 1)
            with chain.loop(LOOPS, 2) as i:
                for q in range(2):
                    j = A_FF + 2 + 3 * q
                    b = (1 + q) % 2
                    split(a_unit(j + 1, i))
                    split(a_unit(j + 2, i))
                    swiglu(None, b, a_unit(j + 1, i), 2 * i + q + 2)
                    split(a_unit(j + 3, i))
                    ff_split(ff_h[b], b, 2 * i + q + 2)

            def select(t, rounds):
                v = wk[:, t, 0:P * (t + 1)]
                for _ in range(rounds):
                    chain.link_apart(dve.max(m8[:], v), apart[:])
                    chain.link_apart(dve.match_replace(v, m8[:], v, TAKEN), apart[:])

            dve.wait_ge(rope_in, 16)

            with chain.loop(LAYERS, LAYER_LINKS) as l:
                n0 = A_OUT + L_CONV * l
                dve.tensor_copy(lg[:], gcol[:, bass.ds(l * LG_N + G_LAYER, LG_N)]).then_inc(lg_ok, 1)
                split(l_unit(l, 0), KD * IKW)
                norm(2 + 2 * l, lg, LG_MIX, l_unit(l, -1))
                split(l_unit(l, 1))
                for j in range(L_CONV):
                    if j >= 14:
                        softmax_max(1 + l, j - 14)
                        softmax_norm(1 + l, j - 14)
                    split(l_unit(l, j + 2), unit_size(True, j + 2))
                    if j == 1:
                        dve.wait_ge(evac, n0 + 1)
                        rotate(dve, link, iqtok.rearrange("p t (h d) -> p t h d", d=64), IDX_HEADS, itmp).then_inc(idx_tok, 1)
                        dve.wait_ge(idx_tok, 2 * l + 1)
                    if j == 2:
                        dve.wait_ge(evac, n0 + 2)
                        link(rotate(dve, link, iktok[:, :, 0:64].rearrange("p t (h d) -> p t h d", d=64), 1, itmp))
                        dve.tensor_copy(iktok[:, :, 64:128], iktok[:, :, 0:64]).then_inc(idx_tok, 1)
                    if j == 5:
                        for h in range(IDX_HEADS):
                            dve.wait_ge(lgt_sb, IDX_HEADS * l + h + 1)
                            for t in range(NT):
                                n = P * (t + 1)
                                out, lgt, wt = wk[:, t, 0:n], big[:, 2 * h + t, 0:n], iw[:, t, h:h + 1]
                                if h == 0:
                                    link(dve.tensor_scalar(out, lgt, wt, None, ALU.mult))
                                else:
                                    link(dve.scalar_tensor_tensor(out, lgt, wt, out, ALU.mult, ALU.add))
                        dve.memset(wk[0:CHUNK, 0, CHUNK:P], NOT_ADMISSIBLE)
                        dve.memset(wk[:, 0, P:T], 0.0)
                        link(dve.memset(wk[0:CHUNK, 1, P + CHUNK:T], NOT_ADMISSIBLE))
                    if 6 <= j < 10:
                        select(0, 2)
                        select(1, 1)
                    if 10 <= j < 12:
                        select(1, 2)
                    if j == 12:
                        dve.tensor_scalar(wk[:], wk[:], -2e38, OUTSIDE, ALU.is_ge, ALU.mult).then_inc(mask_ok, 1)
                        dve.wait_ge(mask_ok, l + 1)
                    if j % 2 == 1 and j >= 17:
                        o_split(1 + l, (j - 17) // 2)
                    if j == 17:
                        dve.wait_ge(c_hi, 3 + l)
                        dve.tensor_tensor(mlo[:, 0:KA, :], y[:], mhi[:, 0:KA, :].bitcast(F32), ALU.subtract).then_inc(c_lo, 1)
                for j in range(L_CONV, L_MLP):
                    if j < L_MLP - 1:
                        split(l_unit(l, j + 2), unit_size(True, j + 2))
                    if j == L_CONV:
                        o_split(1 + l, 3)
                    if L_ATTN < j <= L_MIX:
                        i = j - L_ATTN - 1
                        f = slice(2 * i, 2 * i + 2)
                        dve.wait_ge(g_hi, 4 * l + i + 1)
                        dve.tensor_tensor(ulo[:, f, :], big[:, f, :], uhi[:, f, :].bitcast(F32), ALU.subtract)\
                            .then_inc(g_lo, 1)
                    if j < L_ATTN:
                        i = j - L_CONV
                        g = big[:, KD + 2 * i:KD + 2 * i + 2, :]
                        dve.wait_ge(gate_ok, 8 * l + i + 1)
                        dve.wait_ge(used, l_unit(l, j).upto())
                        dve.tensor_tensor(g, col[i][:].rearrange("p (c t) -> p c t", c=2), g, ALU.mult).then_inc(merge_rd, 1)
                    elif j < L_MIX:
                        i = j - L_ATTN
                        m = big[:, 2 * i:2 * i + 2, :]
                        dve.wait_ge(gate_ok, 8 * l + 4 + i + 1)
                        dve.wait_ge(used, l_unit(l, j).upto())
                        link(dve.tensor_tensor(m, col[i][:].rearrange("p (c t) -> p c t", c=2), m, ALU.mult))
                        dve.tensor_tensor(m, m, big[:, KD + 2 * i:KD + 2 * i + 2, :], ALU.add).then_inc(merge_rd, 1)
                norm(3 + 2 * l, lg, LG_MLP, l_unit(l, L_MLP - 1))

                def square(s, count):
                    dve.wait_ge(ff_act, count)
                    dve.tensor_tensor(mlp_h[s], mlp_h[s], mlp_h[s], ALU.mult).then_inc(ff_ok, 1)

                done = FF_BLOCKS + MLP_BLOCKS * l
                split(l_unit(l, L_MLP + 1))
                square(0, done + 1)
                ff_split(mlp_h[0], 0, done + 1)
                with chain.loop(LOOPS, 0) as i:
                    for q in range(3):
                        s = (1 + q) % 3
                        split(l_unit(l, L_MLP + 2 + 2 * q, i))
                        split(l_unit(l, L_MLP + 3 + 2 * q, i))
                        square(s, done + 3 * i + q + 2)
                        ff_split(mlp_h[s], s, done + 3 * i + q + 2)

            last = 2 + 2 * LAYERS
            dve.wait_ge(gfin_in, 16)
            norm(last, None, None, l_unit(LAYERS - 1, L_UNITS - 1))

        @block.gpsimd
        def _(pool):
            chain = Chain(pool, pool_chain)
            link = chain.link
            tmp = [rtmp[:, 0:2, :].rearrange("p a b -> p (a b)"), rtmp[:, 2:4, :].rearrange("p a b -> p (a b)")]
            link(pool.memset(ident[:], 0.0))
            pool.affine_select(out=ident[:], in_=ident[:], compare_op=ALU.not_equal, fill=1.0, base=0,
                               pattern=[[-1, P]], channel_multiplier=1).then_inc(consts, 1)

            link(pool.memset(wmask[:], 0.0))
            n, half = GRID_W - NA_COLS, NA_COLS // 2
            for i, p0 in enumerate((0, GRID_W)):
                v = wmask[p0:p0 + GRID_W, :, :]
                pool.affine_select(out=v[:, :, 0:n], in_=v[:, :, 0:n], compare_op=ALU.is_ge, fill=OUTSIDE, base=half,
                                   pattern=[[0, GRID_ROWS], [1, n]], channel_multiplier=-1).then_inc(wmask_ok, 1)
                pool.wait_ge(wmask_ok, 2 * i + 1)
                pool.affine_select(out=v[:, :, NA_COLS:GRID_W], in_=v[:, :, NA_COLS:GRID_W], compare_op=ALU.is_ge,
                                   fill=OUTSIDE, base=half - 1 - NA_COLS, pattern=[[0, GRID_ROWS], [-1, n]],
                                   channel_multiplier=1).then_inc(wmask_ok, 1)
                pool.wait_ge(wmask_ok, 2 * i + 2)
            pool.wait_ge(consts, 4)
            pool.tensor_copy(ident16[:], ident[:]).then_inc(wmask_ok, 1)

            prod = [cB[:, 0:2, :], cB[:, 2:4, :]]

            def product(n):
                w = FIRST_TAPS + n
                tap = kcol[:, w * KA:w * KA + 2].unsqueeze(2).broadcast_to([P, 2, T])
                pool.tensor_tensor(prod[n % 2], cu[:, 0:2, w:w + T], tap, ALU.mult).then_inc(conv_prod, 1)

            pool.wait_ge(conv_dve, 2 * FIRST_TAPS)
            pool.wait_ge(par_sb, 3)
            product(0)
            for n in range(GP_SUMS):
                if n:
                    pool.wait_ge(conv_pool, n)
                if n + 1 < GP_SUMS:
                    product(n + 1)
                pool.wait_ge(conv_prod, n + 1)
                pool.tensor_tensor(y[:, 0:2, :], y[:, 0:2, :], prod[n % 2], ALU.add).then_inc(conv_pool, 1)

            pool.wait_ge(rope_in, 16)
            with chain.loop(LAYERS, POOL_LINKS) as l:
                n0 = A_OUT + L_CONV * l
                for n, tok in enumerate((qtok, ktok)):
                    pool.wait_ge(evac, n0 + 4 + 2 * n)
                    rotate(pool, link, tok[:].rearrange("p t (h d) -> p t h d", d=DH), HEADS, rtmp).then_inc(rope_tok, 1)
                    pool.wait_ge(rope_tok, 2 * l + n + 1)
                pool.wait_ge(lg_ok, l + 1)
                pool.wait_ge(evac, n0 + 12)
                link(pool.tensor_tensor(cu[:, :, CONV_K - 1:CONV_K - 1 + T], cC, cH, ALU.mult))
                for w in range(CONV_K):
                    for c in range(KA):
                        tap = lg[:, LG_CONV + w * KA + c:LG_CONV + w * KA + c + 1]
                        out = y[:, c, :] if w == 0 else tmp[c % 2]
                        link(pool.tensor_tensor(out, cu[:, c, w:w + T], tap.broadcast_to([P, T]), ALU.mult))
                        if w:
                            link(pool.tensor_tensor(y[:, c, :], y[:, c, :], out, ALU.add))
                pool.wait_ge(evac, n0 + 14)
                pool.tensor_tensor(y[:], y[:], cB[:], ALU.mult).then_inc(c_ok, 1)


_MATRICES = ["x", "w_in", "rpb", "w_out", "w_gate", "w_up", "w_down", "w_in_2", "w_attn_out_2", "w_conv_out_2",
             "w_mix_out_2", "w_mlp_up_2", "w_mlp_down_2", "norm_final_2"]


def rope_table():
    inv = 1.0 / (np.float32(500000.0) ** (np.arange(0, 16, 2, dtype=np.float32) / np.float32(16)))
    ang = np.arange(T, dtype=np.float32)[:, None] * inv[None, :].astype(np.float32)
    return np.concatenate([np.cos(ang), np.sin(ang)], axis=1).astype(np.float32)


def parameter_rows(inputs):
    def rows(a):
        return np.asarray(a).reshape(-1, P)
    qk = [np.tile(np.asarray(inputs[name])[0], P // DH)[None] for name in ("q_norm_g", "k_norm_g")]
    first = [rows(inputs[name]) for name in ("norm1_g", "norm2_g", "dw_bias", "conv_ln_g", "conv_ln_b")]
    layers = [rows(inputs[name][l]) for l in range(LAYERS) for name in ("norm_mix_2", "norm_mlp_2", "conv_w_2")]
    return np.concatenate(first + qk + layers + [rows(inputs["dw_kernel"])])


def kernel(**inputs):
    import concourse.bacc as bacc
    from concourse.bass_utils import run_bass_kernel_spmd as run

    nc = bacc.Bacc("TRN2", target_bir_lowering=False, num_devices=1)
    arrays, d = {}, {}
    for name in _MATRICES:
        a = np.ascontiguousarray(inputs[name])
        arrays[f"in_{name}"] = a
        d[name] = nc.dram_tensor(f"in_{name}", a.shape, F32, kind="ExternalInput").ap()
    arrays["in_rope"] = rope_table()
    d["rope"] = nc.dram_tensor("in_rope", arrays["in_rope"].shape, F32, kind="ExternalInput").ap()
    arrays["in_params"] = parameter_rows(inputs)
    d["params"] = nc.dram_tensor("in_params", arrays["in_params"].shape, F32, kind="ExternalInput").ap()
    d["out"] = nc.dram_tensor("out", (1, T, D), F32, kind="ExternalOutput").ap()
    d["skew"] = nc.dram_tensor("skew", (HEADS, 2 * GRID_ROWS - 1, GRID_W, GRID_W), F32).ap()
    build(nc, d)
    return run(nc, [arrays], core_ids=[0]).results[0]["out"]
```
